# Optimizing a Trainium2 kernel written in Bass

```python
import jax
import jax.numpy as jnp
from jax import lax
import numpy as np

D_MODEL = 1024
BATCH = 1
SEQ = 256
DEPTH = 2
DEC_BATCH = 1
DEC_SEQ = 2048
PAST_LEN = 128

GRID_W = 64
HEAD_DIM = 64
NORM_EPS = 1e-6
MLSTM_HEADS = 4
MLSTM_W = MLSTM_HEADS * HEAD_DIM
MLSTM_CHUNK = 128
CONV_K = 3
FGATE_BIAS = 3.0
GQA_Q_HEADS = 6
GQA_KV_HEADS = 2
GQA_W = GQA_Q_HEADS * HEAD_DIM
GQA_KV_W = GQA_KV_HEADS * HEAD_DIM
AXIS_DIM = HEAD_DIM // 2
ROPE_THETA = 10000.0
Q_BLOCK = 128
DIL_PATTERNS = ((128, 1), (512, 4), (2048, 16))
DIL_HEADS_PER_GROUP = 2
DIL_HEADS = DIL_HEADS_PER_GROUP * len(DIL_PATTERNS)
DIL_W = DIL_HEADS * HEAD_DIM
MIX_W = MLSTM_W + GQA_W + DIL_W
IN_SPLITS = (MLSTM_W, MLSTM_W, MLSTM_W, MLSTM_W, 4 * MLSTM_HEADS, MLSTM_W,
             GQA_W, GQA_KV_W, GQA_KV_W, GQA_W,
             DIL_W, DIL_W, DIL_W, DIL_W)
IN_COLS = sum(IN_SPLITS)

kernel_name = 'hybrid_mlstm_gqa_dilated_encoder'

F32 = jnp.float32

def rms_norm(x, g):
    xf = x.astype(F32)
    y = xf * lax.rsqrt(jnp.mean(xf * xf, axis=-1, keepdims=True) + NORM_EPS)
    return (y * g.astype(F32)).astype(x.dtype)

def head_rms(a, g):
    return a * lax.rsqrt(jnp.mean(a * a, axis=-1, keepdims=True) + NORM_EPS) * g.astype(F32)

def to_heads(a, n):
    B, T, _ = a.shape
    return a.reshape(B, T, n, -1).transpose(0, 2, 1, 3)

def from_heads(a):
    B, H, T, D = a.shape
    return a.transpose(0, 2, 1, 3).reshape(B, T, H * D)

def centred_dwconv(x, w, b):
    K = w.shape[0]
    p = K // 2
    T = x.shape[1]
    xp = jnp.pad(x, ((0, 0), (p, p), (0, 0)))
    out = xp[:, 0:T] * w[0].astype(F32)
    for j in range(1, K):
        out = out + xp[:, j:j + T] * w[j].astype(F32)
    return out + b.astype(F32)

def axial_rope(T):
    rows = T // GRID_W
    r, c = jnp.meshgrid(jnp.arange(rows), jnp.arange(GRID_W), indexing='ij')
    r = r.reshape(-1).astype(F32)
    c = c.reshape(-1).astype(F32)
    inv = ROPE_THETA ** (-jnp.arange(0, AXIS_DIM, 2, dtype=F32) / AXIS_DIM)
    ang = jnp.concatenate([r[:, None] * inv, c[:, None] * inv], axis=-1)
    return jnp.cos(ang), jnp.sin(ang)

def apply_rope(x, cos, sin):
    half = HEAD_DIM // 2
    x1, x2 = x[..., :half], x[..., half:]
    return jnp.concatenate([x1 * cos - x2 * sin, x1 * sin + x2 * cos], axis=-1)

def alibi_slopes():
    return jnp.exp2(-8.0 * jnp.arange(1, DIL_HEADS + 1, dtype=F32) / DIL_HEADS)

def mlstm_scan(q, k, v, i_pre, f_pre):
    B, H, T, Dh = q.shape
    L = MLSTM_CHUNK
    nc = T // L
    log_f = jax.nn.log_sigmoid(f_pre)

    def chunks(a):
        return jnp.moveaxis(a.reshape(B, H, nc, L, *a.shape[3:]), 2, 0)

    causal = jnp.tril(jnp.ones((L, L), dtype=bool))

    def step(carry, xs):
        C, n, m = carry
        qc, kc, vc, ic, fc = xs
        bcum = jnp.cumsum(fc, axis=-1)
        b_tot = bcum[..., -1]
        d_intra = jnp.where(causal, bcum[..., :, None] - bcum[..., None, :] + ic[..., None, :], -jnp.inf)
        d_inter = bcum + m[..., None]
        m_row = jnp.maximum(d_inter, jnp.max(d_intra, axis=-1))
        w_intra = jnp.exp(d_intra - m_row[..., None]) * jnp.einsum('bhld,bhsd->bhls', qc, kc)
        w_inter = jnp.exp(d_inter - m_row)
        num = (w_inter[..., None] * jnp.einsum('bhld,bhde->bhle', qc, C)
               + jnp.einsum('bhls,bhse->bhle', w_intra, vc))
        den = w_inter * jnp.einsum('bhld,bhd->bhl', qc, n) + jnp.sum(w_intra, axis=-1)
        h = num / jnp.maximum(jnp.abs(den), jnp.exp(-m_row))[..., None]
        g = b_tot[..., None] - bcum + ic
        m_new = jnp.maximum(b_tot + m, jnp.max(g, axis=-1))
        decay = jnp.exp(b_tot + m - m_new)
        kw = jnp.exp(g - m_new[..., None])[..., None] * kc
        C_new = decay[..., None, None] * C + jnp.einsum('bhsd,bhse->bhde', kw, vc)
        n_new = decay[..., None] * n + jnp.sum(kw, axis=2)
        return (C_new, n_new, m_new), h

    init = (jnp.zeros((B, H, Dh, Dh), F32), jnp.zeros((B, H, Dh), F32), jnp.zeros((B, H), F32))
    xs = (chunks(q), chunks(k), chunks(v), chunks(i_pre), chunks(log_f))
    _, hs = lax.scan(step, init, xs)
    return jnp.moveaxis(hs, 0, 2).reshape(B, H, T, Dh)

def mlstm_mixer(q, k, v, o, gates, z, conv_w, conv_b, out_gain):
    qk = jax.nn.silu(centred_dwconv(jnp.concatenate([q, k], axis=-1), conv_w, conv_b))
    q, k = jnp.split(qk, 2, axis=-1)
    qh = to_heads(q, MLSTM_HEADS)
    kh = to_heads(k, MLSTM_HEADS) * HEAD_DIM ** -0.5
    vh = to_heads(v, MLSTM_HEADS)
    i_f, f_f, i_b, f_b = jnp.split(jnp.swapaxes(gates, 1, 2), 4, axis=1)
    h_fwd = mlstm_scan(qh, kh, vh, i_f, f_f)
    rev = lambda t: jnp.flip(t, axis=2)
    h_bwd = rev(mlstm_scan(rev(qh), rev(kh), rev(vh), rev(i_b), rev(f_b)))
    h = jax.nn.sigmoid(to_heads(o, MLSTM_HEADS)) * (h_fwd + h_bwd)
    hn = h * lax.rsqrt(jnp.mean(h * h, axis=-1, keepdims=True) + NORM_EPS)
    return from_heads(hn) * out_gain.astype(F32) * jax.nn.silu(z)

def gqa_mixer(q, k, v, z, q_norm, k_norm, cos, sin):
    B, T, _ = q.shape
    G = GQA_Q_HEADS // GQA_KV_HEADS
    qh = apply_rope(head_rms(to_heads(q, GQA_Q_HEADS), q_norm), cos, sin) * HEAD_DIM ** -0.5
    kh = apply_rope(head_rms(to_heads(k, GQA_KV_HEADS), k_norm), cos, sin)
    vh = to_heads(v, GQA_KV_HEADS)
    nb = T // Q_BLOCK
    qb = jnp.moveaxis(qh.reshape(B, GQA_KV_HEADS, G, nb, Q_BLOCK, HEAD_DIM), 3, 0)

    def attend(qblk):
        s = jnp.einsum('bkgqd,bksd->bkgqs', qblk, kh)
        p = jax.nn.softmax(s, axis=-1)
        return jnp.einsum('bkgqs,bksd->bkgqd', p, vh)

    ob = lax.map(attend, qb)
    o = jnp.moveaxis(ob, 0, 3).reshape(B, GQA_Q_HEADS, T, HEAD_DIM)
    return from_heads(o) * jax.nn.silu(z)

def dilated_branch(q, k, v, slopes, dilation, n_side):
    B, H, T, Dh = q.shape
    S = T // dilation
    nblk = -(-S // n_side)
    pad = nblk * n_side - S

    def gather_blocks(a):
        a = jnp.swapaxes(a.reshape(B, H, S, dilation, Dh), 2, 3)
        a = jnp.pad(a, ((0, 0), (0, 0), (0, 0), (0, pad), (0, 0)))
        return a.reshape(B, H, dilation, nblk, n_side, Dh)

    qb, kb, vb = gather_blocks(q), gather_blocks(k), gather_blocks(v)

    def band(a):
        ap = jnp.pad(a, ((0, 0), (0, 0), (0, 0), (1, 1), (0, 0), (0, 0)))
        return jnp.concatenate([ap[:, :, :, :-2], ap[:, :, :, 1:-1], ap[:, :, :, 2:]], axis=4)

    kw, vw = band(kb), band(vb)
    qi = jnp.arange(n_side)[:, None]
    kj = jnp.arange(3 * n_side)[None, :]
    rel = kj - n_side - qi
    key_pos = jnp.arange(nblk)[:, None, None] * n_side + (kj - n_side)[None]
    valid = (jnp.abs(rel) <= n_side)[None] & (key_pos >= 0) & (key_pos < S)
    bias = -slopes[:, None, None, None, None] * (jnp.abs(rel) * dilation).astype(F32)
    s = jnp.einsum('bhrnqd,bhrnkd->bhrnqk', qb, kw) * HEAD_DIM ** -0.5 + bias
    s = jnp.where(valid, s, -jnp.inf)
    lse = jax.nn.logsumexp(s, axis=-1)
    o = jnp.einsum('bhrnqk,bhrnkd->bhrnqd', jnp.exp(s - lse[..., None]), vw)

    def scatter_back(a, rest):
        a = a.reshape(B, H, dilation, nblk * n_side, *rest)[:, :, :, :S]
        return jnp.swapaxes(a, 2, 3).reshape(B, H, T, *rest)

    return scatter_back(o, (Dh,)), scatter_back(lse, ())

def dilated_mixer(q, k, v, z, slopes):
    qh, kh, vh = to_heads(q, DIL_HEADS), to_heads(k, DIL_HEADS), to_heads(v, DIL_HEADS)
    outs, lses = [], []
    for g, (window, dilation) in enumerate(DIL_PATTERNS):
        sl = slice(g * DIL_HEADS_PER_GROUP, (g + 1) * DIL_HEADS_PER_GROUP)
        o_g, l_g = dilated_branch(qh[:, sl], kh[:, sl], vh[:, sl], slopes[sl], dilation, window // (2 * dilation))
        outs.append(o_g)
        lses.append(l_g)
    alpha = jax.nn.softmax(jnp.stack(lses, axis=0), axis=0)
    o = jnp.concatenate([outs[g] * alpha[g][..., None] for g in range(len(DIL_PATTERNS))], axis=1)
    return from_heads(o) * jax.nn.silu(z)

def mixer_layer(h, w_in, gate_bias, conv_w, conv_b, out_gain, q_norm, k_norm, w_out, cos, sin, slopes):
    proj = jnp.matmul(h, w_in).astype(F32)
    cuts = [int(c) for c in np.cumsum(IN_SPLITS)[:-1]]
    (mq, mk, mv, mo, mg, mz, gq, gk, gv, gz, dq, dk, dv, dz) = jnp.split(proj, cuts, axis=-1)
    a = mlstm_mixer(mq, mk, mv, mo, mg + gate_bias.astype(F32), mz, conv_w, conv_b, out_gain)
    b = gqa_mixer(gq, gk, gv, gz, q_norm, k_norm, cos, sin)
    c = dilated_mixer(dq, dk, dv, dz, slopes)
    mixed = jnp.concatenate([a, b, c], axis=-1).astype(w_out.dtype)
    return jnp.matmul(mixed, w_out)

def trunk(x, norm_pre, w_in, mlstm_gate_bias, mlstm_conv_w, mlstm_conv_b, mlstm_out_gain,
          gqa_q_norm, gqa_k_norm, w_out, norm_post):
    T = x.shape[1]
    cos, sin = axial_rope(T)
    slopes = alibi_slopes()
    for l in range(DEPTH):
        h = rms_norm(x, norm_pre[l])
        y = mixer_layer(h, w_in[l], mlstm_gate_bias[l], mlstm_conv_w[l], mlstm_conv_b[l], mlstm_out_gain[l],
                        gqa_q_norm[l], gqa_k_norm[l], w_out[l], cos, sin, slopes)
        x = x + rms_norm(y, norm_post[l]).astype(x.dtype)
    return x

def setup_inputs(seed: int = 0) -> dict:
    key = jax.random.key(seed)
    ks = jax.random.split(key, 12)
    nrm = lambda k, s: jax.random.normal(k, s, dtype=F32)
    gate_mask = jnp.asarray(np.repeat(np.array([0.0, 1.0, 0.0, 1.0], np.float32), MLSTM_HEADS))
    return {
        'x_prompt': nrm(ks[0], (BATCH, SEQ, D_MODEL)),
        'x_sample': nrm(ks[1], (DEC_BATCH, DEC_SEQ, D_MODEL)),
        'norm_pre': 1.0 + 0.02 * nrm(ks[2], (DEPTH, D_MODEL)),
        'w_in': nrm(ks[3], (DEPTH, D_MODEL, IN_COLS)) * D_MODEL ** -0.5,
        'mlstm_gate_bias': FGATE_BIAS * gate_mask + 0.1 * nrm(ks[4], (DEPTH, 4 * MLSTM_HEADS)),
        'mlstm_conv_w': nrm(ks[5], (DEPTH, CONV_K, 2 * MLSTM_W)) * CONV_K ** -0.5,
        'mlstm_conv_b': 0.02 * nrm(ks[6], (DEPTH, 2 * MLSTM_W)),
        'mlstm_out_gain': 1.0 + 0.02 * nrm(ks[7], (DEPTH, MLSTM_W)),
        'gqa_q_norm': 1.0 + 0.02 * nrm(ks[8], (DEPTH, HEAD_DIM)),
        'gqa_k_norm': 1.0 + 0.02 * nrm(ks[9], (DEPTH, HEAD_DIM)),
        'w_out': nrm(ks[10], (DEPTH, MIX_W, D_MODEL)) * MIX_W ** -0.5,
        'norm_post': 1.0 + 0.02 * nrm(ks[11], (DEPTH, D_MODEL)),
    }

def reference(x_prompt, x_sample, norm_pre, w_in, mlstm_gate_bias, mlstm_conv_w, mlstm_conv_b,
              mlstm_out_gain, gqa_q_norm, gqa_k_norm, w_out, norm_post):
    y_prompt = trunk(x_prompt, norm_pre, w_in, mlstm_gate_bias, mlstm_conv_w, mlstm_conv_b,
                     mlstm_out_gain, gqa_q_norm, gqa_k_norm, w_out, norm_post)
    y_sample = trunk(x_sample, norm_pre, w_in, mlstm_gate_bias, mlstm_conv_w, mlstm_conv_b,
                     mlstm_out_gain, gqa_q_norm, gqa_k_norm, w_out, norm_post)
    return (y_prompt, y_sample)


_drawn_inputs = setup_inputs


def setup_inputs(seed=0):
    import zlib

    import numpy as np

    out = dict(_drawn_inputs(seed))
    spreads = {}
    factors = {'gqa_q_norm': 8.0, 'gqa_k_norm': 8.0}
    for name, (base, spread) in spreads.items():
        noise = np.random.default_rng([zlib.crc32(name.encode()), seed]).standard_normal(out[name].shape)
        drawn = base * np.exp(spread * noise) if base else spread * noise
        out[name] = jnp.asarray(drawn.astype(out[name].dtype))
    for name, factor in factors.items():
        out[name] = (out[name] * factor).astype(out[name].dtype)
    return out
```

```python
from contextlib import ExitStack

import numpy as np

import concourse.bass as bass
from concourse import mybir

F32 = mybir.dt.float32
F32R = mybir.dt.float32r
ALU = mybir.AluOpType
ACT = mybir.ActivationFunctionType
AX = mybir.AxisListType

P = 128
D_MODEL = 1024
KT = D_MODEL // P
SEQ, DEC_SEQ = 256, 2048
TOK = SEQ + DEC_SEQ
NT = TOK // P
NTP = SEQ // P
DEPTH = 2
HD = 64
EPS = 1e-6
DMA = 16

CT_MQ, CT_MK, CT_MV, CT_MO, CT_MZ = 0, 2, 4, 6, 8
CT_GQ, CT_GK, CT_GV, CT_GZ = 10, 13, 14, 15
CT_DQ, CT_DK, CT_DV, CT_DZ = 18, 21, 24, 27
CT_GATES = 30
NCT = 31

CHUNK = 384
NCH = TOK // CHUNK

GQ_HEADS, KV_HEADS = 6, 2
GQ_PER_KV = GQ_HEADS // KV_HEADS
QC = 512
NQC = DEC_SEQ // QC
DIL = ((128, 1), (512, 4), (2048, 16))
NG = len(DIL)
SIDE = 64
PADTOK = SIDE + TOK + SIDE
MH = 4
GR = MH * NT
BIG = 1.0e30


class Steps:

    def __init__(self, engine, sem, base):
        self.engine, self.sem, self.base, self.n = engine, sem, base, 0

    def mark(self, instruction):
        instruction.then_inc(self.sem, 1)
        self.n += 1

    def join(self):
        self.engine.wait_ge(self.sem, self.base + self.n)


CREDITS = {
    "proj_wlo": 2, "proj_acc": 2 * NCH, "proj_ev_act": NCH // 2, "proj_ev_dve": NCH // 2,
    "ga_exped": 2, "ga_pv_done": 2, "ga_max_read": 2, "ga_o_ok": 2,
    "ml_w_ok": 2, "ml_at_ok": 2, "ml_state_ok": 2, "ml_mm_ok": 4,
}


class Kernel:

    def __init__(self, nc, ctx, arrays):
        self.nc, self.ctx, self.a = nc, ctx, arrays
        self.sems = {}

    def sem(self, name):
        if name not in self.sems:
            self.sems[name] = self.ctx.enter_context(self.nc.semaphore(name))
        return self.sems[name]

    def dram(self, name, shape):
        self.a[name] = self.nc.dram_tensor(name, list(shape), F32).ap()
        return self.a[name]


def sbuf(k, ctx, name, shape, dtype=F32):
    return ctx.enter_context(k.nc.sbuf_tensor(name, list(shape), dtype))


def psum(k, ctx, name, shape):
    return ctx.enter_context(k.nc.psum_tensor(name, list(shape), F32))


def pair(k, ctx, name, shape, dtype=F32):
    return [sbuf(k, ctx, f"{name}{u}", shape, dtype) for u in range(2)]


def at(i, n=1):
    return bass.ds(i, n)


def bc_free(ap, n):
    return ap.unsqueeze(2).to_broadcast([*ap.shape, n])


def rows_of(dram, row0, nrows, col0, ncols):
    return dram[at(row0, nrows), at(col0, ncols)]


def pre_norm(k, L, h_hi, h_lo, ident, cols):
    nc = k.nc
    NB = NT // 2
    with ExitStack() as ctx:
        x = pair(k, ctx, "pn_x", [P, D_MODEL])
        hn = pair(k, ctx, "pn_hn", [P, D_MODEL])
        junk = sbuf(k, ctx, "pn_junk", [P, D_MODEL])
        gain = sbuf(k, ctx, "pn_gain", [P, D_MODEL])
        stat = pair(k, ctx, "pn_stat", [P, 4])
        tr = [psum(k, ctx, f"pn_tr{u}", [P, KT, P]) for u in range(2)]
        x_in = [k.sem(f"pn_x_in{u}") for u in range(2)]
        gain_in, stats, rstd_ok, h_ok, turned, hi_ok, lo_ok = (
            k.sem("pn_" + s) for s in ("gain_in", "stats", "rstd_ok", "h_ok", "turned", "hi_ok", "lo_ok"))
        block = ctx.enter_context(nc.Block())

        @block.sync
        def _(sp):
            sp.dma_start(gain[:], k.a["gain_pre"][at(L), :].partition_broadcast(P)).then_inc(gain_in, DMA)
            with sp.Fori(0, NB) as b:
                for u in range(2):
                    sp.wait_ge(h_ok, (L * NB + b) * 2)
                    sp.dma_start(x[u][:], rows_of(k.a["x"], b * 2 * P + u * P, P, 0, D_MODEL)).then_inc(x_in[u], DMA)

        @block.scalar
        def _(act):
            with act.Fori(0, NB) as b:
                n = L * NB + b
                for u in range(2):
                    st = Steps(act, stats, (n * 2 + u) * 2)
                    act.wait_ge(x_in[u], (n + 1) * DMA)
                    st.mark(nc.scalar.activation(junk[:], x[u][:], ACT.Square, accum_out=stat[u][:, 0:1]))
                    st.join()
                    st.mark(nc.scalar.activation(stat[u][:, 1:2], stat[u][:, 0:1], ACT.Ln,
                                                 scale=1.0 / D_MODEL, bias=cols["eps"]))
                    st.join()
                    nc.scalar.activation(stat[u][:, 2:3], stat[u][:, 1:2], ACT.Exp, scale=-0.5).then_inc(rstd_ok, 1)
                for u in range(2):
                    act.wait_ge(turned, n * 2 + u + 1)
                    nc.scalar.copy(h_hi[:, :, at(b * 2 * P + u * P, P)], tr[u][:]).then_inc(hi_ok, 1)

        @block.vector
        def _(dve):
            with dve.Fori(0, NB) as b:
                n = L * NB + b
                dve.wait_ge(gain_in, (L + 1) * DMA)
                for u in range(2):
                    dve.wait_ge(rstd_ok, n * 2 + u + 1)
                    nc.vector.scalar_tensor_tensor(out=hn[u][:], in0=x[u][:], scalar=stat[u][:, 2:3], in1=gain[:],
                                                   op0=ALU.mult, op1=ALU.mult).then_inc(h_ok, 1)
                for u in range(2):
                    dve.wait_ge(hi_ok, n * 2 + u + 1)
                    tile = at(b * 2 * P + u * P, P)
                    nc.vector.tensor_tensor(h_lo[:, :, tile], tr[u][:], h_hi[:, :, tile].bitcast(F32),
                                            ALU.subtract).then_inc(lo_ok, 1)

        @block.tensor
        def _(pe):
            with pe.Fori(0, NB) as b:
                n = L * NB + b
                for u in range(2):
                    pe.wait_ge(h_ok, n * 2 + u + 1)
                    for j in range(KT):
                        last = pe.transpose(tr[u][:, j, :], hn[u][:, j * P:(j + 1) * P], ident)
                    last.then_inc(turned, 1)


def project(k, L, h_hi, h_lo):
    nc = k.nc
    phases = k.sem("phases_stored")
    NB = NCT // 2
    with ExitStack() as ctx:
        w = pair(k, ctx, "pj_w", [P, KT, P])
        w_hi = pair(k, ctx, "pj_whi", [P, KT, P], F32R)
        w_lo = pair(k, ctx, "pj_wlo", [P, KT, P], F32R)
        stage = pair(k, ctx, "pj_stage", [P, TOK])
        acc = [psum(k, ctx, f"pj_acc{c}", [P, 512]) for c in range(NCH)]
        w_in = [k.sem(f"proj_w_in{u}") for u in range(2)]
        stored = [k.sem(f"proj_stored{u}") for u in range(2)]
        whi, wlo, done = k.sem("proj_whi"), k.sem("proj_wlo"), k.sem("proj_acc")
        ev_act, ev_dve = k.sem("proj_ev_act"), k.sem("proj_ev_dve")
        cnt = (L * ((NCT + 1) // 2), L * (NCT // 2))
        block = ctx.enter_context(nc.Block())

        def slots(engine, slot):
            with engine.Fori(0, NB) as b:
                for u in range(2):
                    slot(b * 2 + u, b, u, False)
            slot(NCT - 1, NB, (NCT - 1) % 2, True)

        @block.sync
        def _(sp):
            def load(ct, b, u):
                sp.wait_ge(wlo, L * NCT + ct + 1)
                sp.dma_start(w[u][:], k.a["w_in"][at(L), at(ct)].rearrange("a b p (t c) -> p (a b t) c", c=P)
                             ).then_inc(w_in[u], DMA)

            def slot(ct, b, u, last):
                if not last:
                    load(ct + 1, b + u, 1 - u)
                sp.wait_ge(ev_act, (L * NCT + ct + 2) * (NCH // 2))
                sp.wait_ge(ev_dve, (L * NCT + ct + 2) * (NCH // 2))
                sp.dma_start(k.a["proj"][at(ct)].rearrange("a p t -> p (a t)"), stage[u][:]).then_inc(stored[u], DMA)

            load(0, 0, 0)
            slots(sp, slot)
            for u in range(2):
                sp.wait_ge(stored[u], (cnt[u] + (NCT + 1 - u) // 2) * DMA)
            sp.sem_inc(phases, 1)

        def evacuate(engine, copy, ct, b, u, parity, sem):
            engine.wait_ge(stored[u], (cnt[u] + b) * DMA)
            for c in range(parity, NCH, 2):
                engine.wait_ge(done, (L * NCT + ct) * NCH + c + 1 + 2 * NCH)
                copy(stage[u][:, c * CHUNK:(c + 1) * CHUNK], acc[c][:, 0:CHUNK]).then_inc(sem, 1)

        @block.scalar
        def _(act):
            def split(ct, b, u):
                act.wait_ge(w_in[u], (cnt[u] + b + 1) * DMA)
                act.wait_ge(done, (L * NCT + ct + 1) * NCH - NCH + NCH)
                nc.scalar.copy(w_hi[u][:], w[u][:]).then_inc(whi, 1)

            def slot(ct, b, u, last):
                if not last:
                    split(ct + 1, b + u, 1 - u)
                evacuate(act, nc.scalar.copy, ct, b, u, 0, ev_act)

            split(0, 0, 0)
            slots(act, slot)

        @block.vector
        def _(dve):
            def split(ct, b, u):
                dve.wait_ge(whi, L * NCT + ct + 1)
                nc.vector.tensor_tensor(w_lo[u][:], w[u][:], w_hi[u][:].bitcast(F32), ALU.subtract).then_inc(wlo, 1)

            def slot(ct, b, u, last):
                if not last:
                    split(ct + 1, b + u, 1 - u)
                evacuate(dve, nc.vector.tensor_copy, ct, b, u, 1, ev_dve)

            split(0, 0, 0)
            slots(dve, slot)

        @block.tensor
        def _(pe):
            def slot(ct, b, u, last):
                pe.wait_ge(wlo, L * NCT + ct + 1 + 2)
                for c in range(NCH):
                    pe.wait_ge((ev_act, ev_dve)[c % 2], (L * NCT + ct) * (NCH // 2) + c // 2 + 1)
                    tok = slice(c * CHUNK, (c + 1) * CHUNK)
                    for t in range(KT):
                        for i, (wt, ht) in enumerate(((w_hi, h_hi), (w_hi, h_lo), (w_lo, h_hi))):
                            mm = pe.matmul(acc[c][:, 0:CHUNK], wt[u][:, t, :], ht[:, t, tok],
                                           start=(t == 0 and i == 0), stop=(t == KT - 1 and i == 2))
                    mm.then_inc(done, 1)

            slots(pe, slot)


PIECES = ((0, SEQ + 2 * QC), (SEQ + 2 * QC, TOK))


def rotate_qk(k, L, cols):
    nc = k.nc
    phases = k.sem("phases_stored")
    W = PIECES[0][1]
    with ExitStack() as ctx:
        raw = pair(k, ctx, "rq_raw", [P, W])
        sq = pair(k, ctx, "rq_sq", [P, W])
        rs = pair(k, ctx, "rq_rs", [P, W])
        qn = pair(k, ctx, "rq_qn", [P, W])
        t1 = pair(k, ctx, "rq_t1", [P, W])
        hi = pair(k, ctx, "rq_hi", [P, W], F32R)
        lo = pair(k, ctx, "rq_lo", [P, W], F32R)
        cos = sbuf(k, ctx, "rq_cos", [P, TOK])
        sin = sbuf(k, ctx, "rq_sin", [P, TOK])
        blk = sbuf(k, ctx, "rq_blk", [P, P])
        rot = sbuf(k, ctx, "rq_rot", [P, P])
        gain = sbuf(k, ctx, "rq_gain", [P, 4])
        scale = sbuf(k, ctx, "rq_scale", [P, 4])
        ss = psum(k, ctx, "rq_ss", [P, 3 * 512])
        rx = psum(k, ctx, "rq_rx", [P, 3 * 512])
        const_in, gain_ok = k.sem("rq_const_in"), k.sem("rq_gain_ok")
        raw_in = [k.sem(f"rq_raw_in{u}") for u in range(2)]
        stored = [k.sem(f"rq_stored{u}") for u in range(2)]
        sq_ok, ss_ok, ln_ok, rs_ok, qn_ok, rx_ok, chain, out_ok, hi_ok, lo_ok = (
            k.sem("rq_" + s) for s in ("sq_ok", "ss_ok", "ln_ok", "rs_ok", "qn_ok", "rx_ok", "chain", "out_ok",
                                       "hi_ok", "lo_ok"))
        block = ctx.enter_context(nc.Block())
        NJ = 4

        def each(engine, item):
            with engine.Fori(0, NJ) as j:
                for u in range(2):
                    item(j, u)

        @block.sync
        def _(sp):
            for dst, src in ((cos, "cos"), (sin, "sin"), (blk, "head_ones"), (rot, "rope_swap"), (scale, "rq_scale")):
                sp.dma_start(dst[:], k.a[src]).then_inc(const_in, DMA)
            sp.dma_start(gain[:], k.a["gain_qk"][at(L)].rearrange("a p c -> p (a c)")).then_inc(const_in, DMA)

            with sp.Fori(0, NJ) as j:
                n = L * NJ + j
                for u, (a, z) in enumerate(PIECES):
                    sp.wait_ge(out_ok, 2 * n)
                    sp.dma_start(raw[u][:, 0:z - a],
                                 k.a["proj"][at(j + CT_GQ)].rearrange("a p t -> p (a t)")[:, a:z]).then_inc(raw_in[u], DMA)
                for u, (a, z) in enumerate(PIECES):
                    for half, ok, name in ((hi, hi_ok, "gqk_hi"), (lo, lo_ok, "gqk_lo")):
                        sp.wait_ge(ok, n * 2 + u + 1)
                        sp.dma_start(k.a[name][at(j)].rearrange("a p t -> p (a t)")[:, a:z],
                                     half[u][:, 0:z - a].bitcast(F32)).then_inc(stored[u], DMA)
            for u in range(2):
                sp.wait_ge(stored[u], (L + 1) * NJ * 2 * DMA)
            sp.sem_inc(phases, 1)

        @block.scalar
        def _(act):
            def item(j, u):
                a, z = PIECES[u]
                m = z - a
                n = (L * NJ + j) * 2 + u
                act.wait_ge(raw_in[u], (L * NJ + j + 1) * DMA)
                nc.scalar.activation(sq[u][:, 0:m], raw[u][:, 0:m], ACT.Square).then_inc(sq_ok, 1)
                act.wait_ge(ss_ok, n + 1)
                nc.scalar.activation(sq[u][:, 0:m], ss[:, 0:m], ACT.Ln, scale=1.0 / HD, bias=cols["eps"]).then_inc(ln_ok, 1)
                act.wait_ge(ln_ok, n + 1)
                nc.scalar.activation(rs[u][:, 0:m], sq[u][:, 0:m], ACT.Exp, scale=-0.5).then_inc(rs_ok, 1)
                act.wait_ge(out_ok, n + 1)
                act.wait_ge(stored[u], (L * NJ + j) * 2 * DMA)
                nc.scalar.copy(hi[u][:, 0:m], t1[u][:, 0:m]).then_inc(hi_ok, 1)

            each(act, item)

        @block.vector
        def _(dve):
            dve.wait_ge(const_in, (L + 1) * 6 * DMA)
            nc.vector.tensor_tensor(gain[:], gain[:], scale[:], ALU.mult).then_inc(gain_ok, 1)

            def item(j, u):
                a, z = PIECES[u]
                m = z - a
                n = (L * NJ + j) * 2 + u
                st = Steps(dve, chain, n * 2)
                dve.wait_ge(gain_ok, L + 1)
                dve.wait_ge(rs_ok, n + 1)
                nc.vector.scalar_tensor_tensor(out=qn[u][:, 0:m], in0=raw[u][:, 0:m], scalar=gain[:, at(j)],
                                               in1=rs[u][:, 0:m], op0=ALU.mult, op1=ALU.mult).then_inc(qn_ok, 1)
                dve.wait_ge(qn_ok, n + 1)
                dve.wait_ge(lo_ok, n)
                st.mark(nc.vector.tensor_tensor(t1[u][:, 0:m], qn[u][:, 0:m], cos[:, a:z], ALU.mult))
                dve.wait_ge(rx_ok, n + 1)
                st.join()
                st.mark(nc.vector.tensor_tensor(qn[u][:, 0:m], rx[:, 0:m], sin[:, a:z], ALU.mult))
                st.join()
                nc.vector.tensor_tensor(t1[u][:, 0:m], t1[u][:, 0:m], qn[u][:, 0:m], ALU.add).then_inc(out_ok, 1)
                dve.wait_ge(hi_ok, n + 1)
                nc.vector.tensor_tensor(lo[u][:, 0:m], t1[u][:, 0:m], hi[u][:, 0:m].bitcast(F32),
                                        ALU.subtract).then_inc(lo_ok, 1)

            each(dve, item)

        @block.tensor
        def _(pe):
            def item(j, u):
                a, z = PIECES[u]
                m = z - a
                n = (L * NJ + j) * 2 + u
                pe.wait_ge(const_in, (L + 1) * 6 * DMA)
                cuts = [(c, min(c + 512, m)) for c in range(0, m, 512)]
                pe.wait_ge(sq_ok, n + 1)
                pe.wait_ge(ln_ok, n)
                for c, e in cuts:
                    mm = pe.matmul(ss[:, c:e], blk[:], sq[u][:, c:e], start=True, stop=True)
                mm.then_inc(ss_ok, 1)
                pe.wait_ge(qn_ok, n + 1)
                pe.wait_ge(out_ok, n)
                for c, e in cuts:
                    mm = pe.matmul(rx[:, c:e], rot[:], qn[u][:, c:e], start=True, stop=True)
                mm.then_inc(rx_ok, 1)

            each(pe, item)


def convolve(k, L, cols):
    nc = k.nc
    phases = k.sem("phases_stored")
    NB = 2
    with ExitStack() as ctx:
        x = pair(k, ctx, "cv_x", [P, TOK])
        y = pair(k, ctx, "cv_y", [P, TOK])
        e = pair(k, ctx, "cv_e", [P, TOK])
        par = sbuf(k, ctx, "cv_par", [P, 4, 4])
        scale = sbuf(k, ctx, "cv_scale", [P, 4])
        const_in = k.sem("cv_const_in")
        x_in = [k.sem(f"cv_x_in{u}") for u in range(2)]
        stored = [k.sem(f"cv_stored{u}") for u in range(2)]
        mid_ok, conv_ok, exp_ok, chain, chain2, out_ok = (
            k.sem("cv_" + s) for s in ("mid_ok", "conv_ok", "exp_ok", "chain", "chain2", "out_ok"))
        block = ctx.enter_context(nc.Block())

        @block.sync
        def _(sp):
            sp.dma_start(par[:], k.a["conv_par"][at(L)].rearrange("a p c j -> p (a c) j")).then_inc(const_in, DMA)
            sp.dma_start(scale[:], k.a["cv_scale"]).then_inc(const_in, DMA)
            with sp.Fori(0, NB) as b:
                n = L * NB + b
                for u in range(2):
                    sp.wait_ge(conv_ok, n * 2)
                    sp.dma_start(x[u][:], k.a["proj"][at(CT_MQ + b * 2 + u)].rearrange("a p t -> p (a t)")).then_inc(x_in[u], DMA)
                for u in range(2):
                    sp.wait_ge(out_ok, n * 2 + u + 1)
                    sp.dma_start(k.a["mqk"][at(b * 2 + u)].rearrange("a p t -> p (a t)"), y[u][:]).then_inc(stored[u], DMA)
            for u in range(2):
                sp.wait_ge(stored[u], (L + 1) * NB * DMA)
            sp.sem_inc(phases, 1)

        @block.scalar
        def _(act):
            with act.Fori(0, NB) as b:
                n = L * NB + b
                act.wait_ge(const_in, (L + 1) * 2 * DMA)
                for u in range(2):
                    ct = b * 2 + u
                    act.wait_ge(x_in[u], (n + 1) * DMA)
                    act.wait_ge(stored[u], n * DMA)
                    nc.scalar.activation(y[u][:], x[u][:], ACT.Identity, scale=par[:, at(ct), 1],
                                         bias=par[:, at(ct), 3]).then_inc(mid_ok, 1)
                for u in range(2):
                    act.wait_ge(conv_ok, n * 2 + u + 1)
                    nc.scalar.activation(e[u][:], y[u][:], ACT.Exp, scale=-1.0).then_inc(exp_ok, 1)

        @block.vector
        def _(dve):
            with dve.Fori(0, NB) as b:
                n = L * NB + b
                dve.wait_ge(const_in, (L + 1) * 2 * DMA)
                for u in range(2):
                    ct = b * 2 + u
                    st = Steps(dve, chain, (n * 2 + u) * 3)
                    dve.wait_ge(mid_ok, n * 2 + u + 1)
                    for s0, s1 in ((0, SEQ), (SEQ, TOK)):
                        st.mark(nc.vector.scalar_tensor_tensor(out=y[u][:, s0 + 1:s1], in0=x[u][:, s0:s1 - 1],
                                                               scalar=par[:, at(ct), 0], in1=y[u][:, s0 + 1:s1],
                                                               op0=ALU.mult, op1=ALU.add))
                    for i, (s0, s1) in enumerate(((0, SEQ), (SEQ, TOK))):
                        st.join()
                        ins = nc.vector.scalar_tensor_tensor(out=y[u][:, s0:s1 - 1], in0=x[u][:, s0 + 1:s1],
                                                             scalar=par[:, at(ct), 2], in1=y[u][:, s0:s1 - 1],
                                                             op0=ALU.mult, op1=ALU.add)
                        if i == 0:
                            st.mark(ins)
                        else:
                            ins.then_inc(conv_ok, 1)
                for u in range(2):
                    ct = b * 2 + u
                    st = Steps(dve, chain2, (n * 2 + u) * 2)
                    dve.wait_ge(exp_ok, n * 2 + u + 1)
                    st.mark(nc.vector.tensor_scalar(e[u][:], e[u][:], 1.0, None, ALU.add))
                    st.join()
                    st.mark(nc.vector.reciprocal(e[u][:], e[u][:]))
                    st.join()
                    nc.vector.scalar_tensor_tensor(out=y[u][:], in0=y[u][:], scalar=scale[:, at(ct)], in1=e[u][:],
                                                   op0=ALU.mult, op1=ALU.mult).then_inc(out_ok, 1)


TM = 5


def turn_tokens(k, L, ident):
    nc = k.nc
    phases = k.sem("phases_stored")
    NB = NT // 2
    with ExitStack() as ctx:
        f = pair(k, ctx, "tt_f", [P, TM, P])
        t = pair(k, ctx, "tt_t", [P, TM * P])
        tr = [psum(k, ctx, f"tt_tr{u}", [P, 1024]) for u in range(2)]
        f_in = [k.sem(f"tt_f_in{u}") for u in range(2)]
        stored = [k.sem(f"tt_stored{u}") for u in range(2)]
        turned, out_ok = k.sem("tt_turned"), k.sem("tt_out_ok")
        block = ctx.enter_context(nc.Block())

        @block.sync
        def _(sp):
            with sp.Fori(0, NB) as b:
                n = L * NB + b
                for u in range(2):
                    tok = at(b * 2 * P + u * P, P)
                    sp.wait_ge(turned, n * 2)
                    sp.dma_start(f[u][:, 0:2, :], k.a["mqk"][2:4, :, tok].rearrange("c p t -> p c t")).then_inc(f_in[u], DMA)
                    sp.dma_start(f[u][:, 2:4, :], k.a["proj"][CT_MV:CT_MV + 2, :, tok].rearrange("c p t -> p c t")).then_inc(f_in[u], DMA)
                    sp.dma_start(f[u][:, 4:5, :], k.a["proj"][CT_GV:CT_GV + 1, :, tok].rearrange("c p t -> p c t")).then_inc(f_in[u], DMA)
                for u in range(2):
                    sp.wait_ge(out_ok, n * 2 + u + 1)
                    sp.dma_start(rows_of(k.a["tokmaj"], b * 2 * P + u * P, P, 0, TM * P), t[u][:]).then_inc(stored[u], DMA)
            for u in range(2):
                sp.wait_ge(stored[u], (L + 1) * NB * DMA)
            sp.sem_inc(phases, 1)

        @block.scalar
        def _(act):
            with act.Fori(0, NB) as b:
                n = L * NB + b
                for u in range(2):
                    act.wait_ge(turned, n * 2 + u + 1)
                    act.wait_ge(stored[u], n * DMA)
                    nc.scalar.copy(t[u][:], tr[u][:, 0:TM * P]).then_inc(out_ok, 1)

        @block.tensor
        def _(pe):
            with pe.Fori(0, NB) as b:
                n = L * NB + b
                for u in range(2):
                    pe.wait_ge(f_in[u], (n + 1) * 3 * DMA)
                    pe.wait_ge(out_ok, n * 2)
                    for j in range(TM):
                        last = pe.transpose(tr[u][:, j * P:(j + 1) * P], f[u][:, j, :], ident)
                    last.then_inc(turned, 1)


def attend_gqa(k, L, ident):
    nc = k.nc
    phases = k.sem("phases_stored")
    NKT = DEC_SEQ // P
    with ExitStack() as ctx:
        k_both = [sbuf(k, ctx, f"ga_kboth{g}", [P, TOK], F32R) for g in range(2)]
        k_one = [sbuf(k, ctx, f"ga_kone{g}", [P, TOK], F32R) for g in range(2)]
        v_one = [sbuf(k, ctx, f"ga_vone{g}", [P, NT, P]) for g in range(2)]
        q_hi2 = [sbuf(k, ctx, f"ga_qhi2{c}", [P, QC], F32R) for c in range(NQC)]
        q_lom = [sbuf(k, ctx, f"ga_qlom{c}", [P, QC], F32R) for c in range(NQC)]
        prob = pair(k, ctx, "ga_prob", [P, QC])
        mx = pair(k, ctx, "ga_mx", [P, 4, 4])
        nmax = pair(k, ctx, "ga_nmax", [P, 4])
        rden = pair(k, ctx, "ga_rden", [HD, QC])
        o_t = pair(k, ctx, "ga_o", [HD, QC])
        ps_s = [psum(k, ctx, f"ga_ps_s{r}", [P, QC]) for r in range(2)]
        ps_x = [psum(k, ctx, f"ga_ps_x{r}", [P, QC]) for r in range(2)]
        ps_o = [psum(k, ctx, f"ga_ps_o{r}", [P, QC]) for r in range(2)]
        ps_m = psum(k, ctx, "ga_ps_m", [P, QC])
        fill, kv_in = k.sem("ga_fill"), k.sem("ga_kv_in")
        q_in = [k.sem(f"ga_q_in{c}") for c in range(NQC)]
        stored = [k.sem(f"ga_stored{u}") for u in range(2)]
        (scored, exped, pv_done, max_done, max_read, nmax_ok, row_done, row_ok, rden_ok, o_ok) = (
            k.sem("ga_" + s) for s in ("scored", "exped", "pv_done", "max_done", "max_read", "nmax_ok",
                                       "row_done", "row_ok", "rden_ok", "o_ok"))
        block = ctx.enter_context(nc.Block())
        SAMPLE = GQ_HEADS * NQC
        ITEMS = SAMPLE + GQ_HEADS
        TILES = SAMPLE * NKT + GQ_HEADS * NTP
        USES = [GQ_HEADS + len(range(c, GQ_HEADS, NQC)) for c in range(NQC)]
        NFILL = NQC + 3 * 2

        def item_no(i):
            return L * ITEMS + i

        def tile_no(i):
            return L * TILES + i * NKT

        def prompt_tile_no(p):
            return L * TILES + SAMPLE * NKT + p * NTP

        @block.sync
        def _(sp):
            for g in range(2):
                rows = slice(g * HD, (g + 1) * HD)
                for dst, name in ((k_both[g][0:HD, :], "gqk_hi"), (k_both[g][HD:P, :], "gqk_lo"), (k_one[g][0:HD, :], "gqk_hi")):
                    sp.dma_start(dst.bitcast(F32), k.a[name][3, rows, :]).then_inc(kv_in, DMA)
                v_cols = slice(4 * P + g * HD, 4 * P + (g + 1) * HD)
                sp.dma_start(v_one[g][:, :, 0:HD], k.a["tokmaj"][:, v_cols].rearrange("(n p) d -> p n d", p=P)).then_inc(kv_in, DMA)

            def load(h, c, a, w):
                hi, lo = (k.a[x].rearrange("c (h d) t -> (c h) d t", d=HD)[at(h)].rearrange("a d t -> (a d) t")[:, a:a + w]
                          for x in ("gqk_hi", "gqk_lo"))
                for dst, src in ((q_hi2[c][0:HD, 0:w], hi), (q_hi2[c][HD:P, 0:w], hi), (q_lom[c][0:HD, 0:w], lo)):
                    sp.dma_start(dst.bitcast(F32), src).then_inc(q_in[c], DMA)

            def store(i, u, rows, a, w):
                sp.wait_ge(o_ok, item_no(i) + 1 + 2)
                sp.dma_start(rows[:, a:a + w], o_t[u][:, 0:w]).then_inc(stored[u], DMA)

            def store_head(h, c):
                store(h * NQC + c, c % 2, k.a["gqo"][at(h)].rearrange("a d t -> (a d) t"), SEQ + c * QC, QC)

            for c in range(NQC):
                load(0, c, SEQ + c * QC, QC)
            with sp.Fori(1, GQ_HEADS) as h:
                for c in range(NQC):
                    sp.wait_ge(pv_done, tile_no(h * NQC + c - NQC + 1) + 2)
                    load(h, c, SEQ + c * QC, QC)
                    store_head(h - 1, c)
            for p in range(GQ_HEADS):
                sp.wait_ge(pv_done, (tile_no(SAMPLE + p - NQC + 1) if p < NQC else prompt_tile_no(p - NQC + 1)) + 2)
                load(p, p % NQC, 0, SEQ)
                if p < NQC:
                    store_head(GQ_HEADS - 1, p)
                else:
                    store(SAMPLE + p - NQC, p % 2, k.a["gqo"][p - NQC], 0, SEQ)
            for p in range(GQ_HEADS - NQC, GQ_HEADS):
                store(SAMPLE + p, p % 2, k.a["gqo"][p], 0, SEQ)
            for u in range(2):
                sp.wait_ge(stored[u], (L + 1) * (ITEMS // 2) * DMA)
            sp.sem_inc(phases, 1)

        @block.tensor
        def _(pe):
            pe.wait_ge(fill, (L + 1) * NFILL)
            pe.wait_ge(kv_in, (L + 1) * 8 * DMA)

            def max_product(g, c, q, key0, w, m, r):
                pe.wait_ge(max_read, m + 1)
                pe.matmul(ps_x[r][:, 0:w], q_hi2[c][:, q * P:(q + 1) * P], k_both[g][:, key0:key0 + w],
                          start=True, stop=True).then_inc(max_done, 1)

            def max_rows(u, nq, i):
                pe.wait_ge(nmax_ok, item_no(i) + 1)
                for q in range(nq):
                    mm = pe.matmul(ps_m[HD:HD + 1, q * P:(q + 1) * P], nmax[u][:, q:q + 1], ident, start=True, stop=True)
                mm.then_inc(row_done, 1)

            def scores(g, c, t, kt, w, r, i, first):
                pe.wait_ge(exped, t + 1)
                tile = slice(kt * P, (kt + 1) * P)
                pe.matmul(ps_s[r][:, 0:w], k_both[g][:, tile], q_hi2[c][:, 0:w], start=True, stop=False)
                if first:
                    pe.wait_ge(row_ok, item_no(i) + 1)
                pe.matmul(ps_s[r][:, 0:w], k_one[g][:, tile], q_lom[c][:, 0:w], start=False, stop=True).then_inc(scored, 1)

            def weigh(g, u, t, kt, w, r, first, last):
                pe.wait_ge(exped, t + 1 + 2)
                pe.matmul(ps_o[u][:, 0:w], v_one[g][:, kt, :], prob[r][:, 0:w], start=first, stop=last).then_inc(pv_done, 1)

            def item(g, c, i, nkt, kt0, w, t0, next_max, next_rows):
                u = c % 2
                for kt in range(nkt):
                    scores(g, c, t0 + kt, kt0 + kt, w, kt % 2, i, kt == 0)
                    next_max(kt)
                    if kt == 1:
                        pe.wait_ge(o_ok, item_no(i) + 1)
                    if kt:
                        weigh(g, u, t0 + kt - 1, kt0 + kt - 1, w, (kt - 1) % 2, kt == 1, False)
                next_rows()
                weigh(g, u, t0 + nkt - 1, kt0 + nkt - 1, w, (nkt - 1) % 2, False, True)

            def nothing(*_):
                pass

            def sample_max(g, c, i):
                def one(kt):
                    if kt == 0:
                        pe.wait_ge(q_in[c], (L * USES[c] * 3 + loads_before(i, c) + 3) * DMA)
                    max_product(g, c, kt // 4, SEQ + (kt % 4) * QC, QC, tile_no(i) + kt, kt % 2)
                return one

            def loads_before(i, c):
                return (i - c) * 3 // NQC if isinstance(i, int) else (i - c) // NQC * 3

            for g in range(KV_HEADS):
                base = g * GQ_PER_KV * NQC
                first = sample_max(g, 0, base)
                for kt in range(NKT):
                    first(kt)
                max_rows(0, 4, base)

                def head(hh, last):
                    i0 = base + hh * NQC
                    for c in range(NQC):
                        i, cn = i0 + c, (c + 1) % NQC
                        end = last and c == NQC - 1
                        heads_before = g * GQ_PER_KV + hh + (c == NQC - 1)

                        def one(kt, i=i, cn=cn, heads_before=heads_before):
                            if kt == 0:
                                pe.wait_ge(q_in[cn], (L * USES[cn] + heads_before + 1) * 3 * DMA)
                            max_product(g, cn, kt // 4, SEQ + (kt % 4) * QC, QC, tile_no(i + 1) + kt, kt % 2)

                        item(g, c, i, NKT, NTP, QC, tile_no(i), nothing if end else one,
                             nothing if end else (lambda i=i, cn=cn: max_rows(cn % 2, 4, i + 1)))

                with pe.Fori(0, GQ_PER_KV - 1) as hh:
                    head(hh, False)
                head(GQ_PER_KV - 1, True)
            for p in range(GQ_HEADS):
                g, c, t0 = p // GQ_PER_KV, p % NQC, prompt_tile_no(p)
                pe.wait_ge(q_in[c], (L * USES[c] + GQ_HEADS + p // NQC + 1) * 3 * DMA)
                for q in range(NTP):
                    max_product(g, c, q, 0, SEQ, t0 + q, q % 2)
                max_rows(c % 2, NTP, SAMPLE + p)
                item(g, c, SAMPLE + p, NTP, 0, SEQ, t0, nothing, nothing)

        @block.scalar
        def _(act):
            def exp_tile(t, w, r):
                act.wait_ge(scored, t + 1)
                act.wait_ge(pv_done, t + 1)
                nc.scalar.activation(prob[r][:, 0:w], ps_s[r][:, 0:w], ACT.Exp).then_inc(exped, 1)

            def row(c, i, w):
                act.wait_ge(row_done, item_no(i) + 1)
                nc.scalar.copy(q_lom[c][HD:HD + 1, 0:w], ps_m[HD:HD + 1, 0:w]).then_inc(row_ok, 1)

            for g in range(KV_HEADS):
                base = g * GQ_PER_KV * NQC
                row(0, base, QC)

                def head(hh, last):
                    for c in range(NQC):
                        i = base + hh * NQC + c
                        for kt in range(NKT):
                            exp_tile(tile_no(i) + kt, QC, kt % 2)
                        if not (last and c == NQC - 1):
                            row((c + 1) % NQC, i + 1, QC)

                with act.Fori(0, GQ_PER_KV - 1) as hh:
                    head(hh, False)
                head(GQ_PER_KV - 1, True)
            for p in range(GQ_HEADS):
                row(p % NQC, SAMPLE + p, SEQ)
                for kt in range(NTP):
                    exp_tile(prompt_tile_no(p) + kt, SEQ, kt % 2)

        @block.vector
        def _(dve):
            def maxima(u, i, t0, nq, nk, w):
                for q in range(nq):
                    for c in range(nk):
                        dve.wait_ge(max_done, t0 + q * nk + c + 1)
                        nc.vector.tensor_reduce(mx[u][:, q, c:c + 1], ps_x[(q * nk + c) % 2][:, 0:w], AX.X,
                                                ALU.max).then_inc(max_read, 1)
                dve.wait_ge(max_read, t0 + nq * nk + 2)
                nc.vector.tensor_reduce(nmax[u][:, 0:nq], mx[u][:, 0:nq, 0:nk], AX.X, ALU.max,
                                        negate=True).then_inc(nmax_ok, 1)

            def output(u, i, t_end, w, stored_before):
                dve.wait_ge(pv_done, t_end + 2)
                dve.wait_ge(o_ok, item_no(i) + 1)
                nc.vector.reciprocal(rden[u][:, 0:w], ps_o[u][HD:P, 0:w]).then_inc(rden_ok, 1)
                dve.wait_ge(rden_ok, item_no(i) + 1)
                dve.wait_ge(stored[u], (L * (ITEMS // 2) + stored_before) * DMA)
                nc.vector.tensor_tensor(o_t[u][:, 0:w], ps_o[u][0:HD, 0:w], rden[u][:, 0:w], ALU.mult).then_inc(o_ok, 1)

            for c in range(NQC):
                nc.vector.memset(q_lom[c][HD:P, :].bitcast(F32), 0.0).then_inc(fill, 1)
            for g in range(KV_HEADS):
                nc.vector.memset(k_one[g][HD:P, :].bitcast(F32), 0.0).then_inc(fill, 1)
                nc.vector.memset(v_one[g][:, :, HD:P], 1.0).then_inc(fill, 1)
            for g in range(KV_HEADS):
                dve.wait_ge(fill, L * NFILL + NFILL - 2 + g)
                nc.vector.memset(k_one[g][HD:HD + 1, :].bitcast(F32), 1.0).then_inc(fill, 1)
            for g in range(KV_HEADS):
                base = g * GQ_PER_KV * NQC
                maxima(0, base, tile_no(base), 4, 4, QC)

                def head(hh, last):
                    for c in range(NQC):
                        i = base + hh * NQC + c
                        if not (last and c == NQC - 1):
                            maxima((c + 1) % 2, i + 1, tile_no(i + 1), 4, 4, QC)
                        output(c % 2, i, tile_no(i + 1), QC, (g * GQ_PER_KV + hh) * 2 + c // 2)

                with dve.Fori(0, GQ_PER_KV - 1) as hh:
                    head(hh, False)
                head(GQ_PER_KV - 1, True)
            for p in range(GQ_HEADS):
                maxima(p % 2, SAMPLE + p, prompt_tile_no(p), NTP, 1, SEQ)
                output(p % 2, SAMPLE + p, prompt_tile_no(p + 1), SEQ, SAMPLE // 2 + p // 2)


def gate_rows(k, L, gate_cols, decay, ident, cols):
    nc = k.nc
    phases = k.sem("phases_stored")
    with ExitStack() as ctx:
        def both(name, shape=(GR, P)):
            return pair(k, ctx, "gr_" + name, shape)

        gi, gf, e, mn, b, a, M, bm, wi, em, kws = (both(x) for x in ("i", "f", "e", "mn", "b", "a", "M", "bm", "wi", "em", "kws"))
        ends, m_col, n_end, dec = both("ends", (GR, 2)), both("mcol", (GR, 1)), both("nend", (GR, 2)), both("dec", (GR, 1))
        m_in, m_out = both("m_in", (MH, NT, 2)), both("m_out", (MH, NT))
        zero = sbuf(k, ctx, "gr_zero", [GR, P])
        bias = sbuf(k, ctx, "gr_bias", [GR, 4])
        carries = sbuf(k, ctx, "gr_carries", [GR, 2])
        ps = psum(k, ctx, "gr_ps", [P, 8, P])
        g_in, hop, out = k.sem("gr_g_in"), k.sem("gr_hop"), k.sem("gr_out")
        sa, sv, turned, done = k.sem("gr_act"), k.sem("gr_dve"), k.sem("gr_turned"), k.sem("gr_done")
        block = ctx.enter_context(nc.Block())
        NA, NV = 14, 32
        NA1, NV1, NV2, NV3 = 6, 14, 20, 32
        NIN = 6

        def ends_of(t, d):
            return t[d][:, P - 1:P] if d == 0 else t[d][:, 0:1]

        def flow(t, d):
            return t[d][:, :] if d == 0 else t[d][:, ::-1]

        @block.sync
        def _(sp):
            sp.dma_start(bias[:], k.a["gate_bias"][at(L)].rearrange("a p c -> p (a c)")).then_inc(g_in, DMA)
            sp.dma_start(carries[:], k.a["carries"]).then_inc(g_in, DMA)
            for d in range(2):
                for t, r in ((gi, 0), (gf, MH)):
                    rows = k.a["proj"][CT_GATES, d * 2 * MH + r:d * 2 * MH + r + MH, :]
                    sp.dma_start(t[d][:], rows.rearrange("h (c l) -> (h c) l", l=P)).then_inc(g_in, DMA)
            sp.wait_ge(sv, L * NV + NV1)
            for d in range(2):
                sp.dma_start(k.a["gate_ends"][d], ends[d][:]).then_inc(hop, DMA)
            sp.wait_ge(hop, (L * 8 + 2) * DMA)
            for d in range(2):
                sp.dma_start(m_in[d][:], k.a["gate_ends"][d].rearrange("(h c) x -> h c x", h=MH)).then_inc(hop, DMA)
            sp.wait_ge(sv, L * NV + NV2)
            for d in range(2):
                sp.dma_start(k.a["gate_m"][d].rearrange("(h c) -> h c", h=MH), m_out[d][:]).then_inc(hop, DMA)
            sp.wait_ge(hop, (L * 8 + 6) * DMA)
            for d in range(2):
                sp.dma_start(m_col[d][:], k.a["gate_m"][d].rearrange("(p x) -> p x", x=1)).then_inc(hop, DMA)
            sp.wait_ge(sv, L * NV + NV3)
            for d in range(2):
                sp.dma_start(k.a["gate_M"][d], M[d][:]).then_inc(out, DMA)
                sp.dma_start(k.a["gate_dec"][d].rearrange("(p x) -> p x", x=1), dec[d][:]).then_inc(out, DMA)
            sp.wait_ge(out, (L * 5 + 4) * DMA)
            sp.dma_start(decay[:], k.a["gate_dec"].rearrange("d p -> (d p)").partition_broadcast(HD)).then_inc(out, DMA)
            sp.wait_ge(out, (L + 1) * 5 * DMA)
            sp.sem_inc(phases, 1)

        @block.scalar
        def _(act):
            st = Steps(act, sa, L * NA)
            act.wait_ge(g_in, (L + 1) * NIN * DMA)
            for d in range(2):
                st.mark(nc.scalar.activation(e[d][:], gf[d][:], ACT.Abs, bias=bias[:, 2 * d + 1:2 * d + 2]))
            for d in range(2):
                st.join()
                st.mark(nc.scalar.activation(e[d][:], e[d][:], ACT.Exp, scale=-1.0))
            for d in range(2):
                st.join()
                st.mark(nc.scalar.activation(e[d][:], e[d][:], ACT.Ln, bias=cols["one"][0:GR]))
            assert st.n == NA1
            act.wait_ge(sv, L * NV + NV2 + 8)
            for d in range(2):
                st.mark(nc.scalar.activation(wi[d][:], M[d][:], ACT.Exp, scale=-1.0, bias=m_col[d][:, 0:1]))
                st.mark(nc.scalar.activation(em[d][:], bm[d][:], ACT.Exp, scale=-1.0))
                st.mark(nc.scalar.activation(kws[d][:], a[d][:], ACT.Exp, bias=n_end[d][:, 0:1]))
                st.mark(nc.scalar.activation(dec[d][:], n_end[d][:, 0:1], ACT.Exp, bias=m_col[d][:, 0:1]))
            assert st.n == NA
            act.wait_ge(turned, L + 1)
            nc.scalar.copy(gate_cols[:], ps[:, :, 0:GR]).then_inc(done, 1)

        @block.vector
        def _(dve):
            st = Steps(dve, sv, L * NV)
            st.mark(nc.vector.memset(zero[:], 0.0))
            st.mark(nc.vector.memset(m_out[0][:], 0.0))
            st.mark(nc.vector.memset(m_out[1][:], 0.0))
            dve.wait_ge(g_in, (L + 1) * NIN * DMA)
            for d in range(2):
                st.mark(nc.vector.tensor_scalar(mn[d][:], gf[d][:], bias[:, 2 * d + 1:2 * d + 2], 0.0, ALU.add, ALU.min))
            dve.wait_ge(sa, L * NA + NA1)
            for d in range(2):
                st.join()
                st.mark(nc.vector.tensor_tensor(mn[d][:], mn[d][:], e[d][:], ALU.subtract))
            st.join()
            for d in range(2):
                st.mark(nc.vector.tensor_tensor_scan(flow(b, d), flow(mn, d), zero[:], 0.0, ALU.add, ALU.add))
            st.join()
            for d in range(2):
                st.mark(nc.vector.scalar_tensor_tensor(out=a[d][:], in0=gi[d][:], scalar=bias[:, 2 * d:2 * d + 1],
                                                       in1=b[d][:], op0=ALU.add, op1=ALU.subtract))
            st.join()
            nc.vector.tensor_copy(ends[0][:, 1:2], ends_of(b, 0))
            nc.vector.tensor_copy(ends[1][:, 1:2], ends_of(b, 1))
            st.mark(nc.vector.tensor_reduce(ends[0][:, 0:1], a[0][:], AX.X, ALU.max))
            st.mark(nc.vector.tensor_reduce(ends[1][:, 0:1], a[1][:], AX.X, ALU.max))
            st.mark(nc.vector.memset(n_end[0][:], 0.0))
            assert st.n == NV1, st.n
            dve.wait_ge(hop, (L * 8 + 4) * DMA)

            def run(d, out_, in_):
                st.mark(nc.vector.tensor_tensor_scan(m_out[d][:, out_], m_in[d][:, in_, 0], m_in[d][:, in_, 1], 0.0,
                                                     ALU.max, ALU.add))

            run(0, slice(1, NTP), slice(0, NTP - 1))
            run(0, slice(NTP + 1, NT), slice(NTP, NT - 1))
            run(1, slice(0, NTP - 1), slice(1, NTP))
            run(1, slice(NT - 2, NTP - 1, -1), slice(NT - 1, NTP, -1))
            st.mark(nc.vector.memset(n_end[1][:], 0.0))
            st.mark(nc.vector.memset(n_end[0][:], 0.0))
            assert st.n == NV2, st.n
            dve.wait_ge(hop, (L + 1) * 8 * DMA)
            for d in range(2):
                st.mark(nc.vector.tensor_tensor_scan(flow(M, d), flow(a, d), zero[:], m_col[d][:, 0:1], ALU.max, ALU.add))
            st.join()
            for d in range(2):
                st.mark(nc.vector.tensor_tensor(bm[d][:], b[d][:], M[d][:], ALU.add))
                st.mark(nc.vector.tensor_scalar(n_end[d][:, 0:1], ends_of(M, d), -1.0, None, ALU.mult))
            for d in range(2):
                st.mark(nc.vector.tensor_scalar(n_end[d][:, 1:2], ends_of(M, d), -1.0, None, ALU.mult))
            dve.wait_ge(sa, L * NA + NA)
            for d in range(2):
                st.mark(nc.vector.tensor_scalar(wi[d][:], wi[d][:], carries[:, d:d + 1], None, ALU.mult))
                st.mark(nc.vector.tensor_scalar(dec[d][:], dec[d][:], carries[:, d:d + 1], None, ALU.mult))
            assert st.n == NV3, st.n

        @block.tensor
        def _(pe):
            pe.wait_ge(sv, (L + 1) * NV)
            for d in range(2):
                for j, t in enumerate((a, wi, em, kws)):
                    last = pe.transpose(ps[:, d * 4 + j, 0:GR], t[d][:], ident[0:GR, 0:GR])
            last.then_inc(turned, 1)


def mlstm(k, L, gate_cols, decay):
    nc = k.nc
    phases = k.sem("phases_stored")
    NB = NT // 2
    with ExitStack() as ctx:
        def four(name, shape):
            return [[sbuf(k, ctx, f"ml_{name}{u}{d}", shape) for d in range(2)] for u in range(2)]

        q, kt_, kk, v1, mb = (four("q", [HD, MH, P]), four("kt", [HD, MH, P]), four("kk", [P, MH, HD]),
                              four("v1", [P, MH, HD + 1]), four("mb", [P, MH, P]))
        h_out = four("h", [P, MH, HD])
        arg, w, at_, kw, nd, den = (pair(k, ctx, "ml_" + x, s) for x, s in (
            ("arg", [P, MH, P]), ("w", [P, MH, P]), ("at", [P, MH, P]), ("kw", [P, MH, HD]),
            ("nd", [P, MH, HD + 1]), ("den", [P, MH])))
        state = pair(k, ctx, "ml_state", [HD, MH, HD + 1])
        causal = sbuf(k, ctx, "ml_causal", [P, 2, P])
        ps_s = [psum(k, ctx, f"ml_ps_s{d}", [P, MH, P]) for d in range(2)]
        ps_i = [psum(k, ctx, f"ml_ps_i{d}", [P, 512]) for d in range(2)]
        ps_n = [psum(k, ctx, f"ml_ps_n{d}", [P, 512]) for d in range(2)]
        ps_c = [psum(k, ctx, f"ml_ps_c{d}", [HD, 512]) for d in range(2)]
        loaded = [[k.sem(f"ml_loaded{u}{d}") for d in range(2)] for u in range(2)]
        stored = [[k.sem(f"ml_stored{u}{d}") for d in range(2)] for u in range(2)]
        const_in = k.sem("ml_const_in")
        fill, arg_ok, w_ok, s_ok, at_ok, kw_ok, mm_ok, chain, h_ok, state_ok = (
            k.sem("ml_" + s) for s in ("fill", "arg_ok", "w_ok", "s_ok", "at_ok", "kw_ok", "mm_ok", "chain",
                                       "h_ok", "state_ok"))
        block = ctx.enter_context(nc.Block())
        W = HD + 1

        def chunk(b, u, d):
            return b * 2 + u if d == 0 else b * -2 + (NT - 1 - u)

        def number(b, u, d):
            return (L * NB + b) * 4 + u * 2 + d

        def gate(which, d, c):
            t = gate_cols[:, d * 4 + which, :].rearrange("p (h c) -> p h c", c=NT)
            return t[:, :, at(c)].rearrange("p h x -> p (h x)")

        def decay_of(d, c):
            t = decay[:, d * GR:(d + 1) * GR].rearrange("p (h c) -> p h c", c=NT)
            return t[:, :, at(c)].rearrange("p h x -> p (h x)")

        def heads(ps):
            return ps[:, 0:MH * W].rearrange("p (h e) -> p h e", e=W)

        @block.sync
        def _(sp):
            sp.dma_start(causal[:], k.a["causal"]).then_inc(const_in, DMA)

            def loads(b):
                for u in range(2):
                    for d in range(2):
                        c = chunk(b, u, d)
                        sp.wait_ge(mm_ok, number(b, u, d) + 1)
                        tok = at(c * P, P)
                        qk = k.a["mqk"].rearrange("c (h d) t -> d (c h) t", d=HD)
                        s = loaded[u][d]
                        sp.dma_start(q[u][d][:], qk[:, 0:MH, tok]).then_inc(s, DMA)
                        sp.dma_start(kt_[u][d][:], qk[:, MH:2 * MH, tok]).then_inc(s, DMA)
                        sp.dma_start(kk[u][d][:], k.a["tokmaj"][tok, 0:MH * HD].rearrange("t (h e) -> t h e", e=HD)).then_inc(s, DMA)
                        sp.dma_start(v1[u][d][:, :, 0:HD],
                                     k.a["tokmaj"][tok, MH * HD:2 * MH * HD].rearrange("t (h e) -> t h e", e=HD)).then_inc(s, DMA)
                        M = k.a["gate_M"][d].rearrange("(h c) l -> c h l", c=NT)[at(c)].rearrange("c h l -> (c h) l")
                        sp.dma_start(mb[u][d][:], M.partition_broadcast(P)).then_inc(s, DMA)

            def stores(b):
                for u in range(2):
                    for d in range(2):
                        sp.wait_ge(h_ok, number(b, u, d) + 1)
                        sp.dma_start(rows_of(k.a["mh"][d], chunk(b, u, d) * P, P, 0, MH * HD),
                                     h_out[u][d][:].rearrange("p h e -> p (h e)")).then_inc(stored[u][d], DMA)

            loads(0)
            with sp.Fori(1, NB) as b:
                loads(b)
                stores(b - 1)
            stores(NB - 1)
            for u in range(2):
                for d in range(2):
                    sp.wait_ge(stored[u][d], (L + 1) * NB * DMA)
            sp.sem_inc(phases, 1)

        @block.gpsimd
        def _(pool):
            with pool.Fori(0, NB) as b:
                pool.wait_ge(const_in, (L + 1) * DMA)
                for u in range(2):
                    for d in range(2):
                        m = number(b, u, d)
                        pool.wait_ge(loaded[u][d], (L * NB + b + 1) * 5 * DMA)
                        pool.wait_ge(w_ok, m + 1)
                        mask = causal[:, d, :].unsqueeze(1).to_broadcast([P, MH, P])
                        nc.gpsimd.tensor_tensor(arg[d][:], mask, mb[u][d][:], ALU.subtract).then_inc(arg_ok, 1)
                        pool.wait_ge(mm_ok, m + 1 + 2)
                        nc.gpsimd.tensor_tensor(kw[d][:], kk[u][d][:], bc_free(gate(3, d, chunk(b, u, d)), HD),
                                                ALU.mult).then_inc(kw_ok, 1)

        @block.scalar
        def _(act):
            with act.Fori(0, NB) as b:
                for u in range(2):
                    for d in range(2):
                        m = number(b, u, d)
                        act.wait_ge(arg_ok, m + 1)
                        act.wait_ge(at_ok, m + 1)
                        a = gate_cols[:, d * 4, :]
                        for h in range(MH):
                            ins = nc.scalar.activation(w[d][:, h, :], arg[d][:, h, :], ACT.Exp,
                                                       bias=a[:, at(chunk(b, u, d) + h * NT)])
                        ins.then_inc(w_ok, 1)

        @block.vector
        def _(dve):
            for d in range(2):
                nc.vector.memset(state[d][:], 0.0).then_inc(fill, 1)
                for u in range(2):
                    nc.vector.memset(v1[u][d][:, :, HD:W], 1.0).then_inc(fill, 1)
            with dve.Fori(0, NB) as b:
                dve.wait_ge(fill, (L + 1) * 6)
                for u in range(2):
                    for d in range(2):
                        m = number(b, u, d)
                        dve.wait_ge(w_ok, m + 1 + 2)
                        dve.wait_ge(s_ok, m + 1)
                        dve.wait_ge(mm_ok, m + 1 + 2)
                        nc.vector.tensor_tensor(at_[d][:], w[d][:], ps_s[d][:], ALU.mult).then_inc(at_ok, 1)
                    for d in range(2):
                        m, c = number(b, u, d), chunk(b, u, d)
                        st = Steps(dve, chain, m * 6)
                        dve.wait_ge(mm_ok, m + 1 + 4)
                        st.mark(nc.vector.tensor_tensor(nd[d][:], heads(ps_i[d]), bc_free(gate(1, d, c), W), ALU.mult))
                        st.mark(nc.vector.tensor_tensor(state[d][:], state[d][:],
                                                        bc_free(decay_of(d, c), W), ALU.mult))
                        st.join()
                        st.mark(nc.vector.tensor_tensor(nd[d][:], nd[d][:], heads(ps_n[d]), ALU.add))
                        st.join()
                        dcol = nd[d][:, :, HD:W].rearrange("p h x -> p (h x)")
                        st.mark(nc.vector.scalar_tensor_tensor(out=den[d][:], in0=dcol, scalar=-1.0, in1=dcol,
                                                               op0=ALU.mult, op1=ALU.max))
                        st.join()
                        st.mark(nc.vector.tensor_tensor(den[d][:], den[d][:], gate(2, d, c), ALU.max))
                        st.join()
                        st.mark(nc.vector.reciprocal(den[d][:], den[d][:]))
                        nc.vector.tensor_tensor(state[d][:], state[d][:], heads(ps_c[d]), ALU.add).then_inc(state_ok, 1)
                        st.join()
                        dve.wait_ge(stored[u][d], (L * NB + b) * DMA)
                        nc.vector.tensor_tensor(h_out[u][d][:], nd[d][:, :, 0:HD], bc_free(den[d][:], HD),
                                                ALU.mult).then_inc(h_ok, 1)

        @block.tensor
        def _(pe):
            with pe.Fori(0, NB) as b:
                pe.wait_ge(fill, (L + 1) * 6)
                for u in range(2):
                    for d in range(2):
                        m = number(b, u, d)
                        pe.wait_ge(loaded[u][d], (L * NB + b + 1) * 5 * DMA)
                        pe.wait_ge(at_ok, m + 1)
                        for h in range(MH):
                            mm = pe.matmul(ps_s[d][:, h, :], kt_[u][d][:, h, :], q[u][d][:, h, :], start=True, stop=True)
                        mm.then_inc(s_ok, 1)
                    for d in range(2):
                        m = number(b, u, d)
                        pe.wait_ge(state_ok, m + 1)
                        for h in range(MH):
                            pe.matmul(ps_i[d][:, h * W:(h + 1) * W], q[u][d][:, h, :], state[d][:, h, :], start=True, stop=True)
                        pe.wait_ge(kw_ok, m + 1)
                        for h in range(MH):
                            pe.matmul(ps_c[d][:, h * W:(h + 1) * W], kw[d][:, h, :], v1[u][d][:, h, :], start=True, stop=True)
                        pe.wait_ge(at_ok, m + 1 + 2)
                        for h in range(MH):
                            mm = pe.matmul(ps_n[d][:, h * W:(h + 1) * W], at_[d][:, h, :], v1[u][d][:, h, :], start=True, stop=True)
                        mm.then_inc(mm_ok, 1)


def order_classes(k, L):
    nc = k.nc
    phases = k.sem("phases_stored")
    with ExitStack() as ctx:
        x = [sbuf(k, ctx, f"oc_x{g}", [P, TOK]) for g in range(NG)]
        y = [sbuf(k, ctx, f"oc_y{g}", [P, TOK]) for g in range(NG)]
        scale = sbuf(k, ctx, "oc_scale", [P, 4])
        const_in = k.sem("oc_const_in")
        x_in = [k.sem(f"oc_x_in{g}") for g in range(NG)]
        stored = [k.sem(f"oc_stored{g}") for g in range(NG)]
        ok = [k.sem(f"oc_ok{g}") for g in range(NG)]
        block = ctx.enter_context(nc.Block())

        @block.sync
        def _(sp):
            sp.dma_start(scale[:], k.a["oc_scale"]).then_inc(const_in, DMA)
            with sp.Fori(0, 3) as kind:
                n = L * 3 + kind
                for g in range(NG):
                    sp.wait_ge(ok[g], n * 2)
                    sp.dma_start(x[g][:], k.a["proj"][at(kind * NG + (CT_DQ + g))].rearrange("a p t -> p (a t)")).then_inc(x_in[g], DMA)
                for g in range(NG):
                    sp.wait_ge(ok[g], n * 2 + 2)
                    dst = k.a["dil_in"][at(kind * NG + g)].rearrange("a p t -> p (a t)")[:, SIDE:SIDE + TOK]
                    sp.dma_start(dst, y[g][:]).then_inc(stored[g], DMA)
            for g in range(NG):
                sp.wait_ge(stored[g], (L + 1) * 3 * DMA)
            sp.sem_inc(phases, 1)

        @block.vector
        def _(dve):
            with dve.Fori(0, 3) as kind:
                dve.wait_ge(const_in, (L + 1) * DMA)
                n = L * 3 + kind
                for g, (_, dil) in enumerate(DIL):
                    dve.wait_ge(x_in[g], (n + 1) * DMA)
                    dve.wait_ge(stored[g], n * DMA)
                    for s0, s1 in ((0, SEQ), (SEQ, TOK)):
                        nc.vector.tensor_scalar(y[g][:, s0:s1].rearrange("p (r j) -> p j r", r=dil),
                                                x[g][:, s0:s1].rearrange("p (j r) -> p j r", r=dil),
                                                scale[:, at(kind)], None, ALU.mult).then_inc(ok[g], 1)


KW = P + 2 * SIDE


def attend_dilated(k, L, ident):
    nc = k.nc
    phases = k.sem("phases_stored")
    NB = NT // 2
    slopes = [2.0 ** (-8.0 * (h + 1) / 6.0) for h in range(6)]
    with ExitStack() as ctx:
        q, kw, v, dist = (pair(k, ctx, "dl_" + x, s) for x, s in (
            ("q", [HD, 2, P]), ("k", [HD, 2, KW]), ("v", [P, KW]), ("dist", [P, KW])))
        v_t, sb_, pr, pt = (pair(k, ctx, "dl_" + x, s) for x, s in (
            ("v_t", [P, 2, P]), ("s", [P, 2, KW]), ("p", [P, 2, KW]), ("pt", [P, 4, P])))
        nmax, den, lnd, out = (pair(k, ctx, "dl_" + x, s) for x, s in (
            ("nmax", [P, 2]), ("den", [P, 4]), ("lnd", [P, 2]), ("out", [P, 2, HD + 1])))
        ps_s = [psum(k, ctx, f"dl_ps_s{u}", [P, 2, KW]) for u in range(2)]
        ps_v = [psum(k, ctx, f"dl_ps_v{u}", [P, 4, P]) for u in range(2)]
        ps_t = [psum(k, ctx, f"dl_ps_t{u}", [P, 4, P]) for u in range(2)]
        ps_o = [psum(k, ctx, f"dl_ps_o{u}", [P, 512]) for u in range(2)]
        loaded = [k.sem(f"dl_loaded{u}") for u in range(2)]
        stored = [k.sem(f"dl_stored{u}") for u in range(2)]
        s_ok, vt_ok, bias_ok, nmax_ok, p_ok, turned, pt_ok, pv_ok, lnd_ok, chain, out_ok = (
            k.sem("dl_" + s) for s in ("s_ok", "vt_ok", "bias_ok", "nmax_ok", "p_ok", "turned", "pt_ok", "pv_ok",
                                       "lnd_ok", "chain", "out_ok"))
        block = ctx.enter_context(nc.Block())

        def number(g, b):
            return (L * NG + g) * NB + b

        @block.sync
        def _(sp):
            def loads(g, b):
                for u in range(2):
                    a = b * 2 * P + u * P
                    src = k.a["dil_in"]
                    half = src.rearrange("c (h d) t -> c d h t", h=2)
                    sp.wait_ge(pv_ok, number(g, b) * 2 + u) if u == 0 else sp.wait_ge(pv_ok, number(g, b) * 2)
                    s = loaded[u]
                    sp.dma_start(q[u][:], half[g][:, :, at(a + SIDE, P)]).then_inc(s, DMA)
                    sp.dma_start(kw[u][:], half[NG + g][:, :, at(a, KW)]).then_inc(s, DMA)
                    sp.dma_start(v[u][:], src[2 * NG + g][:, at(a, KW)]).then_inc(s, DMA)
                    sp.dma_start(dist[u][:], k.a["dil_dist"][g][at(b * 2 + u)].rearrange("a p t -> (a p) t")).then_inc(s, DMA)

            def stores(g, b):
                for u in range(2):
                    sp.wait_ge(out_ok, number(g, b) * 2 + u + 1)
                    sp.dma_start(rows_of(k.a["dil_out"][g], b * 2 * P + u * P, P, 0, 2 * (HD + 1)),
                                 out[u][:].rearrange("p h e -> p (h e)")).then_inc(stored[u], DMA)

            for g in range(NG):
                loads(g, 0)
                with sp.Fori(1, NB) as b:
                    loads(g, b)
                    stores(g, b - 1)
                stores(g, NB - 1)
            for u in range(2):
                sp.wait_ge(stored[u], (L + 1) * NG * NB * DMA)
            sp.sem_inc(phases, 1)

        @block.tensor
        def _(pe):
            for g in range(NG):
                with pe.Fori(0, NB) as b:
                    n = number(g, b)
                    for u in range(2):
                        m = n * 2 + u
                        pe.wait_ge(loaded[u], (n + 1) * 4 * DMA)
                        pe.wait_ge(bias_ok, n * 2)
                        for h in range(2):
                            mm = pe.matmul(ps_s[u][:, h, :], q[u][:, h, :], kw[u][:, h, :], start=True, stop=True)
                        mm.then_inc(s_ok, 1)
                        pe.wait_ge(pt_ok, n * 2)
                        for c in range(2):
                            mm = pe.transpose(ps_v[u][:, c, :], v[u][:, c * P:(c + 1) * P], ident)
                        mm.then_inc(vt_ok, 1)
                    for u in range(2):
                        pe.wait_ge(p_ok, n * 2 + u + 1)
                        for h in range(2):
                            for c in range(2):
                                mm = pe.transpose(ps_t[u][:, h * 2 + c, :], pr[u][:, h, c * P:(c + 1) * P], ident)
                        mm.then_inc(turned, 1)
                    for u in range(2):
                        pe.wait_ge(pt_ok, n * 2 + u + 1)
                        pe.wait_ge(out_ok, n * 2)
                        for h in range(2):
                            for c in range(2):
                                mm = pe.matmul(ps_o[u][:, h * HD:(h + 1) * HD], pt[u][:, h * 2 + c, :],
                                               v_t[u][:, c, h * HD:(h + 1) * HD], start=(c == 0), stop=(c == 1))
                        mm.then_inc(pv_ok, 1)

        @block.scalar
        def _(act):
            for g in range(NG):
                with act.Fori(0, NB) as b:
                    n = number(g, b)
                    for u in range(2):
                        act.wait_ge(vt_ok, n * 2 + u + 1)
                        act.wait_ge(pv_ok, n * 2)
                        nc.scalar.copy(v_t[u][:], ps_v[u][:, 0:2, :])
                    for u in range(2):
                        act.wait_ge(nmax_ok, n * 2 + u + 1)
                        act.wait_ge(turned, n * 2)
                        act.wait_ge(out_ok, n * 2)
                        for h in range(2):
                            ins = nc.scalar.activation(pr[u][:, h, :], sb_[u][:, h, :], ACT.Exp,
                                                       bias=nmax[u][:, h:h + 1], accum_out=den[u][:, h:h + 1])
                        ins.then_inc(p_ok, 1)
                    for u in range(2):
                        act.wait_ge(turned, n * 2 + u + 1)
                        nc.scalar.copy(pt[u][:], ps_t[u][:]).then_inc(pt_ok, 1)
                        act.wait_ge(p_ok, n * 2 + u + 1)
                        nc.scalar.activation(lnd[u][:], den[u][:, 0:2], ACT.Ln).then_inc(lnd_ok, 1)

        @block.vector
        def _(dve):
            for g, (_, dil) in enumerate(DIL):
                with dve.Fori(0, NB) as b:
                    n = number(g, b)
                    for u in range(2):
                        m = n * 2 + u
                        dve.wait_ge(s_ok, m + 1)
                        dve.wait_ge(p_ok, n * 2)
                        for h in range(2):
                            nc.vector.scalar_tensor_tensor(
                                out=sb_[u][:, h, :], in0=dist[u][:], scalar=float(-slopes[2 * g + h] * dil),
                                in1=ps_s[u][:, h, :], op0=ALU.mult, op1=ALU.add).then_inc(
                                    bias_ok if h else chain, 1)
                        dve.wait_ge(bias_ok, m + 1)
                        nc.vector.tensor_reduce(nmax[u][:], sb_[u][:], AX.X, ALU.max, negate=True).then_inc(nmax_ok, 1)
                    for u in range(2):
                        m = n * 2 + u
                        dve.wait_ge(lnd_ok, m + 1)
                        nc.vector.reciprocal(den[u][:, 2:4], den[u][:, 0:2]).then_inc(chain, 1)
                        dve.wait_ge(stored[u], n * DMA)
                        lse = out[u][:, :, HD:HD + 1].rearrange("p h x -> p (h x)")
                        nc.vector.tensor_tensor(lse, lnd[u][:], nmax[u][:], ALU.subtract).then_inc(chain, 1)
                        dve.wait_ge(chain, n * 6 + 2 + 2 * (u + 1))
                        dve.wait_ge(pv_ok, m + 1)
                        nc.vector.tensor_tensor(out[u][:, :, 0:HD],
                                                ps_o[u][:, 0:2 * HD].rearrange("p (h e) -> p h e", e=HD),
                                                bc_free(den[u][:, 2:4], HD), ALU.mult).then_inc(out_ok, 1)


NZ = 8


def finish(k, L, ident, cols):
    nc = k.nc
    phases = k.sem("phases_stored")
    with ExitStack() as ctx:
        w_hi = sbuf(k, ctx, "fi_whi", [P, KT, D_MODEL], F32R)
        w_lo = sbuf(k, ctx, "fi_wlo", [P, KT, D_MODEL], F32R)
        w_raw = pair(k, ctx, "fi_wraw", [P, D_MODEL])
        gpost = sbuf(k, ctx, "fi_gpost", [P, D_MODEL])
        mgain = sbuf(k, ctx, "fi_mgain", [P, 2])
        x = pair(k, ctx, "fi_x", [P, D_MODEL])
        z = pair(k, ctx, "fi_z", [P, NZ, P])
        e = sbuf(k, ctx, "fi_e", [P, NZ, P])
        o_f = pair(k, ctx, "fi_of", [P, 2, P])
        gq = pair(k, ctx, "fi_gq", [P, 3, P])
        hf = pair(k, ctx, "fi_hf", [P, MH, HD])
        hb = pair(k, ctx, "fi_hb", [P, MH, HD])
        dl = pair(k, ctx, "fi_dl", [P, NG, 2, HD + 1])
        od = sbuf(k, ctx, "fi_od", [P, NG, 2, HD])
        eo = sbuf(k, ctx, "fi_eo", [P, MH, HD])
        hsq = sbuf(k, ctx, "fi_hsq", [P, MH, HD])
        hst = sbuf(k, ctx, "fi_hst", [P, 3, MH])
        al = sbuf(k, ctx, "fi_al", [P, 2, 2, NG])
        am = sbuf(k, ctx, "fi_am", [P, 2, 2])
        m_hi = pair(k, ctx, "fi_mhi", [P, KT, P], F32R)
        m_lo = pair(k, ctx, "fi_mlo", [P, KT, P], F32R)
        mix = sbuf(k, ctx, "fi_mix", [P, KT, P])
        y = sbuf(k, ctx, "fi_y", [P, D_MODEL])
        xo = pair(k, ctx, "fi_xo", [P, D_MODEL])
        yst = sbuf(k, ctx, "fi_yst", [P, 4])
        ps_y = [psum(k, ctx, f"fi_ps_y{u}", [P, D_MODEL]) for u in range(2)]
        ps_o = psum(k, ctx, "fi_ps_o", [P, 512])
        ps_h = psum(k, ctx, "fi_ps_h", [P, 4, P])
        ps_d = psum(k, ctx, "fi_ps_d", [P, 4, P])
        const_in = k.sem("fi_const_in")
        wr_in = [k.sem(f"fi_wr_in{u}") for u in range(2)]
        loaded = [k.sem(f"fi_loaded{u}") for u in range(2)]
        stored = [k.sem(f"fi_stored{u}") for u in range(2)]
        (whi_ok, wlo_ok, ez_ok, z_ok, o_ok, eo_ok, hs_ok, hss_ok, hrs_a, hrs_ok, lse_ok, ea_ok, hn_ok, gqz_ok, turned,
         mix_ok, hi_ok, lo_ok, y_done, ys_ok, yr_ok, yn_ok, x_ok, chain) = (
            k.sem("fi_" + s) for s in (
                "whi_ok", "wlo_ok", "ez_ok", "z_ok", "o_ok", "eo_ok", "hs_ok", "hss_ok", "hrs_a", "hrs_ok", "lse_ok",
                "ea_ok", "hn_ok", "gqz_ok", "turned", "mix_ok", "hi_ok", "lo_ok", "y_done", "ys_ok", "yr_ok", "yn_ok",
                "x_ok", "chain"))
        block = ctx.enter_context(nc.Block())
        NB = NT // 2
        NLOAD = 3 + 1 + 1 + 2 + NG + 1
        NCHAIN = 13

        def number(n):
            return L * NT + n

        def slots(engine, front, back):
            front(0, 0, 0)
            with engine.Fori(0, NB - 1) as b:
                for u in range(2):
                    front(b * 2 + u + 1, b + u, 1 - u)
                    back(b * 2 + u, b, u)
            front(NT - 1, NB - 1, 1)
            back(NT - 2, NB - 1, 0)
            back(NT - 1, NB - 1, 1)

        @block.sync
        def _(sp):
            sp.dma_start(gpost[:], k.a["gain_post"][at(L), :].partition_broadcast(P)).then_inc(const_in, DMA)
            sp.dma_start(mgain[:], k.a["gain_mlstm"][at(L)].rearrange("a p c -> p (a c)")).then_inc(const_in, DMA)
            for t in range(KT):
                if t >= 2:
                    sp.wait_ge(wlo_ok, L * KT + t - 1)
                sp.dma_start(w_raw[t % 2][:], k.a["w_out"][at(L), t].rearrange("a p c -> p (a c)")).then_inc(wr_in[t % 2], DMA)

            def loads(n, b, u, prompt):
                a = n * P
                s = loaded[u]
                if not prompt:
                    sp.wait_ge(x_ok, number(n) - 1)
                tok = at(a, P)
                for i, ct, m in ((0, CT_MZ, 2), (2, CT_GZ, 3), (5, CT_DZ, 3)):
                    sp.dma_start(z[u][:, i:i + m, :], k.a["proj"][ct:ct + m, :, tok].rearrange("c p t -> p c t")).then_inc(s, DMA)
                sp.dma_start(o_f[u][:], k.a["proj"][CT_MO:CT_MO + 2, :, tok].rearrange("c p t -> p c t")).then_inc(s, DMA)
                sp.dma_start(gq[u][:], k.a["gqo"].rearrange("(c h) d t -> (h d) c t", h=2)[:, :, tok]).then_inc(s, DMA)
                for t, d in ((hf, 0), (hb, 1)):
                    sp.dma_start(t[u][:].rearrange("p h e -> p (h e)"), rows_of(k.a["mh"][d], a, P, 0, MH * HD)).then_inc(s, DMA)
                for g, (_, dil) in enumerate(DIL):
                    s0, s1 = (0, SEQ) if prompt else (SEQ, TOK)
                    seq = k.a["dil_out"][g][s0:s1, :].rearrange("(r j) e -> j r e", r=dil)
                    j0 = (n * (P // dil)) if prompt else (n - NTP) * (P // dil)
                    sp.dma_start(dl[u][:, g].rearrange("p h e -> p (h e)"), seq[at(j0, P // dil)]).then_inc(s, DMA)
                sp.dma_start(x[u][:], rows_of(k.a["x"], a, P, 0, D_MODEL)).then_inc(s, DMA)

            def store(n, b, u):
                sp.wait_ge(x_ok, number(n) + 1)
                sp.dma_start(rows_of(k.a["x"], n * P, P, 0, D_MODEL), xo[u][:]).then_inc(stored[u], DMA)

            loads(0, 0, 0, True)
            loads(1, 0, 1, True)
            with sp.Fori(0, NB - 1) as b:
                for u in range(2):
                    store(b * 2 + u, b, u)
                    loads(b * 2 + u + 2, b + 1, u, False)
            for u in range(2):
                store(NT - 2 + u, NB - 1, u)
            for u in range(2):
                sp.wait_ge(stored[u], (L + 1) * NB * DMA)
            sp.sem_inc(phases, 1)

        @block.gpsimd
        def _(pool):
            def front(n, b, u):
                m = number(n)
                pool.wait_ge(loaded[u], (L * NB + b + 1) * NLOAD * DMA)
                nc.gpsimd.tensor_tensor(hf[u][:], hf[u][:], hb[u][:], ALU.add).then_inc(hs_ok, 1)
                pool.wait_ge(ez_ok, m + 1)
                nc.gpsimd.tensor_tensor(z[u][:], z[u][:], e[:], ALU.mult).then_inc(z_ok, 1)
                pool.wait_ge(z_ok, m + 1)
                pool.wait_ge(lo_ok, m)
                nc.gpsimd.tensor_tensor(mix[:, 2:5, :], gq[u][:], z[u][:, 2:5, :], ALU.mult).then_inc(gqz_ok, 1)

            def back(n, b, u):
                m = number(n)
                pool.wait_ge(yn_ok, m + 1)
                pool.wait_ge(stored[u], (L * NB + b) * DMA)
                nc.gpsimd.tensor_tensor(xo[u][:], x[u][:], y[:], ALU.add).then_inc(x_ok, 1)

            slots(pool, front, back)

        @block.scalar
        def _(act):
            for t in range(KT):
                act.wait_ge(wr_in[t % 2], (L * (KT // 2) + t // 2 + 1) * DMA)
                nc.scalar.copy(w_hi[:, t, :], w_raw[t % 2][:]).then_inc(whi_ok, 1)

            def front(n, b, u):
                m = number(n)
                act.wait_ge(loaded[u], (L * NB + b + 1) * NLOAD * DMA)
                act.wait_ge(z_ok, m)
                nc.scalar.activation(e[:], z[u][:], ACT.Exp, scale=-1.0).then_inc(eo_ok, 1)
                act.wait_ge(o_ok, m + 1)
                nc.scalar.activation(eo[:], ps_o[:, 0:MH * HD].rearrange("p (h e) -> p h e", e=HD), ACT.Exp,
                                     scale=-1.0).then_inc(eo_ok, 1)
                act.wait_ge(lse_ok, m + 1)
                nc.scalar.activation(al[:, 1], al[:, 0], ACT.Exp).then_inc(ea_ok, 1)
                act.wait_ge(hss_ok, m + 1)
                nc.scalar.activation(hst[:, 1, :], hst[:, 0, :], ACT.Ln, scale=1.0 / HD, bias=cols["eps"]).then_inc(hrs_a, 1)
                act.wait_ge(hrs_a, m + 1)
                nc.scalar.activation(hst[:, 2, :], hst[:, 1, :], ACT.Exp, scale=-0.5).then_inc(hrs_ok, 1)
                act.wait_ge(mix_ok, m + 1)
                nc.scalar.copy(m_hi[u][:], mix[:]).then_inc(hi_ok, 1)

            def back(n, b, u):
                m = number(n)
                st = Steps(act, ys_ok, m * 2)
                act.wait_ge(y_done, m + 1)
                act.wait_ge(x_ok, m)
                st.mark(nc.scalar.activation(y[:], ps_y[u][:], ACT.Square, accum_out=yst[:, 0:1]))
                st.join()
                st.mark(nc.scalar.activation(yst[:, 1:2], yst[:, 0:1], ACT.Ln, scale=1.0 / D_MODEL, bias=cols["eps"]))
                st.join()
                nc.scalar.activation(yst[:, 2:3], yst[:, 1:2], ACT.Exp, scale=-0.5).then_inc(yr_ok, 1)

            slots(act, front, back)

        @block.vector
        def _(dve):
            for t in range(KT):
                dve.wait_ge(whi_ok, L * KT + t + 1)
                nc.vector.tensor_tensor(w_lo[:, t, :], w_raw[t % 2][:], w_hi[:, t, :].bitcast(F32), ALU.subtract).then_inc(wlo_ok, 1)
            dve.wait_ge(const_in, (L + 1) * 2 * DMA)

            def front(n, b, u):
                m = number(n)
                st = Steps(dve, chain, m * NCHAIN)
                dve.wait_ge(eo_ok, m * 2 + 1)
                st.mark(nc.vector.tensor_scalar(e[:], e[:], 1.0, None, ALU.add))
                dve.wait_ge(loaded[u], (L * NB + b + 1) * NLOAD * DMA)
                lse = dl[u][:, :, :, HD].rearrange("p g h -> p h g")
                st.mark(nc.vector.tensor_reduce(am[:, 0, :], lse, AX.X, ALU.max))
                st.join()
                nc.vector.reciprocal(e[:], e[:]).then_inc(ez_ok, 1)
                nc.vector.tensor_tensor(al[:, 0], lse, bc_free(am[:, 0, :], NG), ALU.subtract).then_inc(lse_ok, 1)
                dve.wait_ge(eo_ok, m * 2 + 2)
                st.mark(nc.vector.tensor_scalar(eo[:], eo[:], 1.0, None, ALU.add))
                st.join()
                st.mark(nc.vector.reciprocal(eo[:], eo[:]))
                st.join()
                dve.wait_ge(hs_ok, m + 1)
                st.mark(nc.vector.tensor_tensor(eo[:], eo[:], hf[u][:], ALU.mult))
                st.join()
                st.mark(nc.vector.tensor_tensor(hsq[:], eo[:], eo[:], ALU.mult))
                st.join()
                nc.vector.tensor_reduce(hst[:, 0, :], hsq[:], AX.X, ALU.add).then_inc(hss_ok, 1)
                dve.wait_ge(ea_ok, m + 1)
                st.mark(nc.vector.tensor_reduce(am[:, 1, :], al[:, 1], AX.X, ALU.add))
                st.join()
                st.mark(nc.vector.reciprocal(am[:, 1, :], am[:, 1, :]))
                st.join()
                st.mark(nc.vector.tensor_tensor(al[:, 1], al[:, 1], bc_free(am[:, 1, :], NG), ALU.mult))
                st.join()
                for h in range(2):
                    st.mark(nc.vector.tensor_tensor(od[:, :, h, :], dl[u][:, :, h, 0:HD],
                                                    bc_free(al[:, 1, h, :], HD), ALU.mult))
                dve.wait_ge(hrs_ok, m + 1)
                nc.vector.tensor_tensor(hf[u][:], eo[:], bc_free(hst[:, 2, :], HD), ALU.mult).then_inc(hn_ok, 1)
                dve.wait_ge(turned, m + 1)
                dve.wait_ge(z_ok, m + 1)
                for j in range(2):
                    st.mark(nc.vector.scalar_tensor_tensor(out=mix[:, j, :], in0=ps_h[:, j, :], scalar=mgain[:, j:j + 1],
                                                           in1=z[u][:, j, :], op0=ALU.mult, op1=ALU.mult))
                dve.wait_ge(gqz_ok, m + 1)
                nc.vector.tensor_tensor(mix[:, 5:8, :], ps_d[:, 0:3, :], z[u][:, 5:8, :], ALU.mult).then_inc(mix_ok, 1)
                dve.wait_ge(hi_ok, m + 1)
                nc.vector.tensor_tensor(m_lo[u][:], mix[:], m_hi[u][:].bitcast(F32), ALU.subtract).then_inc(lo_ok, 1)
                assert st.n == NCHAIN, st.n

            def back(n, b, u):
                m = number(n)
                dve.wait_ge(yr_ok, m + 1)
                nc.vector.scalar_tensor_tensor(out=y[:], in0=ps_y[u][:], scalar=yst[:, 2:3], in1=gpost[:],
                                               op0=ALU.mult, op1=ALU.mult).then_inc(yn_ok, 1)

            slots(dve, front, back)

        @block.tensor
        def _(pe):
            pe.wait_ge(wlo_ok, (L + 1) * KT)

            def turn_o(n, b, u):
                m = number(n)
                pe.wait_ge(loaded[u], (L * NB + b + 1) * NLOAD * DMA)
                for j in range(2):
                    mm = pe.transpose(ps_o[:, j * P:(j + 1) * P], o_f[u][:, j, :], ident)
                mm.then_inc(o_ok, 1)

            def turn_rest(n, b, u):
                m = number(n)
                pe.wait_ge(hn_ok, m + 1)
                h = hf[u][:].rearrange("p h e -> p (h e)")
                for j in range(2):
                    pe.transpose(ps_h[:, j, :], h[:, j * P:(j + 1) * P], ident)
                for g in range(NG):
                    mm = pe.transpose(ps_d[:, g, :], od[:, g].rearrange("p h e -> p (h e)"), ident)
                mm.then_inc(turned, 1)

            def multiply(n, b, u):
                m = number(n)
                pe.wait_ge(lo_ok, m + 1)
                for c in range(D_MODEL // 512):
                    for t in range(KT):
                        for i, (a, w) in enumerate(((m_hi, w_hi), (m_lo, w_hi), (m_hi, w_lo))):
                            mm = pe.matmul(ps_y[u][:, c * 512:(c + 1) * 512], a[u][:, t, :], w[:, t, c * 512:(c + 1) * 512],
                                           start=(t == 0 and i == 0), stop=(t == KT - 1 and i == 2))
                mm.then_inc(y_done, 1)

            turn_o(0, 0, 0)
            turn_rest(0, 0, 0)
            with pe.Fori(0, NB - 1) as b:
                for u in range(2):
                    turn_o(b * 2 + u + 1, b + u, 1 - u)
                    multiply(b * 2 + u, b, u)
                    turn_rest(b * 2 + u + 1, b + u, 1 - u)
            turn_o(NT - 1, NB - 1, 1)
            multiply(NT - 2, NB - 1, 0)
            turn_rest(NT - 1, NB - 1, 1)
            multiply(NT - 1, NB - 1, 1)



def constants():
    c = {"ident": np.eye(P, dtype=np.float32)}
    half = HD // 2
    inv = (10000.0 ** (-np.arange(0, half, 2, dtype=np.float32) / half)).astype(np.float32)

    def angles(T):
        t = np.arange(T)
        r, col = (t // 64).astype(np.float32), (t % 64).astype(np.float32)
        return np.concatenate([r[:, None] * inv, col[:, None] * inv], axis=-1)

    ang = np.concatenate([angles(SEQ), angles(DEC_SEQ)], axis=0)
    c["cos"] = np.ascontiguousarray(np.tile(np.cos(ang).T, (4, 1)).astype(np.float32))
    c["sin"] = np.ascontiguousarray(np.tile(np.sin(ang).T, (4, 1)).astype(np.float32))
    d = np.arange(P)
    c["head_ones"] = (d[:, None] // HD == d[None, :] // HD).astype(np.float32)
    swap = np.zeros((P, P), np.float32)
    for o in range(P):
        swap[o + half if o % HD < half else o - half, o] = -1.0 if o % HD < half else 1.0
    c["rope_swap"] = swap
    s = np.full(4, HD ** -0.5, np.float32)
    c["rq_scale"] = np.tile(np.array([s[0], s[0], s[0], 1.0], np.float32), (P, 1))
    c["cv_scale"] = np.tile(np.array([1.0, 1.0, s[0], s[0]], np.float32), (P, 1))
    c["oc_scale"] = np.tile(np.array([s[0], 1.0, 1.0, 1.0], np.float32), (P, 1))
    chunk = np.arange(GR) % NT
    c["carries"] = np.stack([~np.isin(chunk, (0, NTP)), ~np.isin(chunk, (NTP - 1, NT - 1))], axis=1).astype(np.float32)
    causal = np.zeros((P, 2, P), np.float32)
    causal[:, 0][d[:, None] > d[None, :]] = -BIG
    causal[:, 1][d[:, None] < d[None, :]] = -BIG
    c["causal"] = causal
    dist = np.full((NG, NT, P, KW), BIG, np.float32)
    for g, (_, dil) in enumerate(DIL):
        for n in range(NT):
            s0, T = (0, SEQ) if n < NTP else (SEQ, DEC_SEQ)
            qi = n * P - s0 + np.arange(P)[:, None]
            ki = n * P - s0 - SIDE + np.arange(KW)[None, :]
            near = (ki >= 0) & (ki < T) & (np.abs(ki - qi) <= SIDE) & (qi // (T // dil) == ki // (T // dil))
            dist[g, n][near] = np.abs(ki - qi)[near]
    c["dil_dist"] = dist
    return c


def encoder(nc, arrays):
    with ExitStack() as ctx:
        k = Kernel(nc, ctx, arrays)
        k.a["x"] = k.a["y"]
        k.dram("proj", (NCT, P, TOK))
        k.dram("mqk", (4, P, TOK))
        k.dram("tokmaj", (TOK, TM * P))
        k.dram("gqk_hi", (4, P, TOK))
        k.dram("gqk_lo", (4, P, TOK))
        k.dram("gqo", (GQ_HEADS, HD, TOK))
        k.dram("gate_ends", (2, GR, 2))
        k.dram("gate_m", (2, GR))
        k.dram("gate_M", (2, GR, P))
        k.dram("gate_dec", (2, GR))
        k.dram("mh", (2, TOK, MH * HD))
        k.dram("dil_in", (3 * NG, P, PADTOK))
        k.dram("dil_out", (NG, TOK, 2 * (HD + 1)))
        ident_t = sbuf(k, ctx, "ident", [P, P])
        col = sbuf(k, ctx, "cols", [P, 4])
        zeros = sbuf(k, ctx, "zeros", [P, SIDE])
        gate_cols = sbuf(k, ctx, "gate_cols", [P, 8, GR])
        decay = sbuf(k, ctx, "decay", [HD, 2 * GR])
        ident = ident_t[:]
        cols = {"eps": col[:, 0:1], "one": col[:, 1:2]}
        once, filled = k.sem("once_dma"), k.sem("once_fill")
        with nc.Block() as block:
            @block.vector
            def _(dve):
                nc.vector.memset(col[:, 0:1], EPS).then_inc(filled, 1)
                nc.vector.memset(col[:, 1:2], 1.0).then_inc(filled, 1)
                nc.vector.memset(zeros[:], 0.0).then_inc(filled, 1)
                dve.wait_ge(filled, 3)

            @block.sync
            def _(sp):
                sp.dma_start(k.a["x"], k.a["x_all"]).then_inc(once, DMA)
                sp.dma_start(ident_t[:], k.a["ident"]).then_inc(once, DMA)
                sp.wait_ge(filled, 3)
                for c in range(3 * NG):
                    for a in (0, SIDE + TOK):
                        sp.dma_start(k.a["dil_in"][c, :, a:a + SIDE], zeros[:]).then_inc(once, DMA)
                sp.wait_ge(once, (2 + 3 * NG * 2) * DMA)

            @block.scalar
            def _(act):
                for name, credit in CREDITS.items():
                    act.sem_inc(k.sem(name), credit)

        with nc.Fori(0, DEPTH) as L:
            with ExitStack() as held:
                h_hi = sbuf(k, held, "h_hi", [P, KT, TOK], F32R)
                h_lo = sbuf(k, held, "h_lo", [P, KT, TOK], F32R)
                pre_norm(k, L, h_hi, h_lo, ident, cols)
                project(k, L, h_hi, h_lo)
            rotate_qk(k, L, cols)
            convolve(k, L, cols)
            turn_tokens(k, L, ident)
            attend_gqa(k, L, ident)
            gate_rows(k, L, gate_cols, decay, ident, cols)
            mlstm(k, L, gate_cols, decay)
            order_classes(k, L)
            attend_dilated(k, L, ident)
            finish(k, L, ident, cols)


def laid_out(inputs):
    f = {n: np.ascontiguousarray(np.asarray(v)) for n, v in inputs.items()}
    D = f["w_in"].shape[0]
    gates0 = 4 * MH * HD
    ng = 4 * MH
    w = f["w_in"]
    w = np.concatenate([w[:, :, :gates0], w[:, :, gates0 + ng:], w[:, :, gates0:gates0 + ng],
                        np.zeros((D, D_MODEL, P - ng), w.dtype)], axis=2)
    w = w.reshape(D, KT, P, NCT, P).transpose(0, 3, 2, 1, 4).reshape(D, NCT, P, KT * P)
    taps = np.stack([f["mlstm_conv_w"][:, 0], f["mlstm_conv_w"][:, 1], f["mlstm_conv_w"][:, 2], f["mlstm_conv_b"]], axis=-1)
    gb = f["mlstm_gate_bias"].reshape(D, 4, MH)
    qk = np.stack([np.tile(f["gqa_q_norm"], (1, 2))] * 3 + [np.tile(f["gqa_k_norm"], (1, 2))], axis=-1)
    return {
        "x_all": np.concatenate([f["x_prompt"][0], f["x_sample"][0]], axis=0),
        "w_in": w,
        "w_out": f["w_out"].reshape(D, KT, P, D_MODEL),
        "gain_pre": f["norm_pre"],
        "gain_post": f["norm_post"],
        "gain_qk": qk,
        "gain_mlstm": f["mlstm_out_gain"].reshape(D, 2, P).transpose(0, 2, 1),
        "conv_par": taps.reshape(D, 4, P, 4).transpose(0, 2, 1, 3),
        "gate_bias": np.repeat(gb, NT, axis=2).transpose(0, 2, 1),
    }


def kernel(**inputs):
    from concourse import bacc
    from concourse.bass_utils import run_bass_kernel_spmd

    nc = bacc.Bacc("TRN2", target_bir_lowering=False, num_devices=1)
    data = {n: np.ascontiguousarray(v) for n, v in (laid_out(inputs) | constants()).items()}
    arrays = {n: nc.dram_tensor(f"in_{n}", list(v.shape), F32, kind="ExternalInput").ap() for n, v in data.items()}
    arrays["y"] = nc.dram_tensor("y", [TOK, D_MODEL], F32, kind="ExternalOutput").ap()
    encoder(nc, arrays)
    y = run_bass_kernel_spmd(nc, [{f"in_{n}": v for n, v in data.items()}], core_ids=[0]).results[0]["y"]
    return y[None, :SEQ], y[None, SEQ:]
```

```python
from contextlib import ExitStack

import numpy as np

import concourse.bass as bass
from concourse import mybir

F32 = mybir.dt.float32
F32R = mybir.dt.float32r
ALU = mybir.AluOpType
ACT = mybir.ActivationFunctionType
AX = mybir.AxisListType

P = 128
D_MODEL = 1024
KT = D_MODEL // P
SEQ, DEC_SEQ = 256, 2048
TOK = SEQ + DEC_SEQ
NT = TOK // P
NTP = SEQ // P
DEPTH = 2
HD = 64
EPS = 1e-6
DMA = 16

CT_MQ, CT_MK, CT_MV, CT_MO, CT_MZ = 0, 2, 4, 6, 8
CT_GQ, CT_GK, CT_GV, CT_GZ = 10, 13, 14, 15
CT_DQ, CT_DK, CT_DV, CT_DZ = 18, 21, 24, 27
CT_GATES = 30
NCT = 31

CHUNK = 384
NCH = TOK // CHUNK

GQ_HEADS, KV_HEADS = 6, 2
GQ_PER_KV = GQ_HEADS // KV_HEADS
QC = 512
NQC = DEC_SEQ // QC
DIL = ((128, 1), (512, 4), (2048, 16))
NG = len(DIL)
SIDE = 64
PADTOK = SIDE + TOK + SIDE
MH = 4
GR = MH * NT
BIG = 1.0e30


class Steps:

    def __init__(self, engine, sem, base):
        self.engine, self.sem, self.base, self.n = engine, sem, base, 0

    def mark(self, instruction):
        instruction.then_inc(self.sem, 1)
        self.n += 1

    def join(self):
        self.engine.wait_ge(self.sem, self.base + self.n)


CREDITS = {
    "proj_wlo": 2, "proj_acc": 2 * NCH, "proj_ev_act": NCH // 2, "proj_ev_dve": NCH // 2,
    "ga_exped": 2, "ga_pv_done": 2, "ga_max_read": 2, "ga_o_ok": 2,
    "ml_w_ok": 2, "ml_at_ok": 2, "ml_state_ok": 2, "ml_mm_ok": 4,
    "pn_h_ok": 1, 
    "oc_ok0": 1, "oc_ok1": 1, "oc_ok2": 1, 
    "dl_pv_ok": 2, "dl_bias_ok": 2, "dl_vc_ok": 2, "dl_vt_ok": 2, "dl_pt_ok": 2, "dl_out_ok": 2, "dl_p_ok": 2, "dl_turned": 2,
    "dl_lse_ok": 2, "fi_z_ok": 1, "fi_o_ok": 1, "fi_lo_ok": 1, "fi_x_ok": 1,
    "stored0": DMA, "stored1": DMA, "stored2": DMA, **{f"ml_stored{u}{d}": DMA for u in range(2) for d in range(2)},
}


STORES = {"project": ((NCT + 1) // 2, NCT // 2, 0), "prepare": (8, 8, 0),
          "gqa": (GQ_HEADS * (NQC + 1) // 2,) * 2 + (0,), "order": (3, 3, 3), "dilated": (NG * NT // 2,) * 2 + (0,),
          "finish": (NT // 2, NT // 2, 0)}
CONSTS = {"prepare": 8, "mlstm": 1, "order": 1, "finish": 2}


def stored_value(L, step, u, n):
    steps = list(STORES)
    before = sum(STORES[s][u] for s in steps[:steps.index(step)])
    return (L * sum(STORES[s][u] for s in steps) + (n + before)) * DMA + DMA


def consts_value(L, step):
    steps = list(CONSTS)
    return (L * sum(CONSTS.values()) + sum(CONSTS[s] for s in steps[:steps.index(step) + 1])) * DMA


class Kernel:

    def __init__(self, nc, ctx, arrays):
        self.nc, self.ctx, self.a = nc, ctx, arrays
        self.sems = {}

    def sem(self, name):
        if name not in self.sems:
            self.sems[name] = self.ctx.enter_context(self.nc.semaphore(name))
        return self.sems[name]

    def dram(self, name, shape):
        self.a[name] = self.nc.dram_tensor(name, list(shape), F32).ap()
        return self.a[name]


def sbuf(k, ctx, name, shape, dtype=F32):
    return ctx.enter_context(k.nc.sbuf_tensor(name, list(shape), dtype))


def psum(k, ctx, name, shape):
    return ctx.enter_context(k.nc.psum_tensor(name, list(shape), F32))


def pair(k, ctx, name, shape, dtype=F32):
    return [sbuf(k, ctx, f"{name}{u}", shape, dtype) for u in range(2)]


def at(i, n=1):
    return bass.ds(i, n)


def bc_free(ap, n):
    return ap.unsqueeze(2).to_broadcast([*ap.shape, n])


def rows_of(dram, row0, nrows, col0, ncols):
    return dram[at(row0, nrows), at(col0, ncols)]


def pre_norm(k, L, h_hi, h_lo, ident, cols):
    nc = k.nc
    NB = NT // 2
    with ExitStack() as ctx:
        x = pair(k, ctx, "pn_x", [P, D_MODEL])
        hn = pair(k, ctx, "pn_hn", [P, D_MODEL])
        junk = sbuf(k, ctx, "pn_junk", [P, D_MODEL])
        gain = sbuf(k, ctx, "pn_gain", [P, D_MODEL])
        stat = pair(k, ctx, "pn_stat", [P, 4])
        tr = [psum(k, ctx, f"pn_tr{u}", [P, KT, P]) for u in range(2)]
        x_in = [k.sem(f"pn_x_in{u}") for u in range(2)]
        gain_in, stats, rstd_ok, h_ok, turned, hi_ok, lo_ok = (
            k.sem("pn_" + s) for s in ("gain_in", "stats", "rstd_ok", "h_ok", "turned", "hi_ok", "lo_ok"))
        block = ctx.enter_context(nc.Block())

        @block.sync
        def _(sp):
            sp.dma_start(gain[:], k.a["gain_pre"][at(L), :].partition_broadcast(P)).then_inc(gain_in, DMA)
            with sp.Fori(0, NB) as b:
                for u in range(2):
                    sp.wait_ge(h_ok, (L * NB + b) * 2 + 1)
                    sp.dma_start(x[u][:], rows_of(k.a["x"], b * 2 * P + u * P, P, 0, D_MODEL)).then_inc(x_in[u], DMA)

        @block.scalar
        def _(act):
            with act.Fori(0, NB) as b:
                n = L * NB + b
                for u in range(2):
                    st = Steps(act, stats, (n * 2 + u) * 2)
                    act.wait_ge(x_in[u], (n + 1) * DMA)
                    st.mark(nc.scalar.activation(junk[:], x[u][:], ACT.Square, accum_out=stat[u][:, 0:1]))
                    st.join()
                    st.mark(nc.scalar.activation(stat[u][:, 1:2], stat[u][:, 0:1], ACT.Ln,
                                                 scale=1.0 / D_MODEL, bias=cols["eps"]))
                    st.join()
                    nc.scalar.activation(stat[u][:, 2:3], stat[u][:, 1:2], ACT.Exp, scale=-0.5).then_inc(rstd_ok, 1)
                for u in range(2):
                    act.wait_ge(turned, n * 2 + u + 1)
                    nc.scalar.copy(h_hi[:, :, at(b * 2 * P + u * P, P)], tr[u][:]).then_inc(hi_ok, 1)

        @block.vector
        def _(dve):
            with dve.Fori(0, NB) as b:
                n = L * NB + b
                dve.wait_ge(gain_in, (L + 1) * DMA)
                for u in range(2):
                    dve.wait_ge(rstd_ok, n * 2 + u + 1)
                    nc.vector.scalar_tensor_tensor(out=hn[u][:], in0=x[u][:], scalar=stat[u][:, 2:3], in1=gain[:],
                                                   op0=ALU.mult, op1=ALU.mult).then_inc(h_ok, 1)
                for u in range(2):
                    dve.wait_ge(hi_ok, n * 2 + u + 1)
                    tile = at(b * 2 * P + u * P, P)
                    nc.vector.tensor_tensor(h_lo[:, :, tile], tr[u][:], h_hi[:, :, tile].bitcast(F32),
                                            ALU.subtract).then_inc(lo_ok, 1)

        @block.tensor
        def _(pe):
            with pe.Fori(0, NB) as b:
                n = L * NB + b
                for u in range(2):
                    pe.wait_ge(h_ok, n * 2 + u + 2)
                    for j in range(KT):
                        last = pe.transpose(tr[u][:, j, :], hn[u][:, j * P:(j + 1) * P], ident)
                    last.then_inc(turned, 1)


def project(k, L, h_hi, h_lo):
    nc = k.nc
    phases = k.sem("phases_stored")
    NB = NCT // 2
    with ExitStack() as ctx:
        w = pair(k, ctx, "pj_w", [P, KT, P])
        w_hi = pair(k, ctx, "pj_whi", [P, KT, P], F32R)
        w_lo = pair(k, ctx, "pj_wlo", [P, KT, P], F32R)
        stage = pair(k, ctx, "pj_stage", [P, TOK])
        acc = [psum(k, ctx, f"pj_acc{c}", [P, 512]) for c in range(NCH)]
        w_in = [k.sem(f"proj_w_in{u}") for u in range(2)]
        stored = [k.sem(f"stored{u}") for u in range(2)]
        whi, wlo, done = k.sem("proj_whi"), k.sem("proj_wlo"), k.sem("proj_acc")
        ev_act, ev_dve = k.sem("proj_ev_act"), k.sem("proj_ev_dve")
        cnt = (L * ((NCT + 1) // 2), L * (NCT // 2))
        block = ctx.enter_context(nc.Block())

        def slots(engine, slot):
            with engine.Fori(0, NB) as b:
                for u in range(2):
                    slot(b * 2 + u, b, u, False)
            slot(NCT - 1, NB, (NCT - 1) % 2, True)

        @block.sync
        def _(sp):
            def load(ct, b, u):
                sp.wait_ge(wlo, L * NCT + ct + 1)
                sp.dma_start(w[u][:], k.a["w_in"][at(L), at(ct)].rearrange("a b p (t c) -> p (a b t) c", c=P)
                             ).then_inc(w_in[u], DMA)

            def slot(ct, b, u, last):
                if not last:
                    load(ct + 1, b + u, 1 - u)
                sp.wait_ge(ev_act, (L * NCT + ct + 2) * (NCH // 2))
                sp.wait_ge(ev_dve, (L * NCT + ct + 2) * (NCH // 2))
                sp.dma_start(k.a["proj"][at(ct)].rearrange("a p t -> p (a t)"), stage[u][:]).then_inc(stored[u], DMA)

            load(0, 0, 0)
            slots(sp, slot)
            for u in range(2):
                sp.wait_ge(stored[u], stored_value(L, "project", u, (NCT + 1 - u) // 2))
            sp.sem_inc(phases, 1)

        def evacuate(engine, copy, ct, b, u, parity, sem):
            engine.wait_ge(stored[u], stored_value(L, "project", u, b))
            for c in range(parity, NCH, 2):
                engine.wait_ge(done, (L * NCT + ct) * NCH + c + 1 + 2 * NCH)
                copy(stage[u][:, c * CHUNK:(c + 1) * CHUNK], acc[c][:, 0:CHUNK]).then_inc(sem, 1)

        @block.scalar
        def _(act):
            def split(ct, b, u):
                act.wait_ge(w_in[u], (cnt[u] + b + 1) * DMA)
                act.wait_ge(done, (L * NCT + ct + 1) * NCH - NCH + NCH)
                nc.scalar.copy(w_hi[u][:], w[u][:]).then_inc(whi, 1)

            def slot(ct, b, u, last):
                if not last:
                    split(ct + 1, b + u, 1 - u)
                evacuate(act, nc.scalar.copy, ct, b, u, 0, ev_act)

            split(0, 0, 0)
            slots(act, slot)

        @block.vector
        def _(dve):
            def split(ct, b, u):
                dve.wait_ge(whi, L * NCT + ct + 1)
                nc.vector.tensor_tensor(w_lo[u][:], w[u][:], w_hi[u][:].bitcast(F32), ALU.subtract).then_inc(wlo, 1)

            def slot(ct, b, u, last):
                if not last:
                    split(ct + 1, b + u, 1 - u)
                evacuate(dve, nc.vector.tensor_copy, ct, b, u, 1, ev_dve)

            split(0, 0, 0)
            slots(dve, slot)

        @block.tensor
        def _(pe):
            def slot(ct, b, u, last):
                pe.wait_ge(wlo, L * NCT + ct + 1 + 2)
                for c in range(NCH):
                    pe.wait_ge((ev_act, ev_dve)[c % 2], (L * NCT + ct) * (NCH // 2) + c // 2 + 1)
                    tok = slice(c * CHUNK, (c + 1) * CHUNK)
                    for t in range(KT):
                        for i, (wt, ht) in enumerate(((w_hi, h_hi), (w_hi, h_lo), (w_lo, h_hi))):
                            mm = pe.matmul(acc[c][:, 0:CHUNK], wt[u][:, t, :], ht[:, t, tok],
                                           start=(t == 0 and i == 0), stop=(t == KT - 1 and i == 2))
                    mm.then_inc(done, 1)

            slots(pe, slot)


PIECES = ((0, SEQ + 2 * QC), (SEQ + 2 * QC, TOK))
TM = 5


def prepare(k, L, gate_cols, decay, ident, cols):
    nc = k.nc
    phases = k.sem("phases_stored")
    W = PIECES[0][1]
    NJ = 4
    SMOOTH = (2, 3, 0, 1)
    TURNS = ((4, "load", CT_GV), (2, "load", CT_MV), (0, "smoothed", 0), (3, "load", CT_MV + 1), (1, "smoothed", 1))
    GROUPS = -(-NT // 4)
    TRA, TRD = (TM * GROUPS + 1) // 2, TM * GROUPS // 2
    with ExitStack() as ctx:
        raw = [sbuf(k, ctx, f"rq_raw{u}", [P, z - a]) for u, (a, z) in enumerate(PIECES)]
        sq, rs, qn, t1 = ([sbuf(k, ctx, f"rq_{x}{u}", [P, z - a]) for u, (a, z) in enumerate(PIECES)]
                          for x in ("sq", "rs", "qn", "t1"))
        hi, lo = ([sbuf(k, ctx, f"rq_{x}{u}", [P, z - a], F32R) for u, (a, z) in enumerate(PIECES)] for x in ("hi", "lo"))
        cos, sin = (sbuf(k, ctx, "rq_" + x, [P, TOK]) for x in ("cos", "sin"))
        blk, rot = (sbuf(k, ctx, "rq_" + x, [P, P]) for x in ("blk", "rot"))
        gain, scale = (sbuf(k, ctx, "rq_" + x, [P, 4]) for x in ("gain", "scale"))
        x, y = pair(k, ctx, "sm_x", [P, TOK]), pair(k, ctx, "sm_y", [P, TOK])
        e = sbuf(k, ctx, "sm_e", [P, TOK])
        par = sbuf(k, ctx, "sm_par", [P, 4, 4])
        sm_scale = sbuf(k, ctx, "sm_scale", [P, 4])
        tv = pair(k, ctx, "tt_f", [P, TOK])
        t_out = pair(k, ctx, "tt_t", [P, NT, P])

        def both(name, shape=(GR, P)):
            return pair(k, ctx, "gr_" + name, shape)

        gi, gf, ge, mn, b, a_, M, bm, wi, em, kws = (both(n) for n in ("i", "f", "e", "mn", "b", "a", "M", "bm", "wi", "em", "kws"))
        ends, m_col, n_end, dec = both("ends", (GR, 2)), both("mcol", (GR, 1)), both("nend", (GR, 2)), both("dec", (GR, 1))
        m_in, m_out = both("m_in", (MH, NT, 2)), both("m_out", (MH, NT))
        zero = sbuf(k, ctx, "gr_zero", [GR, P])
        bias = sbuf(k, ctx, "gr_bias", [GR, 4])
        carries = sbuf(k, ctx, "gr_carries", [GR, 2])
        ss, rx = psum(k, ctx, "rq_ss", [P, 3 * 512]), psum(k, ctx, "rq_rx", [P, 3 * 512])
        tr = [psum(k, ctx, f"tt_tr{u}", [P, 4, P]) for u in range(2)]
        const_in, gain_ok = k.sem("consts_in"), k.sem("rq_gain_ok")
        raw_in, x_in, tv_in = ([k.sem(f"{n}{u}") for u in range(2)] for n in ("rq_raw_in", "sm_x_in", "tt_in"))
        stored, y_stored, t_stored = ([k.sem(f"{n}{u}") for u in range(2)] for n in ("stored", "sm_stored", "tt_stored"))
        sq_ok, ss_ok, ln_ok, rs_ok, qn_ok, t1_ok, rx_ok, rs_sin_ok, sum_ok, hi_ok, lo_ok = (
            k.sem("rq_" + n) for n in ("sq_ok", "ss_ok", "ln_ok", "rs_ok", "qn_ok", "t1_ok", "rx_ok", "sin_ok",
                                       "sum_ok", "hi_ok", "lo_ok"))
        mid_ok, conv_ok, log_ok, logsig_ok, sig_ok, chain, smooth_ok = (
            k.sem("sm_" + n) for n in ("mid_ok", "conv_ok", "log_ok", "logsig_ok", "sig_ok", "chain", "smooth_ok"))
        turned, tr_act, tr_dve = k.sem("tt_turned"), k.sem("tt_act"), k.sem("tt_dve")
        g_in, hop, g_out = k.sem("gr_g_in"), k.sem("gr_hop"), k.sem("gr_out")
        sa, sv, g_turned, g_done = k.sem("gr_act"), k.sem("gr_dve"), k.sem("gr_turned"), k.sem("gr_done")
        block = ctx.enter_context(nc.Block())
        NA, NV = 14, 32
        NA1, NV1, NV2, NV3 = 6, 14, 20, 32
        NIN = 6

        def item(j, u):
            return L * (NJ * 2) + (j * 2 + u)

        def turns_of(j):
            return {0: (0, 1), 1: (2, 3), 2: (4, None), 3: (None, None)}[j]

        def groups(i):
            return [(i * GROUPS + g, g * 4, min(4, NT - g * 4)) for g in range(GROUPS)]

        def copy_turned(engine, copy, parity, i):
            if i is None:
                return
            if i >= 2:
                engine.wait_ge(t_stored[i % 2], (L * ((TM + 1 - i % 2) // 2) + i // 2) * DMA)
            for g, tile, n in groups(i):
                if g % 2 == parity:
                    if g == (i + 1) * GROUPS - 1:
                        engine.wait_ge((tr_dve, tr_act)[parity], L * (TRD, TRA)[parity] + (g - 1) // 2 + 1)
                    engine.wait_ge(turned, L * TM * GROUPS + g + 1)
                    copy(t_out[i % 2][:, tile:tile + n, :], tr[g % 2][:, 0:n, :]).then_inc((tr_act, tr_dve)[parity], 1)

        def ends_of(t, d):
            return t[d][:, P - 1:P] if d == 0 else t[d][:, 0:1]

        def flow(t, d):
            return t[d][:, :] if d == 0 else t[d][:, ::-1]

        @block.sync
        def _(sp):
            def load_rotate(j):
                for u, (a, z) in enumerate(PIECES):
                    if j:
                        sp.wait_ge(qn_ok, item(j - 1, u) + 1)
                    sp.dma_start(raw[u][:], k.a["proj"][CT_GQ + j, :, a:z]).then_inc(raw_in[u], DMA)

            def load_smooth(j):
                if j >= 2:
                    sp.wait_ge(conv_ok, L * NJ + j - 1)
                sp.dma_start(x[j % 2][:], k.a["proj"][CT_MQ + SMOOTH[j]]).then_inc(x_in[j % 2], DMA)

            def load_turn(i, w):
                if w >= 2:
                    sp.wait_ge(turned, L * TM * GROUPS + GROUPS)
                sp.dma_start(tv[w % 2][:], k.a["proj"][TURNS[i][2]]).then_inc(tv_in[w % 2], DMA)

            def store_rotate(j):
                for u, (a, z) in enumerate(PIECES):
                    for half, ok, name in ((hi, hi_ok, "gqk_hi"), (lo, lo_ok, "gqk_lo")):
                        sp.wait_ge(ok, item(j, u) + 1)
                        sp.dma_start(k.a[name][j, :, a:z], half[u][:].bitcast(F32)).then_inc(stored[u], DMA)

            def store_smooth(j):
                sp.wait_ge(smooth_ok, L * NJ + j + 1)
                sp.dma_start(k.a["mqk"][SMOOTH[j]], y[j % 2][:]).then_inc(y_stored[j % 2], DMA)

            def store_turn(i):
                if i is not None:
                    last = (i + 1) * GROUPS - 1
                    sp.wait_ge((tr_act, tr_dve)[last % 2], L * (TRA, TRD)[last % 2] + last // 2 + 1)
                    c = TURNS[i][0]
                    sp.dma_start(k.a["tokmaj"][:, c * P:(c + 1) * P].rearrange("(n p) d -> p n d", p=P),
                                 t_out[i % 2][:]).then_inc(t_stored[i % 2], DMA)

            def ends_to_heads():
                sp.wait_ge(sv, L * NV + NV1)
                for d in range(2):
                    sp.dma_start(k.a["gate_ends"][d], ends[d][:]).then_inc(hop, DMA)
                sp.wait_ge(hop, (L * 8 + 2) * DMA)
                for d in range(2):
                    sp.dma_start(m_in[d][:], k.a["gate_ends"][d].rearrange("(h c) x -> h c x", h=MH)).then_inc(hop, DMA)

            def stabilisers_to_chunks():
                sp.wait_ge(sv, L * NV + NV2)
                for d in range(2):
                    sp.dma_start(k.a["gate_m"][d].rearrange("(h c) -> h c", h=MH), m_out[d][:]).then_inc(hop, DMA)
                sp.wait_ge(hop, (L * 8 + 6) * DMA)
                for d in range(2):
                    sp.dma_start(m_col[d][:], k.a["gate_m"][d].rearrange("(p x) -> p x", x=1)).then_inc(hop, DMA)

            def store_gates():
                sp.wait_ge(sv, L * NV + NV3)
                for d in range(2):
                    sp.dma_start(k.a["gate_M"][d], M[d][:]).then_inc(g_out, DMA)
                    sp.dma_start(k.a["gate_dec"][d].rearrange("(p x) -> p x", x=1), dec[d][:]).then_inc(g_out, DMA)
                sp.wait_ge(g_out, (L * 5 + 4) * DMA)
                sp.dma_start(decay[:], k.a["gate_dec"].rearrange("d p -> (d p)").partition_broadcast(HD)).then_inc(g_out, DMA)

            load_rotate(0)
            load_smooth(0)
            sp.dma_start(par[:], k.a["conv_par"][at(L)].rearrange("a p c j -> p (a c) j")).then_inc(const_in, DMA)
            sp.dma_start(gain[:], k.a["gain_qk"][at(L)].rearrange("a p c -> p (a c)")).then_inc(const_in, DMA)
            for dst, src in ((sm_scale, "cv_scale"), (blk, "head_ones"), (rot, "rope_swap"), (scale, "rq_scale")):
                sp.dma_start(dst[:], k.a[src]).then_inc(const_in, DMA)
            sp.dma_start(bias[:], k.a["gate_bias"][at(L)].rearrange("a p c -> p (a c)")).then_inc(g_in, DMA)
            sp.dma_start(carries[:], k.a["carries"]).then_inc(g_in, DMA)
            for d in range(2):
                for t, r in ((gi, 0), (gf, MH)):
                    rows = k.a["proj"][CT_GATES, d * 2 * MH + r:d * 2 * MH + r + MH, :]
                    sp.dma_start(t[d][:], rows.rearrange("h (c l) -> (h c) l", l=P)).then_inc(g_in, DMA)
            for dst, src in ((cos, "cos"), (sin, "sin")):
                sp.dma_start(dst[:], k.a[src]).then_inc(const_in, DMA)
            load_turn(0, 0)
            load_turn(1, 1)
            for j in range(NJ):
                if j + 1 < NJ:
                    load_smooth(j + 1)
                    load_rotate(j + 1)
                if j == 1:
                    load_turn(3, 2)
                if j < 3:
                    (ends_to_heads, stabilisers_to_chunks, store_gates)[j]()
                store_turn(turns_of(j)[0])
                store_rotate(j)
                store_smooth(j)
                store_turn(turns_of(j)[1])
            for u in range(2):
                sp.wait_ge(stored[u], stored_value(L, "prepare", u, NJ * 2))
                sp.wait_ge(y_stored[u], (L + 1) * (NJ // 2) * DMA)
                sp.wait_ge(t_stored[u], (L + 1) * ((TM + 1 - u) // 2) * DMA)
            sp.wait_ge(g_out, (L + 1) * 5 * DMA)
            sp.sem_inc(phases, 1)

        @block.scalar
        def _(act):
            gates = Steps(act, sa, L * NA)

            def square(j, u):
                act.wait_ge(raw_in[u], (L * NJ + j + 1) * DMA)
                if j:
                    act.wait_ge(rs_ok, item(j - 1, u) + 1)
                nc.scalar.activation(sq[u][:], raw[u][:], ACT.Square).then_inc(sq_ok, 1)

            def rsqrt(j, u):
                n, m = item(j, u), PIECES[u][1] - PIECES[u][0]
                act.wait_ge(ss_ok, n + 1)
                nc.scalar.activation(sq[u][:], ss[:, 0:m], ACT.Ln, scale=1.0 / HD, bias=cols["eps"]).then_inc(ln_ok, 1)
                act.wait_ge(ln_ok, n + 1)
                if j:
                    act.wait_ge(qn_ok, item(j - 1, u) + 1)
                nc.scalar.activation(rs[u][:], sq[u][:], ACT.Exp, scale=-0.5).then_inc(rs_ok, 1)

            def high_part(j, u):
                act.wait_ge(sum_ok, item(j, u) + 1)
                act.wait_ge(stored[u], stored_value(L, "prepare", u, j * 2))
                nc.scalar.copy(hi[u][:], t1[u][:]).then_inc(hi_ok, 1)

            def middle_tap(j):
                u, ct = j % 2, SMOOTH[j]
                act.wait_ge(x_in[u], (L * (NJ // 2) + j // 2 + 1) * DMA)
                if j >= 2:
                    act.wait_ge(y_stored[u], (L * (NJ // 2) + j // 2) * DMA)
                nc.scalar.activation(y[u][:], x[u][:], ACT.Identity, scale=par[:, ct, 1:2], bias=par[:, ct, 3:4]).then_inc(mid_ok, 1)

            def log_part(j):
                act.wait_ge(conv_ok, L * NJ + j + 1)
                if j:
                    act.wait_ge(smooth_ok, L * NJ + j)
                nc.scalar.activation(e[:], y[j % 2][:], ACT.Abs).then_inc(log_ok, 1)
                act.wait_ge(log_ok, (L * NJ + j) * 3 + 1)
                nc.scalar.activation(e[:], e[:], ACT.Exp, scale=-1.0).then_inc(log_ok, 1)
                act.wait_ge(log_ok, (L * NJ + j) * 3 + 2)
                nc.scalar.activation(e[:], e[:], ACT.Ln, bias=cols["one"]).then_inc(log_ok, 1)

            def sigmoid(j):
                act.wait_ge(logsig_ok, L * NJ + j + 1)
                nc.scalar.activation(e[:], e[:], ACT.Exp).then_inc(sig_ok, 1)

            def gate_logs():
                st = gates
                act.wait_ge(g_in, (L + 1) * NIN * DMA)
                for d in range(2):
                    st.mark(nc.scalar.activation(ge[d][:], gf[d][:], ACT.Abs, bias=bias[:, 2 * d + 1:2 * d + 2]))
                for d in range(2):
                    st.join()
                    st.mark(nc.scalar.activation(ge[d][:], ge[d][:], ACT.Exp, scale=-1.0))
                for d in range(2):
                    st.join()
                    st.mark(nc.scalar.activation(ge[d][:], ge[d][:], ACT.Ln, bias=cols["one"][0:GR]))
                assert st.n == NA1

            def gate_weights():
                st = gates
                act.wait_ge(sv, L * NV + NV2 + 8)
                for d in range(2):
                    st.mark(nc.scalar.activation(wi[d][:], M[d][:], ACT.Exp, scale=-1.0, bias=m_col[d][:, 0:1]))
                    st.mark(nc.scalar.activation(em[d][:], bm[d][:], ACT.Exp, scale=-1.0))
                    st.mark(nc.scalar.activation(kws[d][:], a_[d][:], ACT.Exp, bias=n_end[d][:, 0:1]))
                    st.mark(nc.scalar.activation(dec[d][:], n_end[d][:, 0:1], ACT.Exp, bias=m_col[d][:, 0:1]))
                assert st.n == NA

            act.wait_ge(const_in, consts_value(L, "prepare"))
            for j in range(NJ):
                square(j, 0)
                square(j, 1)
                middle_tap(j)
                if j == 0:
                    gate_logs()
                rsqrt(j, 0)
                rsqrt(j, 1)
                copy_turned(act, nc.scalar.copy, 0, turns_of(j)[0])
                if j == 2:
                    gate_weights()
                log_part(j)
                high_part(j, 0)
                high_part(j, 1)
                sigmoid(j)
                copy_turned(act, nc.scalar.copy, 0, turns_of(j)[1])
            for d in range(2):
                act.wait_ge(g_turned, L * 2 + d + 1)
                nc.scalar.copy(gate_cols[:, d * 4:d * 4 + 4, :], tr[d][:, :, 0:GR]).then_inc(g_done, 1)

        @block.vector
        def _(dve):
            gates = Steps(dve, sv, L * NV)

            def normalise(j, u):
                n = item(j, u)
                dve.wait_ge(rs_ok, n + 1)
                if j:
                    dve.wait_ge(sum_ok, item(j - 1, u) + 1)
                nc.vector.scalar_tensor_tensor(out=qn[u][:], in0=raw[u][:], scalar=gain[:, j:j + 1], in1=rs[u][:],
                                               op0=ALU.mult, op1=ALU.mult).then_inc(qn_ok, 1)

            def add_turn(j, u):
                n, (a, z) = item(j, u), PIECES[u]
                dve.wait_ge(t1_ok, n + 1)
                dve.wait_ge(rx_ok, n + 1)
                nc.vector.tensor_tensor(qn[u][:], rx[:, 0:z - a], sin[:, a:z], ALU.mult).then_inc(rs_sin_ok, 1)
                dve.wait_ge(rs_sin_ok, n + 1)
                nc.vector.tensor_tensor(t1[u][:], t1[u][:], qn[u][:], ALU.add).then_inc(sum_ok, 1)

            def low_part(j, u):
                dve.wait_ge(hi_ok, item(j, u) + 1)
                nc.vector.tensor_tensor(lo[u][:], t1[u][:], hi[u][:].bitcast(F32), ALU.subtract).then_inc(lo_ok, 1)

            def outer_taps(j):
                u, ct = j % 2, SMOOTH[j]
                st = Steps(dve, chain, (L * NJ + j) * 3)
                dve.wait_ge(mid_ok, L * NJ + j + 1)
                for s0, s1 in ((0, SEQ), (SEQ, TOK)):
                    st.mark(nc.vector.scalar_tensor_tensor(out=y[u][:, s0 + 1:s1], in0=x[u][:, s0:s1 - 1],
                                                           scalar=par[:, ct, 0:1], in1=y[u][:, s0 + 1:s1],
                                                           op0=ALU.mult, op1=ALU.add))
                for i, (s0, s1) in enumerate(((0, SEQ), (SEQ, TOK))):
                    st.join()
                    ins = nc.vector.scalar_tensor_tensor(out=y[u][:, s0:s1 - 1], in0=x[u][:, s0 + 1:s1],
                                                         scalar=par[:, ct, 2:3], in1=y[u][:, s0:s1 - 1],
                                                         op0=ALU.mult, op1=ALU.add)
                    if i == 0:
                        st.mark(ins)
                    else:
                        ins.then_inc(conv_ok, 1)

            def log_sigmoid(j):
                dve.wait_ge(log_ok, (L * NJ + j + 1) * 3)
                nc.vector.scalar_tensor_tensor(out=e[:], in0=y[j % 2][:], scalar=0.0, in1=e[:], op0=ALU.min,
                                               op1=ALU.subtract).then_inc(logsig_ok, 1)

            def gated(j):
                u, ct = j % 2, SMOOTH[j]
                dve.wait_ge(sig_ok, L * NJ + j + 1)
                nc.vector.scalar_tensor_tensor(out=y[u][:], in0=y[u][:], scalar=sm_scale[:, ct:ct + 1], in1=e[:],
                                               op0=ALU.mult, op1=ALU.mult).then_inc(smooth_ok, 1)

            def gate_sums():
                st = gates
                st.mark(nc.vector.memset(zero[:], 0.0))
                st.mark(nc.vector.memset(m_out[0][:], 0.0))
                st.mark(nc.vector.memset(m_out[1][:], 0.0))
                dve.wait_ge(g_in, (L + 1) * NIN * DMA)
                for d in range(2):
                    st.mark(nc.vector.tensor_scalar(mn[d][:], gf[d][:], bias[:, 2 * d + 1:2 * d + 2], 0.0, ALU.add, ALU.min))
                dve.wait_ge(sa, L * NA + NA1)
                for d in range(2):
                    st.join()
                    st.mark(nc.vector.tensor_tensor(mn[d][:], mn[d][:], ge[d][:], ALU.subtract))
                st.join()
                for d in range(2):
                    st.mark(nc.vector.tensor_tensor_scan(flow(b, d), flow(mn, d), zero[:], 0.0, ALU.add, ALU.add))
                st.join()
                for d in range(2):
                    st.mark(nc.vector.scalar_tensor_tensor(out=a_[d][:], in0=gi[d][:], scalar=bias[:, 2 * d:2 * d + 1],
                                                           in1=b[d][:], op0=ALU.add, op1=ALU.subtract))
                st.join()
                nc.vector.tensor_copy(ends[0][:, 1:2], ends_of(b, 0))
                nc.vector.tensor_copy(ends[1][:, 1:2], ends_of(b, 1))
                st.mark(nc.vector.tensor_reduce(ends[0][:, 0:1], a_[0][:], AX.X, ALU.max))
                st.mark(nc.vector.tensor_reduce(ends[1][:, 0:1], a_[1][:], AX.X, ALU.max))
                st.mark(nc.vector.memset(n_end[0][:], 0.0))
                assert st.n == NV1, st.n

            def gate_stabilisers():
                st = gates
                dve.wait_ge(hop, (L * 8 + 4) * DMA)

                def run(d, out_, in_):
                    st.mark(nc.vector.tensor_tensor_scan(m_out[d][:, out_], m_in[d][:, in_, 0], m_in[d][:, in_, 1], 0.0,
                                                         ALU.max, ALU.add))

                run(0, slice(1, NTP), slice(0, NTP - 1))
                run(0, slice(NTP + 1, NT), slice(NTP, NT - 1))
                run(1, slice(0, NTP - 1), slice(1, NTP))
                run(1, slice(NT - 2, NTP - 1, -1), slice(NT - 1, NTP, -1))
                st.mark(nc.vector.memset(n_end[1][:], 0.0))
                st.mark(nc.vector.memset(n_end[0][:], 0.0))
                assert st.n == NV2, st.n

            def gate_maxima():
                st = gates
                dve.wait_ge(hop, (L + 1) * 8 * DMA)
                for d in range(2):
                    st.mark(nc.vector.tensor_tensor_scan(flow(M, d), flow(a_, d), zero[:], m_col[d][:, 0:1], ALU.max, ALU.add))
                st.join()
                for d in range(2):
                    st.mark(nc.vector.tensor_tensor(bm[d][:], b[d][:], M[d][:], ALU.add))
                    st.mark(nc.vector.tensor_scalar(n_end[d][:, 0:1], ends_of(M, d), -1.0, None, ALU.mult))
                for d in range(2):
                    st.mark(nc.vector.tensor_scalar(n_end[d][:, 1:2], ends_of(M, d), -1.0, None, ALU.mult))

            def gate_carries():
                st = gates
                dve.wait_ge(sa, L * NA + NA)
                for d in range(2):
                    st.mark(nc.vector.tensor_scalar(wi[d][:], wi[d][:], carries[:, d:d + 1], None, ALU.mult))
                    st.mark(nc.vector.tensor_scalar(dec[d][:], dec[d][:], carries[:, d:d + 1], None, ALU.mult))
                assert st.n == NV3, st.n

            dve.wait_ge(const_in, consts_value(L, "prepare"))
            nc.vector.tensor_tensor(gain[:], gain[:], scale[:], ALU.mult).then_inc(gain_ok, 1)
            dve.wait_ge(gain_ok, L + 1)
            for j in range(NJ):
                if j == 1:
                    gate_stabilisers()
                if j == 2:
                    gate_maxima()
                outer_taps(j)
                if j == 0:
                    gate_sums()
                copy_turned(dve, nc.vector.tensor_copy, 1, turns_of(j)[0])
                normalise(j, 0)
                normalise(j, 1)
                add_turn(j, 0)
                log_sigmoid(j)
                add_turn(j, 1)
                if j == 2:
                    gate_carries()
                low_part(j, 0)
                low_part(j, 1)
                gated(j)
                copy_turned(dve, nc.vector.tensor_copy, 1, turns_of(j)[1])

        @block.gpsimd
        def _(pool):
            pool.wait_ge(const_in, consts_value(L, "prepare"))
            for j in range(NJ):
                for u, (a, z) in enumerate(PIECES):
                    pool.wait_ge(qn_ok, item(j, u) + 1)
                    if j:
                        pool.wait_ge(lo_ok, item(j - 1, u) + 1)
                    nc.gpsimd.tensor_tensor(t1[u][:], qn[u][:], cos[:, a:z], ALU.mult).then_inc(t1_ok, 1)

        @block.tensor
        def _(pe):
            def each_512(u, out, weights, src):
                m = PIECES[u][1] - PIECES[u][0]
                for c in range(0, m, 512):
                    mm = pe.matmul(out[:, c:min(c + 512, m)], weights[:], src[u][:, c:min(c + 512, m)], start=True, stop=True)
                return mm

            def sum_squares(j, u):
                n = item(j, u)
                pe.wait_ge(sq_ok, n + 1)
                if j or u:
                    pe.wait_ge(ln_ok, n)
                each_512(u, ss, blk, sq).then_inc(ss_ok, 1)

            def swap_halves(j, u):
                n = item(j, u)
                pe.wait_ge(qn_ok, n + 1)
                if j or u:
                    pe.wait_ge(rs_sin_ok, n)
                each_512(u, rx, rot, qn).then_inc(rx_ok, 1)

            def turn(i):
                if i is None:
                    return
                _, how, src = TURNS[i]
                if how == "load":
                    w = [t for t, (_, h, _) in enumerate(TURNS) if h == "load"].index(i)
                    pe.wait_ge(tv_in[w % 2], (L * (2 - w % 2) + w // 2 + 1) * DMA)
                    tile_src = tv[w % 2]
                else:
                    pe.wait_ge(smooth_ok, L * NJ + src + 1)
                    tile_src = y[src % 2]
                for g, tile, n in groups(i):
                    if g >= 2:
                        pe.wait_ge((tr_act, tr_dve)[g % 2], L * (TRA, TRD)[g % 2] + g // 2)
                    for t in range(n):
                        mm = pe.transpose(tr[g % 2][:, t, :], tile_src[:, (tile + t) * P:(tile + t + 1) * P], ident)
                    mm.then_inc(turned, 1)

            pe.wait_ge(const_in, consts_value(L, "prepare"))
            for j in range(NJ):
                sum_squares(j, 0)
                sum_squares(j, 1)
                turn(turns_of(j)[0])
                swap_halves(j, 0)
                swap_halves(j, 1)
                turn(turns_of(j)[1])
            pe.wait_ge(sv, (L + 1) * NV)
            pe.wait_ge(tr_act, (L + 1) * TRA)
            pe.wait_ge(tr_dve, (L + 1) * TRD)
            for d in range(2):
                for i, t in enumerate((a_, wi, em, kws)):
                    mm = pe.transpose(tr[d][:, i, 0:GR], t[d][:], ident[0:GR, 0:GR])
                mm.then_inc(g_turned, 1)


def attend_gqa(k, L, ident):
    nc = k.nc
    phases = k.sem("phases_stored")
    NKT = DEC_SEQ // P
    with ExitStack() as ctx:
        k_both = [sbuf(k, ctx, f"ga_kboth{g}", [P, TOK], F32R) for g in range(2)]
        k_one = [sbuf(k, ctx, f"ga_kone{g}", [P, TOK], F32R) for g in range(2)]
        v_one = [sbuf(k, ctx, f"ga_vone{g}", [P, NT, P]) for g in range(2)]
        q_hi2 = [sbuf(k, ctx, f"ga_qhi2{c}", [P, QC], F32R) for c in range(NQC)]
        q_lom = [sbuf(k, ctx, f"ga_qlom{c}", [P, QC], F32R) for c in range(NQC)]
        prob = pair(k, ctx, "ga_prob", [P, QC])
        mx = pair(k, ctx, "ga_mx", [P, 4, 4])
        nmax = pair(k, ctx, "ga_nmax", [P, 4])
        rden = pair(k, ctx, "ga_rden", [HD, QC])
        o_t = pair(k, ctx, "ga_o", [HD, QC])
        ps_s = [psum(k, ctx, f"ga_ps_s{r}", [P, QC]) for r in range(2)]
        ps_x = [psum(k, ctx, f"ga_ps_x{r}", [P, QC]) for r in range(2)]
        ps_o = [psum(k, ctx, f"ga_ps_o{r}", [P, QC]) for r in range(2)]
        ps_m = psum(k, ctx, "ga_ps_m", [P, QC])
        fill, kv_in = k.sem("ga_fill"), k.sem("ga_kv_in")
        q_in = [k.sem(f"ga_q_in{c}") for c in range(NQC)]
        stored = [k.sem(f"stored{u}") for u in range(2)]
        (scored, exped, pv_done, max_done, max_read, nmax_ok, row_done, row_ok, rden_ok, o_ok) = (
            k.sem("ga_" + s) for s in ("scored", "exped", "pv_done", "max_done", "max_read", "nmax_ok",
                                       "row_done", "row_ok", "rden_ok", "o_ok"))
        block = ctx.enter_context(nc.Block())
        SAMPLE = GQ_HEADS * NQC
        ITEMS = SAMPLE + GQ_HEADS
        TILES = SAMPLE * NKT + GQ_HEADS * NTP
        USES = [GQ_HEADS + len(range(c, GQ_HEADS, NQC)) for c in range(NQC)]
        NFILL = NQC + 3 * 2

        def item_no(i):
            return L * ITEMS + i

        def tile_no(i):
            return L * TILES + i * NKT

        def prompt_tile_no(p):
            return L * TILES + SAMPLE * NKT + p * NTP

        @block.sync
        def _(sp):
            for g in range(2):
                rows = slice(g * HD, (g + 1) * HD)
                for dst, name in ((k_both[g][0:HD, :], "gqk_hi"), (k_both[g][HD:P, :], "gqk_lo"), (k_one[g][0:HD, :], "gqk_hi")):
                    sp.dma_start(dst.bitcast(F32), k.a[name][3, rows, :]).then_inc(kv_in, DMA)
                v_cols = slice(4 * P + g * HD, 4 * P + (g + 1) * HD)
                sp.dma_start(v_one[g][:, :, 0:HD], k.a["tokmaj"][:, v_cols].rearrange("(n p) d -> p n d", p=P)).then_inc(kv_in, DMA)

            def load(h, c, a, w):
                hi, lo = (k.a[x].rearrange("c (h d) t -> (c h) d t", d=HD)[at(h)].rearrange("a d t -> (a d) t")[:, a:a + w]
                          for x in ("gqk_hi", "gqk_lo"))
                for dst, src in ((q_hi2[c][0:HD, 0:w], hi), (q_hi2[c][HD:P, 0:w], hi), (q_lom[c][0:HD, 0:w], lo)):
                    sp.dma_start(dst.bitcast(F32), src).then_inc(q_in[c], DMA)

            def store(i, u, rows, a, w):
                sp.wait_ge(o_ok, item_no(i) + 1 + 2)
                sp.dma_start(rows[:, a:a + w], o_t[u][:, 0:w]).then_inc(stored[u], DMA)

            def store_head(h, c):
                store(h * NQC + c, c % 2, k.a["gqo"][at(h)].rearrange("a d t -> (a d) t"), SEQ + c * QC, QC)

            for c in range(NQC):
                load(0, c, SEQ + c * QC, QC)
            with sp.Fori(1, GQ_HEADS) as h:
                for c in range(NQC):
                    sp.wait_ge(pv_done, tile_no(h * NQC + c - NQC + 1) + 2)
                    load(h, c, SEQ + c * QC, QC)
                    store_head(h - 1, c)
            for p in range(GQ_HEADS):
                sp.wait_ge(pv_done, (tile_no(SAMPLE + p - NQC + 1) if p < NQC else prompt_tile_no(p - NQC + 1)) + 2)
                load(p, p % NQC, 0, SEQ)
                if p < NQC:
                    store_head(GQ_HEADS - 1, p)
                else:
                    store(SAMPLE + p - NQC, p % 2, k.a["gqo"][p - NQC], 0, SEQ)
            for p in range(GQ_HEADS - NQC, GQ_HEADS):
                store(SAMPLE + p, p % 2, k.a["gqo"][p], 0, SEQ)
            for u in range(2):
                sp.wait_ge(stored[u], stored_value(L, "gqa", u, ITEMS // 2))
            sp.sem_inc(phases, 1)

        @block.tensor
        def _(pe):
            pe.wait_ge(fill, (L + 1) * NFILL)
            pe.wait_ge(kv_in, (L + 1) * 8 * DMA)

            def max_product(g, c, q, key0, w, m, r):
                pe.wait_ge(max_read, m + 1)
                pe.matmul(ps_x[r][:, 0:w], q_hi2[c][:, q * P:(q + 1) * P], k_both[g][:, key0:key0 + w],
                          start=True, stop=True).then_inc(max_done, 1)

            def max_rows(u, nq, i):
                pe.wait_ge(nmax_ok, item_no(i) + 1)
                for q in range(nq):
                    mm = pe.matmul(ps_m[HD:HD + 1, q * P:(q + 1) * P], nmax[u][:, q:q + 1], ident, start=True, stop=True)
                mm.then_inc(row_done, 1)

            def scores(g, c, t, kt, w, r, i, first):
                pe.wait_ge(exped, t + 1)
                tile = slice(kt * P, (kt + 1) * P)
                pe.matmul(ps_s[r][:, 0:w], k_both[g][:, tile], q_hi2[c][:, 0:w], start=True, stop=False)
                if first:
                    pe.wait_ge(row_ok, item_no(i) + 1)
                pe.matmul(ps_s[r][:, 0:w], k_one[g][:, tile], q_lom[c][:, 0:w], start=False, stop=True).then_inc(scored, 1)

            def weigh(g, u, t, kt, w, r, first, last):
                pe.wait_ge(exped, t + 1 + 2)
                pe.matmul(ps_o[u][:, 0:w], v_one[g][:, kt, :], prob[r][:, 0:w], start=first, stop=last).then_inc(pv_done, 1)

            def item(g, c, i, nkt, kt0, w, t0, next_max, next_rows):
                u = c % 2
                for kt in range(nkt):
                    scores(g, c, t0 + kt, kt0 + kt, w, kt % 2, i, kt == 0)
                    next_max(kt)
                    if kt == 1:
                        pe.wait_ge(o_ok, item_no(i) + 1)
                    if kt:
                        weigh(g, u, t0 + kt - 1, kt0 + kt - 1, w, (kt - 1) % 2, kt == 1, False)
                next_rows()
                weigh(g, u, t0 + nkt - 1, kt0 + nkt - 1, w, (nkt - 1) % 2, False, True)

            def nothing(*_):
                pass

            def sample_max(g, c, i):
                def one(kt):
                    if kt == 0:
                        pe.wait_ge(q_in[c], (L * USES[c] * 3 + loads_before(i, c) + 3) * DMA)
                    max_product(g, c, kt // 4, SEQ + (kt % 4) * QC, QC, tile_no(i) + kt, kt % 2)
                return one

            def loads_before(i, c):
                return (i - c) * 3 // NQC if isinstance(i, int) else (i - c) // NQC * 3

            for g in range(KV_HEADS):
                base = g * GQ_PER_KV * NQC
                first = sample_max(g, 0, base)
                for kt in range(NKT):
                    first(kt)
                max_rows(0, 4, base)

                def head(hh, last):
                    i0 = base + hh * NQC
                    for c in range(NQC):
                        i, cn = i0 + c, (c + 1) % NQC
                        end = last and c == NQC - 1
                        heads_before = g * GQ_PER_KV + hh + (c == NQC - 1)

                        def one(kt, i=i, cn=cn, heads_before=heads_before):
                            if kt == 0:
                                pe.wait_ge(q_in[cn], (L * USES[cn] + heads_before + 1) * 3 * DMA)
                            max_product(g, cn, kt // 4, SEQ + (kt % 4) * QC, QC, tile_no(i + 1) + kt, kt % 2)

                        item(g, c, i, NKT, NTP, QC, tile_no(i), nothing if end else one,
                             nothing if end else (lambda i=i, cn=cn: max_rows(cn % 2, 4, i + 1)))

                with pe.Fori(0, GQ_PER_KV - 1) as hh:
                    head(hh, False)
                head(GQ_PER_KV - 1, True)
            for p in range(GQ_HEADS):
                g, c, t0 = p // GQ_PER_KV, p % NQC, prompt_tile_no(p)
                pe.wait_ge(q_in[c], (L * USES[c] + GQ_HEADS + p // NQC + 1) * 3 * DMA)
                for q in range(NTP):
                    max_product(g, c, q, 0, SEQ, t0 + q, q % 2)
                max_rows(c % 2, NTP, SAMPLE + p)
                item(g, c, SAMPLE + p, NTP, 0, SEQ, t0, nothing, nothing)

        @block.scalar
        def _(act):
            def exp_tile(t, w, r):
                act.wait_ge(scored, t + 1)
                act.wait_ge(pv_done, t + 1)
                nc.scalar.activation(prob[r][:, 0:w], ps_s[r][:, 0:w], ACT.Exp).then_inc(exped, 1)

            def row(c, i, w):
                act.wait_ge(row_done, item_no(i) + 1)
                nc.scalar.copy(q_lom[c][HD:HD + 1, 0:w], ps_m[HD:HD + 1, 0:w]).then_inc(row_ok, 1)

            for g in range(KV_HEADS):
                base = g * GQ_PER_KV * NQC
                row(0, base, QC)

                def head(hh, last):
                    for c in range(NQC):
                        i = base + hh * NQC + c
                        for kt in range(NKT):
                            exp_tile(tile_no(i) + kt, QC, kt % 2)
                        if not (last and c == NQC - 1):
                            row((c + 1) % NQC, i + 1, QC)

                with act.Fori(0, GQ_PER_KV - 1) as hh:
                    head(hh, False)
                head(GQ_PER_KV - 1, True)
            for p in range(GQ_HEADS):
                row(p % NQC, SAMPLE + p, SEQ)
                for kt in range(NTP):
                    exp_tile(prompt_tile_no(p) + kt, SEQ, kt % 2)

        @block.vector
        def _(dve):
            def maxima(u, i, t0, nq, nk, w):
                for q in range(nq):
                    for c in range(nk):
                        dve.wait_ge(max_done, t0 + q * nk + c + 1)
                        nc.vector.tensor_reduce(mx[u][:, q, c:c + 1], ps_x[(q * nk + c) % 2][:, 0:w], AX.X,
                                                ALU.max).then_inc(max_read, 1)
                dve.wait_ge(max_read, t0 + nq * nk + 2)
                nc.vector.tensor_reduce(nmax[u][:, 0:nq], mx[u][:, 0:nq, 0:nk], AX.X, ALU.max,
                                        negate=True).then_inc(nmax_ok, 1)

            def output(u, i, t_end, w, stored_before):
                dve.wait_ge(pv_done, t_end + 2)
                dve.wait_ge(o_ok, item_no(i) + 1)
                nc.vector.reciprocal(rden[u][:, 0:w], ps_o[u][HD:P, 0:w]).then_inc(rden_ok, 1)
                dve.wait_ge(rden_ok, item_no(i) + 1)
                dve.wait_ge(stored[u], stored_value(L, "gqa", u, stored_before))
                nc.vector.tensor_tensor(o_t[u][:, 0:w], ps_o[u][0:HD, 0:w], rden[u][:, 0:w], ALU.mult).then_inc(o_ok, 1)

            for c in range(NQC):
                nc.vector.memset(q_lom[c][HD:P, :].bitcast(F32), 0.0).then_inc(fill, 1)
            for g in range(KV_HEADS):
                nc.vector.memset(k_one[g][HD:P, :].bitcast(F32), 0.0).then_inc(fill, 1)
                nc.vector.memset(v_one[g][:, :, HD:P], 1.0).then_inc(fill, 1)
            for g in range(KV_HEADS):
                dve.wait_ge(fill, L * NFILL + NFILL - 2 + g)
                nc.vector.memset(k_one[g][HD:HD + 1, :].bitcast(F32), 1.0).then_inc(fill, 1)
            for g in range(KV_HEADS):
                base = g * GQ_PER_KV * NQC
                maxima(0, base, tile_no(base), 4, 4, QC)

                def head(hh, last):
                    for c in range(NQC):
                        i = base + hh * NQC + c
                        if not (last and c == NQC - 1):
                            maxima((c + 1) % 2, i + 1, tile_no(i + 1), 4, 4, QC)
                        output(c % 2, i, tile_no(i + 1), QC, (g * GQ_PER_KV + hh) * 2 + c // 2)

                with dve.Fori(0, GQ_PER_KV - 1) as hh:
                    head(hh, False)
                head(GQ_PER_KV - 1, True)
            for p in range(GQ_HEADS):
                maxima(p % 2, SAMPLE + p, prompt_tile_no(p), NTP, 1, SEQ)
                output(p % 2, SAMPLE + p, prompt_tile_no(p + 1), SEQ, SAMPLE // 2 + p // 2)


def mlstm(k, L, gate_cols, decay):
    nc = k.nc
    phases = k.sem("phases_stored")
    NB = NT // 2
    with ExitStack() as ctx:
        def four(name, shape):
            return [[sbuf(k, ctx, f"ml_{name}{u}{d}", shape) for d in range(2)] for u in range(2)]

        q, kt_, kk, v1, mb = (four("q", [HD, MH, P]), four("kt", [HD, MH, P]), four("kk", [P, MH, HD]),
                              four("v1", [P, MH, HD + 1]), four("mb", [P, MH, P]))
        h_out = four("h", [P, MH, HD])
        arg, w, at_, kw, nd, den = (pair(k, ctx, "ml_" + x, s) for x, s in (
            ("arg", [P, MH, P]), ("w", [P, MH, P]), ("at", [P, MH, P]), ("kw", [P, MH, HD]),
            ("nd", [P, MH, HD + 1]), ("den", [P, MH])))
        state = pair(k, ctx, "ml_state", [HD, MH, HD + 1])
        causal = sbuf(k, ctx, "ml_causal", [P, 2, P])
        ps_s = [psum(k, ctx, f"ml_ps_s{d}", [P, MH, P]) for d in range(2)]
        ps_i = [psum(k, ctx, f"ml_ps_i{d}", [P, 512]) for d in range(2)]
        ps_n = [psum(k, ctx, f"ml_ps_n{d}", [P, 512]) for d in range(2)]
        ps_c = [psum(k, ctx, f"ml_ps_c{d}", [HD, 512]) for d in range(2)]
        loaded = [[k.sem(f"ml_loaded{u}{d}") for d in range(2)] for u in range(2)]
        stored = [[k.sem(f"ml_stored{u}{d}") for d in range(2)] for u in range(2)]
        const_in = k.sem("consts_in")
        fill, arg_ok, w_ok, s_ok, at_ok, kw_ok, mm_ok, chain, h_ok, state_ok = (
            k.sem("ml_" + s) for s in ("fill", "arg_ok", "w_ok", "s_ok", "at_ok", "kw_ok", "mm_ok", "chain",
                                       "h_ok", "state_ok"))
        block = ctx.enter_context(nc.Block())
        W = HD + 1

        def chunk(b, u, d):
            return b * 2 + u if d == 0 else b * -2 + (NT - 1 - u)

        def number(b, u, d):
            return (L * NB + b) * 4 + u * 2 + d

        def gate(which, d, c):
            t = gate_cols[:, d * 4 + which, :].rearrange("p (h c) -> p h c", c=NT)
            return t[:, :, at(c)].rearrange("p h x -> p (h x)")

        def decay_of(d, c):
            t = decay[:, d * GR:(d + 1) * GR].rearrange("p (h c) -> p h c", c=NT)
            return t[:, :, at(c)].rearrange("p h x -> p (h x)")

        def heads(ps):
            return ps[:, 0:MH * W].rearrange("p (h e) -> p h e", e=W)

        @block.sync
        def _(sp):
            sp.dma_start(causal[:], k.a["causal"]).then_inc(const_in, DMA)

            def loads(b):
                for u in range(2):
                    for d in range(2):
                        c = chunk(b, u, d)
                        sp.wait_ge(mm_ok, number(b, u, d) + 1)
                        tok = at(c * P, P)
                        qk = k.a["mqk"].rearrange("c (h d) t -> d (c h) t", d=HD)
                        s = loaded[u][d]
                        sp.dma_start(q[u][d][:], qk[:, 0:MH, tok]).then_inc(s, DMA)
                        sp.dma_start(kt_[u][d][:], qk[:, MH:2 * MH, tok]).then_inc(s, DMA)
                        sp.dma_start(kk[u][d][:], k.a["tokmaj"][tok, 0:MH * HD].rearrange("t (h e) -> t h e", e=HD)).then_inc(s, DMA)
                        sp.dma_start(v1[u][d][:, :, 0:HD],
                                     k.a["tokmaj"][tok, MH * HD:2 * MH * HD].rearrange("t (h e) -> t h e", e=HD)).then_inc(s, DMA)
                        M = k.a["gate_M"][d].rearrange("(h c) l -> c h l", c=NT)[at(c)].rearrange("c h l -> (c h) l")
                        sp.dma_start(mb[u][d][:], M.partition_broadcast(P)).then_inc(s, DMA)

            def stores(b):
                for u in range(2):
                    for d in range(2):
                        sp.wait_ge(h_ok, number(b, u, d) + 1)
                        sp.dma_start(rows_of(k.a["mh"][d], chunk(b, u, d) * P, P, 0, MH * HD),
                                     h_out[u][d][:].rearrange("p h e -> p (h e)")).then_inc(stored[u][d], DMA)

            loads(0)
            with sp.Fori(1, NB) as b:
                loads(b)
                stores(b - 1)
            stores(NB - 1)
            for u in range(2):
                for d in range(2):
                    sp.wait_ge(stored[u][d], (L + 1) * NB * DMA + DMA)
            sp.sem_inc(phases, 1)

        @block.gpsimd
        def _(pool):
            with pool.Fori(0, NB) as b:
                pool.wait_ge(const_in, consts_value(L, "mlstm"))
                for u in range(2):
                    for d in range(2):
                        m = number(b, u, d)
                        pool.wait_ge(loaded[u][d], (L * NB + b + 1) * 5 * DMA)
                        pool.wait_ge(w_ok, m + 1)
                        mask = causal[:, d, :].unsqueeze(1).to_broadcast([P, MH, P])
                        nc.gpsimd.tensor_tensor(arg[d][:], mask, mb[u][d][:], ALU.subtract).then_inc(arg_ok, 1)
                        pool.wait_ge(mm_ok, m + 1 + 2)
                        nc.gpsimd.tensor_tensor(kw[d][:], kk[u][d][:], bc_free(gate(3, d, chunk(b, u, d)), HD),
                                                ALU.mult).then_inc(kw_ok, 1)

        @block.scalar
        def _(act):
            with act.Fori(0, NB) as b:
                for u in range(2):
                    for d in range(2):
                        m = number(b, u, d)
                        act.wait_ge(arg_ok, m + 1)
                        act.wait_ge(at_ok, m + 1)
                        a = gate_cols[:, d * 4, :]
                        for h in range(MH):
                            ins = nc.scalar.activation(w[d][:, h, :], arg[d][:, h, :], ACT.Exp,
                                                       bias=a[:, at(chunk(b, u, d) + h * NT)])
                        ins.then_inc(w_ok, 1)

        @block.vector
        def _(dve):
            for d in range(2):
                nc.vector.memset(state[d][:], 0.0).then_inc(fill, 1)
                for u in range(2):
                    nc.vector.memset(v1[u][d][:, :, HD:W], 1.0).then_inc(fill, 1)
            with dve.Fori(0, NB) as b:
                dve.wait_ge(fill, (L + 1) * 6)
                for u in range(2):
                    for d in range(2):
                        m = number(b, u, d)
                        dve.wait_ge(w_ok, m + 1 + 2)
                        dve.wait_ge(s_ok, m + 1)
                        dve.wait_ge(mm_ok, m + 1 + 2)
                        nc.vector.tensor_tensor(at_[d][:], w[d][:], ps_s[d][:], ALU.mult).then_inc(at_ok, 1)
                    for d in range(2):
                        m, c = number(b, u, d), chunk(b, u, d)
                        st = Steps(dve, chain, m * 6)
                        dve.wait_ge(mm_ok, m + 1 + 4)
                        st.mark(nc.vector.tensor_tensor(nd[d][:], heads(ps_i[d]), bc_free(gate(1, d, c), W), ALU.mult))
                        st.mark(nc.vector.tensor_tensor(state[d][:], state[d][:],
                                                        bc_free(decay_of(d, c), W), ALU.mult))
                        st.join()
                        st.mark(nc.vector.tensor_tensor(nd[d][:], nd[d][:], heads(ps_n[d]), ALU.add))
                        st.join()
                        dcol = nd[d][:, :, HD:W].rearrange("p h x -> p (h x)")
                        st.mark(nc.vector.scalar_tensor_tensor(out=den[d][:], in0=dcol, scalar=-1.0, in1=dcol,
                                                               op0=ALU.mult, op1=ALU.max))
                        st.join()
                        st.mark(nc.vector.tensor_tensor(den[d][:], den[d][:], gate(2, d, c), ALU.max))
                        st.join()
                        st.mark(nc.vector.reciprocal(den[d][:], den[d][:]))
                        nc.vector.tensor_tensor(state[d][:], state[d][:], heads(ps_c[d]), ALU.add).then_inc(state_ok, 1)
                        st.join()
                        dve.wait_ge(stored[u][d], (L * NB + b) * DMA + DMA)
                        nc.vector.tensor_tensor(h_out[u][d][:], nd[d][:, :, 0:HD], bc_free(den[d][:], HD),
                                                ALU.mult).then_inc(h_ok, 1)

        @block.tensor
        def _(pe):
            with pe.Fori(0, NB) as b:
                pe.wait_ge(fill, (L + 1) * 6)
                for u in range(2):
                    for d in range(2):
                        m = number(b, u, d)
                        pe.wait_ge(loaded[u][d], (L * NB + b + 1) * 5 * DMA)
                        pe.wait_ge(at_ok, m + 1)
                        for h in range(MH):
                            mm = pe.matmul(ps_s[d][:, h, :], kt_[u][d][:, h, :], q[u][d][:, h, :], start=True, stop=True)
                        mm.then_inc(s_ok, 1)
                    for d in range(2):
                        m = number(b, u, d)
                        pe.wait_ge(state_ok, m + 1)
                        for h in range(MH):
                            pe.matmul(ps_i[d][:, h * W:(h + 1) * W], q[u][d][:, h, :], state[d][:, h, :], start=True, stop=True)
                        pe.wait_ge(kw_ok, m + 1)
                        for h in range(MH):
                            pe.matmul(ps_c[d][:, h * W:(h + 1) * W], kw[d][:, h, :], v1[u][d][:, h, :], start=True, stop=True)
                        pe.wait_ge(at_ok, m + 1 + 2)
                        for h in range(MH):
                            mm = pe.matmul(ps_n[d][:, h * W:(h + 1) * W], at_[d][:, h, :], v1[u][d][:, h, :], start=True, stop=True)
                        mm.then_inc(mm_ok, 1)


def order_classes(k, L):
    nc = k.nc
    phases = k.sem("phases_stored")
    with ExitStack() as ctx:
        x = [sbuf(k, ctx, f"oc_x{g}", [P, TOK]) for g in range(NG)]
        y = [sbuf(k, ctx, f"oc_y{g}", [P, TOK]) for g in range(NG)]
        scale = sbuf(k, ctx, "oc_scale", [P, 4])
        const_in = k.sem("consts_in")
        x_in = [k.sem(f"oc_x_in{g}") for g in range(NG)]
        stored = [k.sem(f"stored{g}") for g in range(NG)]
        ok = [k.sem(f"oc_ok{g}") for g in range(NG)]
        block = ctx.enter_context(nc.Block())

        @block.sync
        def _(sp):
            sp.dma_start(scale[:], k.a["oc_scale"]).then_inc(const_in, DMA)
            with sp.Fori(0, 3) as kind:
                n = L * 3 + kind
                for g in range(NG):
                    sp.wait_ge(ok[g], n * 2 + 1)
                    sp.dma_start(x[g][:], k.a["proj"][at(kind * NG + (CT_DQ + g))].rearrange("a p t -> p (a t)")).then_inc(x_in[g], DMA)
                for g in range(NG):
                    sp.wait_ge(ok[g], n * 2 + 2 + 1)
                    dst = k.a["dil_in"][at(kind * NG + g)].rearrange("a p t -> p (a t)")[:, SIDE:SIDE + TOK]
                    sp.dma_start(dst, y[g][:]).then_inc(stored[g], DMA)
            for g in range(NG):
                sp.wait_ge(stored[g], stored_value(L, "order", g, 3))
            sp.sem_inc(phases, 1)

        @block.vector
        def _(dve):
            with dve.Fori(0, 3) as kind:
                dve.wait_ge(const_in, consts_value(L, "order"))
                n = L * 3 + kind
                for g, (_, dil) in enumerate(DIL):
                    dve.wait_ge(x_in[g], (n + 1) * DMA)
                    dve.wait_ge(stored[g], stored_value(L, "order", g, kind))
                    for s0, s1 in ((0, SEQ), (SEQ, TOK)):
                        nc.vector.tensor_scalar(y[g][:, s0:s1].rearrange("p (r j) -> p j r", r=dil),
                                                x[g][:, s0:s1].rearrange("p (j r) -> p j r", r=dil),
                                                scale[:, at(kind)], None, ALU.mult).then_inc(ok[g], 1)


KW = P + 2 * SIDE


def attend_dilated(k, L, ident):
    nc = k.nc
    phases = k.sem("phases_stored")
    NBLK = NG * NT
    with ExitStack() as ctx:
        q, kw, v, dist = (pair(k, ctx, "dl_" + x, s) for x, s in (
            ("q", [HD, 2, P]), ("k", [HD, 2, KW]), ("v", [P, KW]), ("dist", [P, KW + 2])))
        v_t, sb_, pr, pt = (pair(k, ctx, "dl_" + x, s) for x, s in (
            ("v_t", [P, 2, P]), ("s", [P, 2, KW]), ("p", [P, 2, KW]), ("pt", [P, 4, P])))
        nmax, den, lnd, out = (pair(k, ctx, "dl_" + x, s) for x, s in (
            ("nmax", [P, 2]), ("den", [P, 4]), ("lnd", [P, 2]), ("out", [P, 2, HD + 1])))
        ps_s = [psum(k, ctx, f"dl_ps_s{u}", [P, 2, KW]) for u in range(2)]
        ps_v = [psum(k, ctx, f"dl_ps_v{u}", [P, 4, P]) for u in range(2)]
        ps_t = [psum(k, ctx, f"dl_ps_t{u}", [P, 4, P]) for u in range(2)]
        ps_o = [psum(k, ctx, f"dl_ps_o{u}", [P, 512]) for u in range(2)]
        loaded = [k.sem(f"dl_loaded{u}") for u in range(2)]
        stored = [k.sem(f"stored{u}") for u in range(2)]
        s_ok, vt_ok, vc_ok, bias_ok, nmax_ok, p_ok, turned, pt_ok, pv_ok, ln_ok, lse_ok, chain, out_ok = (
            k.sem("dl_" + s) for s in ("s_ok", "vt_ok", "vc_ok", "bias_ok", "nmax_ok", "p_ok", "turned", "pt_ok",
                                       "pv_ok", "ln_ok", "lse_ok", "chain", "out_ok"))
        block = ctx.enter_context(nc.Block())

        def number(b, c):
            return L * NBLK + (b * 2 + c)

        def loads_before(b, c):
            return L * (NBLK // 2) + (b + c // 2)

        def exists(b, c):
            return not isinstance(b, int) or 0 <= c < NBLK

        def slots(engine, slot):
            for c in range(-2, 0):
                slot(0, c)
            with engine.Fori(0, NBLK // 2 - 1) as b:
                for v_ in range(2):
                    slot(b, v_)
            for c in range(NBLK - 2, NBLK):
                slot(0, c)

        @block.sync
        def _(sp):
            half = k.a["dil_in"].rearrange("c (h d) t -> c d h t", h=2)

            def loads(g, b, c, m):
                u, a, s = c % 2, (b * 2 + c) * P, loaded[c % 2]
                if m is not None:
                    past = m + 1
                    sp.wait_ge(bias_ok, past)
                    sp.wait_ge(vt_ok, past)
                sp.dma_start(q[u][:], half[g][:, :, at(a + SIDE, P)]).then_inc(s, DMA)
                sp.dma_start(kw[u][:], half[NG + g][:, :, at(a, KW)]).then_inc(s, DMA)
                sp.dma_start(dist[u][:], k.a["dil_dist"][g][at(b * 2 + c)].rearrange("a p t -> (a p) t")).then_inc(s, DMA)
                sp.dma_start(v[u][:], k.a["dil_in"][2 * NG + g][:, at(a, KW)]).then_inc(s, DMA)

            def store(g, b, c, m):
                sp.wait_ge(out_ok, m + 3)
                sp.dma_start(rows_of(k.a["dil_out"][g], (b * 2 + c) * P, P, 0, 2 * (HD + 1)),
                             out[c % 2][:].rearrange("p h e -> p (h e)")).then_inc(stored[c % 2], DMA)

            for c in range(4):
                loads(0, 0, c, number(0, c) if c >= 2 else None)
            for g in range(NG):
                with sp.Fori(0, (NT - 4) // 2) as b:
                    for c in range(2):
                        loads(g, b, c + 4, number(b, g * NT + c + 4))
                        store(g, b, c, number(b, g * NT + c))
                for c in range(NT - 4, NT):
                    if g + 1 < NG:
                        loads(g + 1, 0, c + 4 - NT, number(0, g * NT + c + 4))
                    store(g, 0, c, number(0, g * NT + c))
            for u in range(2):
                sp.wait_ge(stored[u], stored_value(L, "dilated", u, NBLK // 2))
            sp.sem_inc(phases, 1)

        @block.tensor
        def _(pe):
            def score(b, c):
                u, m = c % 2, number(b, c)
                pe.wait_ge(loaded[u], (loads_before(b, c) + 1) * 4 * DMA)
                pe.wait_ge(bias_ok, m + 1)
                for h in range(2):
                    mm = pe.matmul(ps_s[u][:, h, :], q[u][:, h, :], kw[u][:, h, :], start=True, stop=True)
                mm.then_inc(s_ok, 1)

            def turn_v(b, c):
                u, m = c % 2, number(b, c)
                pe.wait_ge(vc_ok, m + 1)
                for i in range(2):
                    mm = pe.transpose(ps_v[u][:, i, :], v[u][:, i * P:(i + 1) * P], ident)
                mm.then_inc(vt_ok, 1)

            def turn(b, c):
                u, m = c % 2, number(b, c)
                pe.wait_ge(p_ok, m + 3)
                pe.wait_ge(pt_ok, m + 1)
                for h in range(2):
                    for i in range(2):
                        mm = pe.transpose(ps_t[u][:, h * 2 + i, :], pr[u][:, h, i * P:(i + 1) * P], ident)
                mm.then_inc(turned, 1)

            def weigh(b, c):
                u, m = c % 2, number(b, c)
                pe.wait_ge(pt_ok, m + 3)
                pe.wait_ge(vc_ok, m + 3)
                pe.wait_ge(out_ok, m + 1)
                for h in range(2):
                    for i in range(2):
                        mm = pe.matmul(ps_o[u][:, h * HD:(h + 1) * HD], pt[u][:, h * 2 + i, :],
                                       v_t[u][:, i, h * HD:(h + 1) * HD], start=(i == 0), stop=(i == 1))
                mm.then_inc(pv_ok, 1)

            def slot(b, c):
                if exists(b, c + 2):
                    score(b, c + 2)
                if exists(b, c + 1):
                    turn(b, c + 1)
                if exists(b, c):
                    weigh(b, c)
                if exists(b, c + 2):
                    turn_v(b, c + 2)

            slots(pe, slot)

        @block.scalar
        def _(act):
            def exp(b, c):
                u, m = c % 2, number(b, c)
                act.wait_ge(nmax_ok, m + 1)
                act.wait_ge(turned, m + 1)
                act.wait_ge(lse_ok, m + 1)
                for h in range(2):
                    ins = nc.scalar.activation(pr[u][:, h, :], sb_[u][:, h, :], ACT.Exp,
                                               bias=nmax[u][:, h:h + 1], accum_out=den[u][:, h:h + 1])
                ins.then_inc(p_ok, 1)

            def copy_v(b, c):
                u, m = c % 2, number(b, c)
                act.wait_ge(vt_ok, m + 3)
                act.wait_ge(pv_ok, m + 1)
                nc.scalar.copy(v_t[u][:], ps_v[u][:, 0:2, :]).then_inc(vc_ok, 1)

            def turn(b, c):
                u, m = c % 2, number(b, c)
                act.wait_ge(p_ok, m + 3)
                act.wait_ge(lse_ok, m + 1)
                nc.scalar.activation(lnd[u][:], den[u][:, 0:2], ACT.Ln).then_inc(ln_ok, 1)
                act.wait_ge(turned, m + 3)
                act.wait_ge(pv_ok, m + 1)
                nc.scalar.copy(pt[u][:], ps_t[u][:]).then_inc(pt_ok, 1)

            def slot(b, c):
                if exists(b, c + 1):
                    turn(b, c + 1)
                if exists(b, c + 2):
                    exp(b, c + 2)
                    copy_v(b, c + 2)

            slots(act, slot)

        @block.vector
        def _(dve):
            def bias(b, c):
                u, m = c % 2, number(b, c)
                dve.wait_ge(s_ok, m + 1)
                dve.wait_ge(p_ok, m + 1)
                for h in range(2):
                    ins = nc.vector.scalar_tensor_tensor(
                        out=sb_[u][:, h, :], in0=dist[u][:, 0:KW], scalar=dist[u][:, KW + h:KW + h + 1],
                        in1=ps_s[u][:, h, :], op0=ALU.mult, op1=ALU.add)
                ins.then_inc(bias_ok, 1)
                dve.wait_ge(bias_ok, m + 3)
                dve.wait_ge(lse_ok, m + 1)
                nc.vector.tensor_reduce(nmax[u][:], sb_[u][:], AX.X, ALU.max, negate=True).then_inc(nmax_ok, 1)

            def denominators(b, c):
                u, m = c % 2, number(b, c)
                dve.wait_ge(ln_ok, m + 1)
                dve.wait_ge(out_ok, m + 1)
                nc.vector.reciprocal(den[u][:, 2:4], den[u][:, 0:2]).then_inc(chain, 1)
                dve.wait_ge(stored[u], stored_value(L, "dilated", u, b + c // 2))
                lse = out[u][:, :, HD:HD + 1].rearrange("p h x -> p (h x)")
                nc.vector.tensor_tensor(lse, lnd[u][:], nmax[u][:], ALU.subtract).then_inc(lse_ok, 1)

            def output(b, c):
                u, m = c % 2, number(b, c)
                dve.wait_ge(pv_ok, m + 3)
                dve.wait_ge(lse_ok, m + 3)
                nc.vector.tensor_tensor(out[u][:, :, 0:HD], ps_o[u][:, 0:2 * HD].rearrange("p (h e) -> p h e", e=HD),
                                        bc_free(den[u][:, 2:4], HD), ALU.mult).then_inc(out_ok, 1)

            def slot(b, c):
                if exists(b, c + 2):
                    bias(b, c + 2)
                if exists(b, c + 1):
                    denominators(b, c + 1)
                if exists(b, c):
                    output(b, c)

            slots(dve, slot)


NZ = 8


def finish(k, L, ident, cols):
    nc = k.nc
    phases = k.sem("phases_stored")
    with ExitStack() as ctx:
        w_hi = sbuf(k, ctx, "fi_whi", [P, KT, D_MODEL], F32R)
        w_lo = sbuf(k, ctx, "fi_wlo", [P, KT, D_MODEL], F32R)
        w_raw = pair(k, ctx, "fi_wraw", [P, D_MODEL])
        gpost = sbuf(k, ctx, "fi_gpost", [P, D_MODEL])
        mgain = sbuf(k, ctx, "fi_mgain", [P, 2])
        x = pair(k, ctx, "fi_x", [P, D_MODEL])
        z = pair(k, ctx, "fi_z", [P, NZ + 2, P])
        e = sbuf(k, ctx, "fi_e", [P, NZ + 2, P])
        gq = pair(k, ctx, "fi_gq", [P, 3, P])
        hf = pair(k, ctx, "fi_hf", [P, MH, HD])
        hb = pair(k, ctx, "fi_hb", [P, MH, HD])
        dl = pair(k, ctx, "fi_dl", [P, NG, 2, HD + 1])
        od = sbuf(k, ctx, "fi_od", [P, NG, 2, HD])
        eo = sbuf(k, ctx, "fi_eo", [P, MH, HD])
        hsq = sbuf(k, ctx, "fi_hsq", [P, MH, HD])
        hst = sbuf(k, ctx, "fi_hst", [P, 3, MH])
        al = sbuf(k, ctx, "fi_al", [P, 2, 2, NG])
        am = sbuf(k, ctx, "fi_am", [P, 2, 2])
        m_hi = pair(k, ctx, "fi_mhi", [P, KT, P], F32R)
        m_lo = pair(k, ctx, "fi_mlo", [P, KT, P], F32R)
        mix = sbuf(k, ctx, "fi_mix", [P, KT, P])
        y = sbuf(k, ctx, "fi_y", [P, D_MODEL])
        xo = pair(k, ctx, "fi_xo", [P, D_MODEL])
        yst = sbuf(k, ctx, "fi_yst", [P, 4])
        ps_y = [psum(k, ctx, f"fi_ps_y{u}", [P, D_MODEL]) for u in range(2)]
        ps_o = psum(k, ctx, "fi_ps_o", [P, 512])
        ps_h = psum(k, ctx, "fi_ps_h", [P, 4, P])
        ps_d = psum(k, ctx, "fi_ps_d", [P, 4, P])
        const_in = k.sem("consts_in")
        wr_in = [k.sem(f"fi_wr_in{u}") for u in range(2)]
        loaded = [k.sem(f"fi_loaded{u}") for u in range(2)]
        x_in = [k.sem(f"fi_x_in{u}") for u in range(2)]
        stored = [k.sem(f"stored{u}") for u in range(2)]
        (whi_ok, wlo_ok, sig_chain, ln_ok, logsig_ok, sig_ok, z_ok, o_ok, hs_ok, hss_ok, hrs_a, hrs_ok, lse_ok, ea_ok,
         hn_ok, gqz_ok, turned, mix_ok, hi_ok, lo_ok, y_done, ys_ok, yr_ok, yn_ok, x_ok, chain) = (
            k.sem("fi_" + s) for s in (
                "whi_ok", "wlo_ok", "sig_chain", "ln_ok", "logsig_ok", "sig_ok", "z_ok", "o_ok", "hs_ok", "hss_ok",
                "hrs_a", "hrs_ok", "lse_ok", "ea_ok", "hn_ok", "gqz_ok", "turned", "mix_ok", "hi_ok", "lo_ok",
                "y_done", "ys_ok", "yr_ok", "yn_ok", "x_ok", "chain"))
        block = ctx.enter_context(nc.Block())
        NB = NT // 2
        NLOAD = 3 + 1 + 1 + 2 + NG
        NCHAIN = 9

        def number(b, c):
            return L * NT + (b * 2 + c)

        def uses(b, c):
            return L * NB + (b + c // 2)

        def exists(b, c):
            return not isinstance(b, int) or 0 <= c < NT

        def slots(engine, slot):
            for c in range(-2, 1):
                slot(0, c)
            with engine.Fori(0, NB - 2) as b:
                for v in range(2):
                    slot(b, 1 + v)
            for c in range(NT - 3, NT + 1):
                slot(0, c)

        @block.sync
        def _(sp):
            def loads(b, c, prompt):
                u, n = c % 2, b * 2 + c
                if not prompt:
                    sp.wait_ge(mix_ok, number(b, c) - 1)
                s, tok = loaded[u], at(n * P, P)
                for i, ct, m in ((0, CT_MZ, 2), (2, CT_GZ, 3), (5, CT_DZ, 3), (NZ, CT_MO, 2)):
                    sp.dma_start(z[u][:, i:i + m, :], k.a["proj"][ct:ct + m, :, tok].rearrange("c p t -> p c t")).then_inc(s, DMA)
                for t, d in ((hf, 0), (hb, 1)):
                    sp.dma_start(t[u][:].rearrange("p h e -> p (h e)"), rows_of(k.a["mh"][d], n * P, P, 0, MH * HD)).then_inc(s, DMA)
                sp.dma_start(gq[u][:], k.a["gqo"].rearrange("(c h) d t -> (h d) c t", h=2)[:, :, tok]).then_inc(s, DMA)
                for g, (_, dil) in enumerate(DIL):
                    s0, s1 = (0, SEQ) if prompt else (SEQ, TOK)
                    seq = k.a["dil_out"][g][s0:s1, :].rearrange("(r j) e -> j r e", r=dil)
                    j0 = (n * (P // dil)) if prompt else (n - NTP) * (P // dil)
                    sp.dma_start(dl[u][:, g].rearrange("p h e -> p (h e)"), seq[at(j0, P // dil)]).then_inc(s, DMA)

            def load_x(b, c):
                sp.dma_start(x[c % 2][:], rows_of(k.a["x"], (b * 2 + c) * P, P, 0, D_MODEL)).then_inc(x_in[c % 2], DMA)

            def slot(b, c):
                if exists(b, c - 1):
                    sp.wait_ge(x_ok, number(b, c - 1) + 2)
                    sp.dma_start(rows_of(k.a["x"], (b * 2 + c - 1) * P, P, 0, D_MODEL), xo[(c - 1) % 2][:]
                                 ).then_inc(stored[(c - 1) % 2], DMA)
                    if exists(b, c + 1):
                        load_x(b, c + 1)
                if exists(b, c + 3) and not (isinstance(b, int) and c + 3 < NTP):
                    loads(b, c + 3, False)

            loads(0, 0, True)
            for t in range(2):
                sp.dma_start(w_raw[t][:], k.a["w_out"][at(L), t].rearrange("a p c -> p (a c)")).then_inc(wr_in[t], DMA)
            loads(0, 1, True)
            for t in range(2, KT):
                sp.wait_ge(wlo_ok, L * KT + t - 1)
                sp.dma_start(w_raw[t % 2][:], k.a["w_out"][at(L), t].rearrange("a p c -> p (a c)")).then_inc(wr_in[t % 2], DMA)
            sp.dma_start(gpost[:], k.a["gain_post"][at(L), :].partition_broadcast(P)).then_inc(const_in, DMA)
            sp.dma_start(mgain[:], k.a["gain_mlstm"][at(L)].rearrange("a p c -> p (a c)")).then_inc(const_in, DMA)
            load_x(0, 0)
            load_x(0, 1)
            slots(sp, slot)
            for u in range(2):
                sp.wait_ge(stored[u], stored_value(L, "finish", u, NB))
            sp.sem_inc(phases, 1)

        @block.gpsimd
        def _(pool):
            def gate(b, c):
                u, m = c % 2, number(b, c)
                pool.wait_ge(loaded[u], (uses(b, c) + 1) * NLOAD * DMA)
                nc.gpsimd.tensor_tensor(hf[u][:], hf[u][:], hb[u][:], ALU.add).then_inc(hs_ok, 1)
                pool.wait_ge(sig_ok, m + 1)
                nc.gpsimd.tensor_tensor(z[u][:, 0:NZ], z[u][:, 0:NZ], e[:, 0:NZ], ALU.mult).then_inc(z_ok, 1)

            def mix_gq(b, c):
                u, m = c % 2, number(b, c)
                pool.wait_ge(z_ok, m + 2)
                pool.wait_ge(lo_ok, m + 1)
                nc.gpsimd.tensor_tensor(mix[:, 2:5, :], gq[u][:], z[u][:, 2:5, :], ALU.mult).then_inc(gqz_ok, 1)

            def residual(b, c):
                u, m = c % 2, number(b, c)
                pool.wait_ge(yn_ok, m + 1)
                pool.wait_ge(x_in[u], (uses(b, c) + 1) * DMA)
                pool.wait_ge(stored[u], stored_value(L, "finish", u, b + c // 2))
                nc.gpsimd.tensor_tensor(xo[u][:], x[u][:], y[:], ALU.add).then_inc(x_ok, 1)

            def slot(b, c):
                if exists(b, c + 1):
                    mix_gq(b, c + 1)
                if exists(b, c - 1):
                    residual(b, c - 1)
                if exists(b, c + 2):
                    gate(b, c + 2)

            slots(pool, slot)

        @block.scalar
        def _(act):
            for t in range(KT):
                act.wait_ge(wr_in[t % 2], (L * (KT // 2) + t // 2 + 1) * DMA)
                nc.scalar.copy(w_hi[:, t, :], w_raw[t % 2][:]).then_inc(whi_ok, 1)

            def log_part(b, c):
                u, m = c % 2, number(b, c)
                st = Steps(act, sig_chain, m * 2)
                act.wait_ge(loaded[u], (uses(b, c) + 1) * NLOAD * DMA)
                act.wait_ge(z_ok, m + 1)
                act.wait_ge(o_ok, m + 1)
                st.mark(nc.scalar.activation(e[:], z[u][:], ACT.Abs))
                st.join()
                st.mark(nc.scalar.activation(e[:], e[:], ACT.Exp, scale=-1.0))
                st.join()
                nc.scalar.activation(e[:], e[:], ACT.Ln, bias=cols["one"]).then_inc(ln_ok, 1)

            def sigmoid(b, c):
                act.wait_ge(logsig_ok, number(b, c) + 1)
                nc.scalar.activation(e[:], e[:], ACT.Exp).then_inc(sig_ok, 1)

            def head_scales(b, c):
                m = number(b, c)
                act.wait_ge(hss_ok, m + 1)
                nc.scalar.activation(hst[:, 1, :], hst[:, 0, :], ACT.Ln, scale=1.0 / HD, bias=cols["eps"]).then_inc(hrs_a, 1)
                act.wait_ge(lse_ok, m + 1)
                nc.scalar.activation(al[:, 1], al[:, 0], ACT.Exp).then_inc(ea_ok, 1)
                act.wait_ge(hrs_a, m + 1)
                nc.scalar.activation(hst[:, 2, :], hst[:, 1, :], ACT.Exp, scale=-0.5).then_inc(hrs_ok, 1)

            def high_part(b, c):
                act.wait_ge(mix_ok, number(b, c) + 1)
                nc.scalar.copy(m_hi[c % 2][:], mix[:]).then_inc(hi_ok, 1)

            def row_scale(b, c):
                u, m = c % 2, number(b, c)
                st = Steps(act, ys_ok, m * 2)
                act.wait_ge(y_done, m + 1)
                act.wait_ge(x_ok, m + 1)
                st.mark(nc.scalar.activation(y[:], ps_y[u][:], ACT.Square, accum_out=yst[:, 0:1]))
                st.join()
                st.mark(nc.scalar.activation(yst[:, 1:2], yst[:, 0:1], ACT.Ln, scale=1.0 / D_MODEL, bias=cols["eps"]))
                st.join()
                nc.scalar.activation(yst[:, 2:3], yst[:, 1:2], ACT.Exp, scale=-0.5).then_inc(yr_ok, 1)

            def slot(b, c):
                if exists(b, c - 1):
                    row_scale(b, c - 1)
                if exists(b, c + 1):
                    head_scales(b, c + 1)
                if exists(b, c + 2):
                    log_part(b, c + 2)
                    sigmoid(b, c + 2)
                if exists(b, c + 1):
                    high_part(b, c + 1)

            slots(act, slot)

        @block.vector
        def _(dve):
            for t in range(KT):
                dve.wait_ge(whi_ok, L * KT + t + 1)
                nc.vector.tensor_tensor(w_lo[:, t, :], w_raw[t % 2][:], w_hi[:, t, :].bitcast(F32), ALU.subtract).then_inc(wlo_ok, 1)
            dve.wait_ge(const_in, consts_value(L, "finish"))

            def normalise(b, c):
                u, m = c % 2, number(b, c)
                st = Steps(dve, chain, m * NCHAIN)
                dve.wait_ge(o_ok, m + 2)
                dve.wait_ge(hs_ok, m + 1)
                st.mark(nc.vector.tensor_tensor(eo[:], ps_o[:, 0:MH * HD].rearrange("p (h e) -> p h e", e=HD), hf[u][:],
                                                ALU.mult))
                lse = dl[u][:, :, :, HD].rearrange("p g h -> p h g")
                st.mark(nc.vector.tensor_reduce(am[:, 0, :], lse, AX.X, ALU.max))
                st.join()
                st.mark(nc.vector.tensor_tensor(hsq[:], eo[:], eo[:], ALU.mult))
                nc.vector.tensor_tensor(al[:, 0], lse, bc_free(am[:, 0, :], NG), ALU.subtract).then_inc(lse_ok, 1)
                st.join()
                nc.vector.tensor_reduce(hst[:, 0, :], hsq[:], AX.X, ALU.add).then_inc(hss_ok, 1)
                dve.wait_ge(ea_ok, m + 1)
                st.mark(nc.vector.tensor_reduce(am[:, 1, :], al[:, 1], AX.X, ALU.add))
                st.join()
                st.mark(nc.vector.reciprocal(am[:, 1, :], am[:, 1, :]))
                st.join()
                st.mark(nc.vector.tensor_tensor(al[:, 1], al[:, 1], bc_free(am[:, 1, :], NG), ALU.mult))
                st.join()
                for h in range(2):
                    st.mark(nc.vector.tensor_tensor(od[:, :, h, :], dl[u][:, :, h, 0:HD],
                                                    bc_free(al[:, 1, h, :], HD), ALU.mult))
                dve.wait_ge(hrs_ok, m + 1)
                nc.vector.tensor_tensor(hf[u][:], eo[:], bc_free(hst[:, 2, :], HD), ALU.mult).then_inc(hn_ok, 1)
                return st

            def gate_mixed(b, c, st):
                u, m = c % 2, number(b, c)
                dve.wait_ge(turned, m + 1)
                dve.wait_ge(gqz_ok, m + 1)
                for j in range(2):
                    ins = nc.vector.scalar_tensor_tensor(out=mix[:, j, :], in0=ps_h[:, j, :], scalar=mgain[:, j:j + 1],
                                                         in1=z[u][:, j, :], op0=ALU.mult, op1=ALU.mult)
                st.mark(ins)
                nc.vector.tensor_tensor(mix[:, 5:8, :], ps_d[:, 0:3, :], z[u][:, 5:8, :], ALU.mult).then_inc(mix_ok, 1)
                dve.wait_ge(hi_ok, m + 1)
                nc.vector.tensor_tensor(m_lo[u][:], mix[:], m_hi[u][:].bitcast(F32), ALU.subtract).then_inc(lo_ok, 1)
                assert st.n == NCHAIN, st.n

            def scale_rows(b, c):
                u, m = c % 2, number(b, c)
                dve.wait_ge(yr_ok, m + 1)
                nc.vector.scalar_tensor_tensor(out=y[:], in0=ps_y[u][:], scalar=yst[:, 2:3], in1=gpost[:],
                                               op0=ALU.mult, op1=ALU.mult).then_inc(yn_ok, 1)

            def log_sigmoid(b, c):
                u, m = c % 2, number(b, c)
                dve.wait_ge(ln_ok, m + 1)
                nc.vector.scalar_tensor_tensor(out=e[:], in0=z[u][:], scalar=0.0, in1=e[:], op0=ALU.min,
                                               op1=ALU.subtract).then_inc(logsig_ok, 1)

            def slot(b, c):
                if exists(b, c + 1):
                    st = normalise(b, c + 1)
                if exists(b, c - 1):
                    scale_rows(b, c - 1)
                if exists(b, c + 2):
                    log_sigmoid(b, c + 2)
                if exists(b, c + 1):
                    gate_mixed(b, c + 1, st)

            slots(dve, slot)

        @block.tensor
        def _(pe):
            def turn_o(b, c):
                pe.wait_ge(sig_ok, number(b, c) + 1)
                for j in range(2):
                    mm = pe.transpose(ps_o[:, j * P:(j + 1) * P], e[:, NZ + j, :], ident)
                mm.then_inc(o_ok, 1)

            def turn_heads(b, c):
                pe.wait_ge(hn_ok, number(b, c) + 1)
                h = hf[c % 2][:].rearrange("p h e -> p (h e)")
                for j in range(2):
                    pe.transpose(ps_h[:, j, :], h[:, j * P:(j + 1) * P], ident)
                for g in range(NG):
                    mm = pe.transpose(ps_d[:, g, :], od[:, g].rearrange("p h e -> p (h e)"), ident)
                mm.then_inc(turned, 1)

            def multiply(b, c, half):
                u, cols_ = c % 2, slice(half * 512, (half + 1) * 512)
                for t in range(KT):
                    for i, (a, w) in enumerate(((m_hi, w_hi), (m_lo, w_hi), (m_hi, w_lo))):
                        mm = pe.matmul(ps_y[u][:, cols_], a[u][:, t, :], w[:, t, cols_],
                                       start=(t == 0 and i == 0), stop=(t == KT - 1 and i == 2))
                return mm

            def slot(b, c):
                if exists(b, c):
                    if isinstance(b, int) and c == 0:
                        pe.wait_ge(wlo_ok, (L + 1) * KT)
                    pe.wait_ge(lo_ok, number(b, c) + 2)
                    multiply(b, c, 0)
                if exists(b, c + 1):
                    turn_heads(b, c + 1)
                if exists(b, c):
                    multiply(b, c, 1).then_inc(y_done, 1)
                if exists(b, c + 2):
                    turn_o(b, c + 2)

            slots(pe, slot)



def constants():
    c = {"ident": np.eye(P, dtype=np.float32)}
    half = HD // 2
    inv = (10000.0 ** (-np.arange(0, half, 2, dtype=np.float32) / half)).astype(np.float32)

    def angles(T):
        t = np.arange(T)
        r, col = (t // 64).astype(np.float32), (t % 64).astype(np.float32)
        return np.concatenate([r[:, None] * inv, col[:, None] * inv], axis=-1)

    ang = np.concatenate([angles(SEQ), angles(DEC_SEQ)], axis=0)
    c["cos"] = np.ascontiguousarray(np.tile(np.cos(ang).T, (4, 1)).astype(np.float32))
    c["sin"] = np.ascontiguousarray(np.tile(np.sin(ang).T, (4, 1)).astype(np.float32))
    d = np.arange(P)
    c["head_ones"] = (d[:, None] // HD == d[None, :] // HD).astype(np.float32)
    swap = np.zeros((P, P), np.float32)
    for o in range(P):
        swap[o + half if o % HD < half else o - half, o] = -1.0 if o % HD < half else 1.0
    c["rope_swap"] = swap
    s = np.full(4, HD ** -0.5, np.float32)
    c["rq_scale"] = np.tile(np.array([s[0], s[0], s[0], 1.0], np.float32), (P, 1))
    c["cv_scale"] = np.tile(np.array([1.0, 1.0, s[0], s[0]], np.float32), (P, 1))
    c["oc_scale"] = np.tile(np.array([s[0], 1.0, 1.0, 1.0], np.float32), (P, 1))
    chunk = np.arange(GR) % NT
    c["carries"] = np.stack([~np.isin(chunk, (0, NTP)), ~np.isin(chunk, (NTP - 1, NT - 1))], axis=1).astype(np.float32)
    causal = np.zeros((P, 2, P), np.float32)
    causal[:, 0][d[:, None] > d[None, :]] = -BIG
    causal[:, 1][d[:, None] < d[None, :]] = -BIG
    c["causal"] = causal
    dist = np.full((NG, NT, P, KW + 2), BIG, np.float32)
    for g, (_, dil) in enumerate(DIL):
        for h in range(2):
            dist[g, :, :, KW + h] = -2.0 ** (-8.0 * (2 * g + h + 1) / 6.0) * dil
        for n in range(NT):
            s0, T = (0, SEQ) if n < NTP else (SEQ, DEC_SEQ)
            qi = n * P - s0 + np.arange(P)[:, None]
            ki = n * P - s0 - SIDE + np.arange(KW)[None, :]
            near = (ki >= 0) & (ki < T) & (np.abs(ki - qi) <= SIDE) & (qi // (T // dil) == ki // (T // dil))
            dist[g, n, :, :KW][near] = np.abs(ki - qi)[near]
    c["dil_dist"] = dist
    return c


def encoder(nc, arrays):
    with ExitStack() as ctx:
        k = Kernel(nc, ctx, arrays)
        k.a["x"] = k.a["y"]
        k.dram("proj", (NCT, P, TOK))
        k.dram("mqk", (4, P, TOK))
        k.dram("tokmaj", (TOK, TM * P))
        k.dram("gqk_hi", (4, P, TOK))
        k.dram("gqk_lo", (4, P, TOK))
        k.dram("gqo", (GQ_HEADS, HD, TOK))
        k.dram("gate_ends", (2, GR, 2))
        k.dram("gate_m", (2, GR))
        k.dram("gate_M", (2, GR, P))
        k.dram("gate_dec", (2, GR))
        k.dram("mh", (2, TOK, MH * HD))
        k.dram("dil_in", (3 * NG, P, PADTOK))
        k.dram("dil_out", (NG, TOK, 2 * (HD + 1)))
        ident_t = sbuf(k, ctx, "ident", [P, P])
        col = sbuf(k, ctx, "cols", [P, 4])
        zeros = sbuf(k, ctx, "zeros", [P, SIDE])
        gate_cols = sbuf(k, ctx, "gate_cols", [P, 8, GR])
        decay = sbuf(k, ctx, "decay", [HD, 2 * GR])
        ident = ident_t[:]
        cols = {"eps": col[:, 0:1], "one": col[:, 1:2]}
        once, filled = k.sem("once_dma"), k.sem("once_fill")
        with nc.Block() as block:
            @block.vector
            def _(dve):
                nc.vector.memset(col[:, 0:1], EPS).then_inc(filled, 1)
                nc.vector.memset(col[:, 1:2], 1.0).then_inc(filled, 1)
                nc.vector.memset(zeros[:], 0.0).then_inc(filled, 1)
                dve.wait_ge(filled, 3)

            @block.sync
            def _(sp):
                sp.dma_start(k.a["x"], k.a["x_all"]).then_inc(once, DMA)
                sp.dma_start(ident_t[:], k.a["ident"]).then_inc(once, DMA)
                sp.wait_ge(filled, 3)
                for c in range(3 * NG):
                    for a in (0, SIDE + TOK):
                        sp.dma_start(k.a["dil_in"][c, :, a:a + SIDE], zeros[:]).then_inc(once, DMA)
                sp.wait_ge(once, (2 + 3 * NG * 2) * DMA)

            @block.scalar
            def _(act):
                nc.scalar.preload_act_table_set("natural_log_exp_and_others")
                for name, credit in CREDITS.items():
                    act.sem_inc(k.sem(name), credit)

        with nc.Fori(0, DEPTH) as L:
            with ExitStack() as held:
                h_hi = sbuf(k, held, "h_hi", [P, KT, TOK], F32R)
                h_lo = sbuf(k, held, "h_lo", [P, KT, TOK], F32R)
                pre_norm(k, L, h_hi, h_lo, ident, cols)
                project(k, L, h_hi, h_lo)
            prepare(k, L, gate_cols, decay, ident, cols)
            attend_gqa(k, L, ident)
            mlstm(k, L, gate_cols, decay)
            order_classes(k, L)
            attend_dilated(k, L, ident)
            finish(k, L, ident, cols)


def laid_out(inputs):
    f = {n: np.ascontiguousarray(np.asarray(v)) for n, v in inputs.items()}
    D = f["w_in"].shape[0]
    gates0 = 4 * MH * HD
    ng = 4 * MH
    w = f["w_in"]
    w = np.concatenate([w[:, :, :gates0], w[:, :, gates0 + ng:], w[:, :, gates0:gates0 + ng],
                        np.zeros((D, D_MODEL, P - ng), w.dtype)], axis=2)
    w = w.reshape(D, KT, P, NCT, P).transpose(0, 3, 2, 1, 4).reshape(D, NCT, P, KT * P)
    taps = np.stack([f["mlstm_conv_w"][:, 0], f["mlstm_conv_w"][:, 1], f["mlstm_conv_w"][:, 2], f["mlstm_conv_b"]], axis=-1)
    gb = f["mlstm_gate_bias"].reshape(D, 4, MH)
    qk = np.stack([np.tile(f["gqa_q_norm"], (1, 2))] * 3 + [np.tile(f["gqa_k_norm"], (1, 2))], axis=-1)
    return {
        "x_all": np.concatenate([f["x_prompt"][0], f["x_sample"][0]], axis=0),
        "w_in": w,
        "w_out": f["w_out"].reshape(D, KT, P, D_MODEL),
        "gain_pre": f["norm_pre"],
        "gain_post": f["norm_post"],
        "gain_qk": qk,
        "gain_mlstm": f["mlstm_out_gain"].reshape(D, 2, P).transpose(0, 2, 1),
        "conv_par": taps.reshape(D, 4, P, 4).transpose(0, 2, 1, 3),
        "gate_bias": np.repeat(gb, NT, axis=2).transpose(0, 2, 1),
    }


def kernel(**inputs):
    from concourse import bacc
    from concourse.bass_utils import run_bass_kernel_spmd

    nc = bacc.Bacc("TRN2", target_bir_lowering=False, num_devices=1)
    data = {n: np.ascontiguousarray(v) for n, v in (laid_out(inputs) | constants()).items()}
    arrays = {n: nc.dram_tensor(f"in_{n}", list(v.shape), F32, kind="ExternalInput").ap() for n, v in data.items()}
    arrays["y"] = nc.dram_tensor("y", [TOK, D_MODEL], F32, kind="ExternalOutput").ap()
    encoder(nc, arrays)
    y = run_bass_kernel_spmd(nc, [{f"in_{n}": v for n, v in data.items()}], core_ids=[0]).results[0]["y"]
    return y[None, :SEQ], y[None, SEQ:]
```

```python
from contextlib import ExitStack

import numpy as np

import concourse.bass as bass
from concourse import mybir

F32 = mybir.dt.float32
F32R = mybir.dt.float32r
ALU = mybir.AluOpType
ACT = mybir.ActivationFunctionType
AX = mybir.AxisListType

P = 128
D_MODEL = 1024
KT = D_MODEL // P
SEQ, DEC_SEQ = 256, 2048
TOK = SEQ + DEC_SEQ
NT = TOK // P
NTP = SEQ // P
DEPTH = 2
HD = 64
EPS = 1e-6
DMA = 16

CT_MQ, CT_MK, CT_MV, CT_MO, CT_MZ = 0, 2, 4, 6, 8
CT_GQ, CT_GK, CT_GV, CT_GZ = 10, 13, 14, 15
CT_DZ, CT_GATES = 18, 21
CT_DILATED = 22
NCT = 31

CHUNK = 384
NCH = TOK // CHUNK

GQ_HEADS, KV_HEADS = 6, 2
GQ_PER_KV = GQ_HEADS // KV_HEADS
QC = 512
NQC = DEC_SEQ // QC
DIL = ((128, 1), (512, 4), (2048, 16))
NG = len(DIL)
SIDE = 64
PADTOK = SIDE + TOK + SIDE
MH = 4
GR = MH * NT
BIG = 1.0e30


class Steps:

    def __init__(self, engine, sem, base):
        self.engine, self.sem, self.base, self.n = engine, sem, base, 0

    def mark(self, instruction):
        instruction.then_inc(self.sem, 1)
        self.n += 1

    def join(self):
        self.engine.wait_ge(self.sem, self.base + self.n)


CREDITS = {
    "proj_wlo": 2, "proj_acc": 2 * NCH, "proj_ev_act": NCH // 2, "proj_ev_dve": NCH // 2,
    "ga_exped": 2, "ga_pv_done": 4, "ga_plo_pool": 1, "ga_plo_dve": 1, "ga_max_read": 2, "ga_o_ok": 2,
    "ml_w_ok": 2, "ml_at_ok": 2, "ml_state_ok": 2, "ml_mm_ok": 6, "ml_nd_ok": 2,
    "pn_h_ok": 1, 
    
    "dl_pv_ok": 2, "dl_bias_ok": 2, "dl_vc_ok": 2, "dl_vt_ok": 2, "dl_pt_ok": 2, "dl_out_ok": 2, "dl_p_ok": 2, "dl_turned": 2,
    "dl_lse_ok": 2, "fi_z_ok": 1, "fi_o_ok": 1, "fi_lo_ok": 1, "fi_x_ok": 1,
    "stored0": DMA, "stored1": DMA, **{f"ml_stored{u}{d}": DMA for u in range(3) for d in range(2)},
}


STORES = {"project": ((NCT + 1) // 2 + 2, NCT // 2 + 1), "prepare": (8, 8),
          "gqa": (GQ_HEADS * (NQC + 1) // 2,) * 2, "dilated": (NG * NT // 2,) * 2,
          "finish": (NT // 2, NT // 2)}
CONSTS = {"prepare": 6, "mlstm": 1, "finish": 2}


def stored_value(L, step, u, n):
    steps = list(STORES)
    before = sum(STORES[s][u] for s in steps[:steps.index(step)])
    return (L * sum(STORES[s][u] for s in steps) + (n + before)) * DMA + DMA


def consts_value(L, step):
    steps = list(CONSTS)
    return (L * sum(CONSTS.values()) + sum(CONSTS[s] for s in steps[:steps.index(step) + 1])) * DMA


class Kernel:

    def __init__(self, nc, ctx, arrays):
        self.nc, self.ctx, self.a = nc, ctx, arrays
        self.sems = {}

    def sem(self, name):
        if name not in self.sems:
            self.sems[name] = self.ctx.enter_context(self.nc.semaphore(name))
        return self.sems[name]

    def dram(self, name, shape):
        self.a[name] = self.nc.dram_tensor(name, list(shape), F32).ap()
        return self.a[name]


def sbuf(k, ctx, name, shape, dtype=F32):
    return ctx.enter_context(k.nc.sbuf_tensor(name, list(shape), dtype))


def psum(k, ctx, name, shape):
    return ctx.enter_context(k.nc.psum_tensor(name, list(shape), F32))


def pair(k, ctx, name, shape, dtype=F32):
    return [sbuf(k, ctx, f"{name}{u}", shape, dtype) for u in range(2)]


def at(i, n=1):
    return bass.ds(i, n)


def bc_free(ap, n):
    return ap.unsqueeze(2).to_broadcast([*ap.shape, n])


def rows_of(dram, row0, nrows, col0, ncols):
    return dram[at(row0, nrows), at(col0, ncols)]


def pre_norm(k, L, h_hi, h_lo, ident, cols):
    nc = k.nc
    NB = NT // 2
    with ExitStack() as ctx:
        x = pair(k, ctx, "pn_x", [P, D_MODEL])
        hn = pair(k, ctx, "pn_hn", [P, D_MODEL])
        junk = sbuf(k, ctx, "pn_junk", [P, D_MODEL])
        gain = sbuf(k, ctx, "pn_gain", [P, D_MODEL])
        stat = pair(k, ctx, "pn_stat", [P, 4])
        tr = [psum(k, ctx, f"pn_tr{u}", [P, KT, P]) for u in range(2)]
        x_in = [k.sem(f"pn_x_in{u}") for u in range(2)]
        gain_in, stats, rstd_ok, h_ok, turned, hi_ok, lo_ok = (
            k.sem("pn_" + s) for s in ("gain_in", "stats", "rstd_ok", "h_ok", "turned", "hi_ok", "lo_ok"))
        block = ctx.enter_context(nc.Block())

        @block.sync
        def _(sp):
            sp.dma_start(gain[:], k.a["gain_pre"][at(L), :].partition_broadcast(P)).then_inc(gain_in, DMA)
            with sp.Fori(0, NB) as b:
                for u in range(2):
                    sp.wait_ge(h_ok, (L * NB + b) * 2 + 1)
                    sp.dma_start(x[u][:], rows_of(k.a["x"], b * 2 * P + u * P, P, 0, D_MODEL)).then_inc(x_in[u], DMA)

        @block.scalar
        def _(act):
            with act.Fori(0, NB) as b:
                n = L * NB + b
                for u in range(2):
                    st = Steps(act, stats, (n * 2 + u) * 2)
                    act.wait_ge(x_in[u], (n + 1) * DMA)
                    st.mark(nc.scalar.activation(junk[:], x[u][:], ACT.Square, accum_out=stat[u][:, 0:1]))
                    st.join()
                    st.mark(nc.scalar.activation(stat[u][:, 1:2], stat[u][:, 0:1], ACT.Ln,
                                                 scale=1.0 / D_MODEL, bias=cols["eps"]))
                    st.join()
                    nc.scalar.activation(stat[u][:, 2:3], stat[u][:, 1:2], ACT.Exp, scale=-0.5).then_inc(rstd_ok, 1)
                for u in range(2):
                    act.wait_ge(turned, n * 2 + u + 1)
                    nc.scalar.copy(h_hi[:, :, at(b * 2 * P + u * P, P)], tr[u][:]).then_inc(hi_ok, 1)

        @block.vector
        def _(dve):
            with dve.Fori(0, NB) as b:
                n = L * NB + b
                dve.wait_ge(gain_in, (L + 1) * DMA)
                for u in range(2):
                    dve.wait_ge(rstd_ok, n * 2 + u + 1)
                    nc.vector.scalar_tensor_tensor(out=hn[u][:], in0=x[u][:], scalar=stat[u][:, 2:3], in1=gain[:],
                                                   op0=ALU.mult, op1=ALU.mult).then_inc(h_ok, 1)
                for u in range(2):
                    dve.wait_ge(hi_ok, n * 2 + u + 1)
                    tile = at(b * 2 * P + u * P, P)
                    nc.vector.tensor_tensor(h_lo[:, :, tile], tr[u][:], h_hi[:, :, tile].bitcast(F32),
                                            ALU.subtract).then_inc(lo_ok, 1)

        @block.tensor
        def _(pe):
            with pe.Fori(0, NB) as b:
                n = L * NB + b
                for u in range(2):
                    pe.wait_ge(h_ok, n * 2 + u + 2)
                    for j in range(KT):
                        last = pe.transpose(tr[u][:, j, :], hn[u][:, j * P:(j + 1) * P], ident)
                    last.then_inc(turned, 1)


def project(k, L, h_hi, h_lo):
    nc = k.nc
    phases = k.sem("phases_stored")
    NB = NCT // 2
    with ExitStack() as ctx:
        w = pair(k, ctx, "pj_w", [P, KT, P])
        w_hi = pair(k, ctx, "pj_whi", [P, KT, P], F32R)
        w_lo = pair(k, ctx, "pj_wlo", [P, KT, P], F32R)
        stage = pair(k, ctx, "pj_stage", [P, TOK])
        acc = [psum(k, ctx, f"pj_acc{c}", [P, 512]) for c in range(NCH)]
        w_in = [k.sem(f"proj_w_in{u}") for u in range(2)]
        stored = [k.sem(f"stored{u}") for u in range(2)]
        whi, wlo, done = k.sem("proj_whi"), k.sem("proj_wlo"), k.sem("proj_acc")
        ev_act, ev_dve = k.sem("proj_ev_act"), k.sem("proj_ev_dve")
        cnt = (L * ((NCT + 1) // 2), L * (NCT // 2))
        block = ctx.enter_context(nc.Block())

        def slots(engine, slot, ordered=None):
            with engine.Fori(0, (CT_DILATED if ordered else NCT - 1) // 2) as b:
                for u in range(2):
                    slot(b * 2 + u, b, u, False)
            for ct in range(CT_DILATED if ordered else NCT - 1, NCT):
                (ordered or slot)(ct, ct // 2, ct % 2, ct == NCT - 1)

        @block.sync
        def _(sp):
            def load(ct, b, u):
                sp.wait_ge(wlo, L * NCT + ct + 1)
                sp.dma_start(w[u][:], k.a["w_in"][at(L), at(ct)].rearrange("a b p (t c) -> p (a b t) c", c=P)
                             ).then_inc(w_in[u], DMA)

            def evacuated(ct):
                both = (L * NCT + ct + 2) * (NCH // 2)
                sp.wait_ge(ev_act, both)
                sp.wait_ge(ev_dve, both)

            def slot(ct, b, u, last):
                load(ct + 1, b + u, 1 - u)
                evacuated(ct)
                sp.dma_start(k.a["proj"][at(ct)].rearrange("a p t -> p (a t)"), stage[u][:]).then_inc(stored[u], DMA)

            def ordered(ct, b, u, last):
                if not last:
                    load(ct + 1, b + u, 1 - u)
                evacuated(ct)
                kind, g = divmod(ct - CT_DILATED, NG)
                if kind:
                    sp.dma_start(k.a["dil_kv"][g, kind - 1][:, SIDE:SIDE + TOK], stage[u][:]).then_inc(stored[u], DMA)
                else:
                    for h in range(2):
                        rows = slice(h * HD, (h + 1) * HD)
                        sp.dma_start(k.a["dil_q"][g, h, rows], stage[u][rows, :]).then_inc(stored[u], DMA)

            load(0, 0, 0)
            slots(sp, slot, ordered)
            for u in range(2):
                sp.wait_ge(stored[u], stored_value(L, "project", u, STORES["project"][u]))
            sp.sem_inc(phases, 1)

        def evacuate(engine, copy, ct, b, u, parity, sem):
            engine.wait_ge(stored[u], stored_value(L, "project", u, b))
            for c in range(parity, NCH, 2):
                engine.wait_ge(done, (L * NCT + ct) * NCH + c + 1 + 2 * NCH)
                copy(stage[u][:, c * CHUNK:(c + 1) * CHUNK], acc[c][:, 0:CHUNK]).then_inc(sem, 1)

        def evacuate_ordered(engine, copy, ct, b, u, parity, sem):
            kind, g = divmod(ct - CT_DILATED, NG)
            dil, factor = DIL[g][1], HD ** -0.5 if kind == 0 else 1.0
            q_before = len(range(CT_DILATED + (CT_DILATED + u) % 2, min(ct, CT_DILATED + NG), 2))
            engine.wait_ge(stored[u], stored_value(L, "project", u, b + q_before))
            for c in range(parity, NCH, 2):
                engine.wait_ge(done, (L * NCT + ct) * NCH + c + 1 + 2 * NCH)
                for s0, s1 in ((0, SEQ), (SEQ, TOK)):
                    a, z = max(s0, c * CHUNK), min(s1, (c + 1) * CHUNK)
                    if a < z:
                        places = stage[u][:, s0:s1].rearrange("p (r j) -> p j r", r=dil)
                        ins = copy(places[:, (a - s0) // dil:(z - s0) // dil, :],
                                   acc[c][:, a - c * CHUNK:z - c * CHUNK].rearrange("p (j r) -> p j r", r=dil), factor)
                ins.then_inc(sem, 1)

        @block.scalar
        def _(act):
            def split(ct, b, u):
                act.wait_ge(w_in[u], (cnt[u] + b + 1) * DMA)
                act.wait_ge(done, (L * NCT + ct + 1) * NCH - NCH + NCH)
                nc.scalar.copy(w_hi[u][:], w[u][:]).then_inc(whi, 1)

            def slot(ct, b, u, last):
                if not last:
                    split(ct + 1, b + u, 1 - u)
                evacuate(act, nc.scalar.copy, ct, b, u, 0, ev_act)

            def ordered(ct, b, u, last):
                if not last:
                    split(ct + 1, b + u, 1 - u)
                evacuate_ordered(act, lambda o, i, f: nc.scalar.activation(o, i, ACT.Copy, scale=f), ct, b, u, 0, ev_act)

            split(0, 0, 0)
            slots(act, slot, ordered)

        @block.vector
        def _(dve):
            def split(ct, b, u):
                dve.wait_ge(whi, L * NCT + ct + 1)
                nc.vector.tensor_tensor(w_lo[u][:], w[u][:], w_hi[u][:].bitcast(F32), ALU.subtract).then_inc(wlo, 1)

            def slot(ct, b, u, last):
                if not last:
                    split(ct + 1, b + u, 1 - u)
                evacuate(dve, nc.vector.tensor_copy, ct, b, u, 1, ev_dve)

            def ordered(ct, b, u, last):
                if not last:
                    split(ct + 1, b + u, 1 - u)
                evacuate_ordered(dve, lambda o, i, f: nc.vector.tensor_scalar(o, i, f, None, ALU.mult), ct, b, u, 1, ev_dve)

            split(0, 0, 0)
            slots(dve, slot, ordered)

        @block.tensor
        def _(pe):
            def slot(ct, b, u, last):
                pe.wait_ge(wlo, L * NCT + ct + 1 + 2)
                for c in range(NCH):
                    pe.wait_ge((ev_act, ev_dve)[c % 2], (L * NCT + ct) * (NCH // 2) + c // 2 + 1)
                    tok = slice(c * CHUNK, (c + 1) * CHUNK)
                    for t in range(KT):
                        for i, (wt, ht) in enumerate(((w_hi, h_hi), (w_hi, h_lo), (w_lo, h_hi))):
                            mm = pe.matmul(acc[c][:, 0:CHUNK], wt[u][:, t, :], ht[:, t, tok],
                                           start=(t == 0 and i == 0), stop=(t == KT - 1 and i == 2))
                    mm.then_inc(done, 1)

            slots(pe, slot)


PIECES = ((0, SEQ + 2 * QC), (SEQ + 2 * QC, TOK))
TM = 5


def prepare(k, L, gate_cols, decay, ident, cols):
    nc = k.nc
    phases = k.sem("phases_stored")
    W = PIECES[0][1]
    NJ = 4
    SMOOTH = (2, 3, 0, 1)
    TURNS = ((4, "load", CT_GV), (2, "load", CT_MV), (0, "smoothed", 0), (3, "load", CT_MV + 1), (1, "smoothed", 1))
    GROUPS = -(-NT // 4)
    TRA, TRD = (TM * GROUPS + 1) // 2, TM * GROUPS // 2
    with ExitStack() as ctx:
        raw = [sbuf(k, ctx, f"rq_raw{u}", [P, z - a]) for u, (a, z) in enumerate(PIECES)]
        sq, rs, qn, t1 = ([sbuf(k, ctx, f"rq_{x}{u}", [P, z - a]) for u, (a, z) in enumerate(PIECES)]
                          for x in ("sq", "rs", "qn", "t1"))
        hi, lo = ([sbuf(k, ctx, f"rq_{x}{u}", [P, z - a], F32R) for u, (a, z) in enumerate(PIECES)] for x in ("hi", "lo"))
        cos, sin = (sbuf(k, ctx, "rq_" + x, [P, TOK]) for x in ("cos", "sin"))
        blk, rot = (sbuf(k, ctx, "rq_" + x, [P, P]) for x in ("blk", "rot"))
        gain, scale = (sbuf(k, ctx, "rq_" + x, [P, 4]) for x in ("gain", "scale"))
        x, y = pair(k, ctx, "sm_x", [P, TOK]), pair(k, ctx, "sm_y", [P, TOK])
        e = sbuf(k, ctx, "sm_e", [P, TOK])
        par = sbuf(k, ctx, "sm_par", [P, 4, 4])
        sm_scale = sbuf(k, ctx, "sm_scale", [P, 4])
        tv = pair(k, ctx, "tt_f", [P, TOK])
        t_out = pair(k, ctx, "tt_t", [P, NT, P])

        def both(name, shape=(GR, P)):
            return pair(k, ctx, "gr_" + name, shape)

        gi, gf, ge, mn, b, a_, M, bm, wi, em, kws = (both(n) for n in ("i", "f", "e", "mn", "b", "a", "M", "bm", "wi", "em", "kws"))
        ends, m_col, n_end, dec = both("ends", (GR, 2)), both("mcol", (GR, 1)), both("nend", (GR, 2)), both("dec", (GR, 1))
        m_in, m_out = both("m_in", (MH, NT, 2)), both("m_out", (MH, NT))
        zero = sbuf(k, ctx, "gr_zero", [GR, P])
        bias = sbuf(k, ctx, "gr_bias", [GR, 4])
        carries = sbuf(k, ctx, "gr_carries", [GR, 2])
        ss, rx = psum(k, ctx, "rq_ss", [P, 3 * 512]), psum(k, ctx, "rq_rx", [P, 3 * 512])
        tr = [psum(k, ctx, f"tt_tr{u}", [P, 4, P]) for u in range(2)]
        const_in, table_in, gain_ok = k.sem("consts_in"), k.sem("rq_table_in"), k.sem("rq_gain_ok")
        raw_in, x_in, tv_in = ([k.sem(f"{n}{u}") for u in range(2)] for n in ("rq_raw_in", "sm_x_in", "tt_in"))
        stored, y_stored, t_stored = ([k.sem(f"{n}{u}") for u in range(2)] for n in ("stored", "sm_stored", "tt_stored"))
        sq_ok, ss_ok, ln_ok, rs_ok, qn_ok, t1_ok, rx_ok, rs_sin_ok, sum_ok, hi_ok, lo_ok = (
            k.sem("rq_" + n) for n in ("sq_ok", "ss_ok", "ln_ok", "rs_ok", "qn_ok", "t1_ok", "rx_ok", "sin_ok",
                                       "sum_ok", "hi_ok", "lo_ok"))
        mid_ok, conv_ok, log_ok, logsig_ok, sig_ok, chain, smooth_ok = (
            k.sem("sm_" + n) for n in ("mid_ok", "conv_ok", "log_ok", "logsig_ok", "sig_ok", "chain", "smooth_ok"))
        turned, tr_act, tr_dve = k.sem("tt_turned"), k.sem("tt_act"), k.sem("tt_dve")
        g_in, hop, g_out = k.sem("gr_g_in"), k.sem("gr_hop"), k.sem("gr_out")
        sa, sv, g_turned, g_done = k.sem("gr_act"), k.sem("gr_dve"), k.sem("gr_turned"), k.sem("gr_done")
        block = ctx.enter_context(nc.Block())
        NA, NV = 14, 32
        NA1, NV1, NV2, NV3 = 6, 14, 20, 32
        NIN = 6

        def item(j, u):
            return L * (NJ * 2) + (j * 2 + u)

        def turns_of(j):
            return {0: (0, 1), 1: (2, 3), 2: (4, None), 3: (None, None)}[j]

        def groups(i):
            return [(i * GROUPS + g, g * 4, min(4, NT - g * 4)) for g in range(GROUPS)]

        def copy_turned(engine, copy, parity, i):
            if i is None:
                return
            if i >= 2:
                engine.wait_ge(t_stored[i % 2], (L * ((TM + 1 - i % 2) // 2) + i // 2) * DMA)
            for g, tile, n in groups(i):
                if g % 2 == parity:
                    if g == (i + 1) * GROUPS - 1:
                        engine.wait_ge((tr_dve, tr_act)[parity], L * (TRD, TRA)[parity] + (g - 1) // 2 + 1)
                    engine.wait_ge(turned, L * TM * GROUPS + g + 1)
                    copy(t_out[i % 2][:, tile:tile + n, :], tr[g % 2][:, 0:n, :]).then_inc((tr_act, tr_dve)[parity], 1)

        def ends_of(t, d):
            return t[d][:, P - 1:P] if d == 0 else t[d][:, 0:1]

        def flow(t, d):
            return t[d][:, :] if d == 0 else t[d][:, ::-1]

        @block.sync
        def _(sp):
            def load_rotate(j):
                for u, (a, z) in enumerate(PIECES):
                    if j:
                        sp.wait_ge(qn_ok, item(j - 1, u) + 1)
                    sp.dma_start(raw[u][:], k.a["proj"][CT_GQ + j, :, a:z]).then_inc(raw_in[u], DMA)

            def load_smooth(j):
                if j >= 2:
                    sp.wait_ge(conv_ok, L * NJ + j - 1)
                sp.dma_start(x[j % 2][:], k.a["proj"][CT_MQ + SMOOTH[j]]).then_inc(x_in[j % 2], DMA)

            def load_turn(i, w):
                if w >= 2:
                    sp.wait_ge(turned, L * TM * GROUPS + GROUPS)
                sp.dma_start(tv[w % 2][:], k.a["proj"][TURNS[i][2]]).then_inc(tv_in[w % 2], DMA)

            def store_rotate(j):
                for u, (a, z) in enumerate(PIECES):
                    for half, ok, name in ((hi, hi_ok, "gqk_hi"), (lo, lo_ok, "gqk_lo")):
                        sp.wait_ge(ok, item(j, u) + 1)
                        sp.dma_start(k.a[name][j, :, a:z], half[u][:].bitcast(F32)).then_inc(stored[u], DMA)

            def store_smooth(j):
                sp.wait_ge(smooth_ok, L * NJ + j + 1)
                if j < 2:
                    sp.dma_start(k.a["mqk"][4 + j], y[j % 2][:]).then_inc(y_stored[j % 2], DMA)
                else:
                    for e_ in range(2):
                        rows = slice(e_ * HD, (e_ + 1) * HD)
                        sp.dma_start(k.a["mqk"][(j - 2) * 2 + e_, rows], y[j % 2][rows, :]).then_inc(y_stored[j % 2], DMA)

            def store_turn(i):
                if i is not None:
                    last = (i + 1) * GROUPS - 1
                    sp.wait_ge((tr_act, tr_dve)[last % 2], L * (TRA, TRD)[last % 2] + last // 2 + 1)
                    c = TURNS[i][0]
                    sp.dma_start(k.a["tokmaj"][:, c * P:(c + 1) * P].rearrange("(n p) d -> p n d", p=P),
                                 t_out[i % 2][:]).then_inc(t_stored[i % 2], DMA)

            def ends_to_heads():
                sp.wait_ge(sv, L * NV + NV1)
                for d in range(2):
                    sp.dma_start(k.a["gate_ends"][d], ends[d][:]).then_inc(hop, DMA)
                sp.wait_ge(hop, (L * 8 + 2) * DMA)
                for d in range(2):
                    sp.dma_start(m_in[d][:], k.a["gate_ends"][d].rearrange("(h c) x -> h c x", h=MH)).then_inc(hop, DMA)

            def stabilisers_to_chunks():
                sp.wait_ge(sv, L * NV + NV2)
                for d in range(2):
                    sp.dma_start(k.a["gate_m"][d].rearrange("(h c) -> h c", h=MH), m_out[d][:]).then_inc(hop, DMA)
                sp.wait_ge(hop, (L * 8 + 6) * DMA)
                for d in range(2):
                    sp.dma_start(m_col[d][:], k.a["gate_m"][d].rearrange("(p x) -> p x", x=1)).then_inc(hop, DMA)

            def store_gates():
                sp.wait_ge(sv, L * NV + NV3)
                for d in range(2):
                    sp.dma_start(k.a["gate_M"][d], M[d][:]).then_inc(g_out, DMA)
                    sp.dma_start(k.a["gate_dec"][d].rearrange("(p x) -> p x", x=1), dec[d][:]).then_inc(g_out, DMA)
                sp.wait_ge(g_out, (L * 8 + 4) * DMA)
                for d in range(2):
                    for e in range(2):
                        dec_e = k.a["gate_dec"][d].rearrange("(r e c) -> e r c", e=2, c=NT)[e]
                        sp.dma_start(decay[e * HD:(e + 1) * HD, d], dec_e.partition_broadcast(HD)).then_inc(g_out, DMA)

            load_rotate(0)
            load_smooth(0)
            sp.dma_start(par[:], k.a["conv_par"][at(L)].rearrange("a p c j -> p (a c) j")).then_inc(const_in, DMA)
            sp.dma_start(gain[:], k.a["gain_qk"][at(L)].rearrange("a p c -> p (a c)")).then_inc(const_in, DMA)
            for dst, src in ((sm_scale, "cv_scale"), (blk, "head_ones"), (rot, "rope_swap"), (scale, "rq_scale")):
                sp.dma_start(dst[:], k.a[src]).then_inc(const_in, DMA)
            sp.dma_start(bias[:], k.a["gate_bias"][at(L)].rearrange("a p c -> p (a c)")).then_inc(g_in, DMA)
            sp.dma_start(carries[:], k.a["carries"]).then_inc(g_in, DMA)
            for d in range(2):
                for t, r in ((gi, 0), (gf, MH)):
                    rows = k.a["proj"][CT_GATES, d * 2 * MH + r:d * 2 * MH + r + MH, :]
                    sp.dma_start(t[d][:], rows.rearrange("h (c l) -> (h c) l", l=P)).then_inc(g_in, DMA)
            for dst, src in ((cos, "cos"), (sin, "sin")):
                sp.dma_start(dst[:], k.a[src]).then_inc(table_in, DMA)
            load_turn(0, 0)
            load_turn(1, 1)
            for j in range(NJ):
                if j + 1 < NJ:
                    load_smooth(j + 1)
                    load_rotate(j + 1)
                if j == 1:
                    load_turn(3, 2)
                if j < 3:
                    (ends_to_heads, stabilisers_to_chunks, store_gates)[j]()
                store_turn(turns_of(j)[0])
                store_rotate(j)
                store_smooth(j)
                store_turn(turns_of(j)[1])
            for u in range(2):
                sp.wait_ge(stored[u], stored_value(L, "prepare", u, NJ * 2))
                sp.wait_ge(y_stored[u], (L + 1) * 3 * DMA)
                sp.wait_ge(t_stored[u], (L + 1) * ((TM + 1 - u) // 2) * DMA)
            sp.wait_ge(g_out, (L + 1) * 8 * DMA)
            sp.sem_inc(phases, 1)

        @block.scalar
        def _(act):
            gates = Steps(act, sa, L * NA)

            def square(j, u):
                act.wait_ge(raw_in[u], (L * NJ + j + 1) * DMA)
                if j:
                    act.wait_ge(rs_ok, item(j - 1, u) + 1)
                nc.scalar.activation(sq[u][:], raw[u][:], ACT.Square).then_inc(sq_ok, 1)

            def rsqrt(j, u):
                n, m = item(j, u), PIECES[u][1] - PIECES[u][0]
                act.wait_ge(ss_ok, n + 1)
                nc.scalar.activation(sq[u][:], ss[:, 0:m], ACT.Ln, scale=1.0 / HD, bias=cols["eps"]).then_inc(ln_ok, 1)
                act.wait_ge(ln_ok, n + 1)
                if j:
                    act.wait_ge(qn_ok, item(j - 1, u) + 1)
                nc.scalar.activation(rs[u][:], sq[u][:], ACT.Exp, scale=-0.5).then_inc(rs_ok, 1)

            def high_part(j, u):
                act.wait_ge(sum_ok, item(j, u) + 1)
                act.wait_ge(stored[u], stored_value(L, "prepare", u, j * 2))
                nc.scalar.copy(hi[u][:], t1[u][:]).then_inc(hi_ok, 1)

            def middle_tap(j):
                u, ct = j % 2, SMOOTH[j]
                act.wait_ge(x_in[u], (L * (NJ // 2) + j // 2 + 1) * DMA)
                if j >= 2:
                    act.wait_ge(y_stored[u], (L * 3 + 1) * DMA)
                nc.scalar.activation(y[u][:], x[u][:], ACT.Identity, scale=par[:, ct, 1:2], bias=par[:, ct, 3:4]).then_inc(mid_ok, 1)

            def log_part(j):
                act.wait_ge(conv_ok, L * NJ + j + 1)
                if j:
                    act.wait_ge(smooth_ok, L * NJ + j)
                nc.scalar.activation(e[:], y[j % 2][:], ACT.Abs).then_inc(log_ok, 1)
                act.wait_ge(log_ok, (L * NJ + j) * 3 + 1)
                nc.scalar.activation(e[:], e[:], ACT.Exp, scale=-1.0).then_inc(log_ok, 1)
                act.wait_ge(log_ok, (L * NJ + j) * 3 + 2)
                nc.scalar.activation(e[:], e[:], ACT.Ln, bias=cols["one"]).then_inc(log_ok, 1)

            def sigmoid(j):
                act.wait_ge(logsig_ok, L * NJ + j + 1)
                nc.scalar.activation(e[:], e[:], ACT.Exp).then_inc(sig_ok, 1)

            def gate_logs():
                st = gates
                act.wait_ge(g_in, (L + 1) * NIN * DMA)
                for d in range(2):
                    st.mark(nc.scalar.activation(ge[d][:], gf[d][:], ACT.Abs, bias=bias[:, 2 * d + 1:2 * d + 2]))
                for d in range(2):
                    st.join()
                    st.mark(nc.scalar.activation(ge[d][:], ge[d][:], ACT.Exp, scale=-1.0))
                for d in range(2):
                    st.join()
                    st.mark(nc.scalar.activation(ge[d][:], ge[d][:], ACT.Ln, bias=cols["one"][0:GR]))
                assert st.n == NA1

            def gate_weights():
                st = gates
                act.wait_ge(sv, L * NV + NV2 + 8)
                for d in range(2):
                    st.mark(nc.scalar.activation(wi[d][:], M[d][:], ACT.Exp, scale=-1.0, bias=m_col[d][:, 0:1]))
                    st.mark(nc.scalar.activation(em[d][:], bm[d][:], ACT.Exp, scale=-1.0))
                    st.mark(nc.scalar.activation(kws[d][:], a_[d][:], ACT.Exp, bias=n_end[d][:, 0:1]))
                    st.mark(nc.scalar.activation(dec[d][:], n_end[d][:, 0:1], ACT.Exp, bias=m_col[d][:, 0:1]))
                assert st.n == NA

            act.wait_ge(const_in, consts_value(L, "prepare"))
            for j in range(NJ):
                square(j, 0)
                square(j, 1)
                middle_tap(j)
                if j == 0:
                    gate_logs()
                rsqrt(j, 0)
                rsqrt(j, 1)
                copy_turned(act, nc.scalar.copy, 0, turns_of(j)[0])
                if j == 2:
                    gate_weights()
                log_part(j)
                high_part(j, 0)
                high_part(j, 1)
                sigmoid(j)
                copy_turned(act, nc.scalar.copy, 0, turns_of(j)[1])
            for d in range(2):
                act.wait_ge(g_turned, L * 2 + d + 1)
                nc.scalar.copy(gate_cols[:, d * 4:d * 4 + 4, :], tr[d][:, :, 0:GR]).then_inc(g_done, 1)

        @block.vector
        def _(dve):
            gates = Steps(dve, sv, L * NV)

            def normalise(j, u):
                n = item(j, u)
                dve.wait_ge(rs_ok, n + 1)
                if j:
                    dve.wait_ge(sum_ok, item(j - 1, u) + 1)
                nc.vector.scalar_tensor_tensor(out=qn[u][:], in0=raw[u][:], scalar=gain[:, j:j + 1], in1=rs[u][:],
                                               op0=ALU.mult, op1=ALU.mult).then_inc(qn_ok, 1)

            def add_turn(j, u):
                n, (a, z) = item(j, u), PIECES[u]
                dve.wait_ge(t1_ok, n + 1)
                dve.wait_ge(rx_ok, n + 1)
                nc.vector.tensor_tensor(qn[u][:], rx[:, 0:z - a], sin[:, a:z], ALU.mult).then_inc(rs_sin_ok, 1)
                dve.wait_ge(rs_sin_ok, n + 1)
                nc.vector.tensor_tensor(t1[u][:], t1[u][:], qn[u][:], ALU.add).then_inc(sum_ok, 1)

            def low_part(j, u):
                dve.wait_ge(hi_ok, item(j, u) + 1)
                nc.vector.tensor_tensor(lo[u][:], t1[u][:], hi[u][:].bitcast(F32), ALU.subtract).then_inc(lo_ok, 1)

            def outer_taps(j):
                u, ct = j % 2, SMOOTH[j]
                st = Steps(dve, chain, (L * NJ + j) * 3)
                dve.wait_ge(mid_ok, L * NJ + j + 1)
                for s0, s1 in ((0, SEQ), (SEQ, TOK)):
                    st.mark(nc.vector.scalar_tensor_tensor(out=y[u][:, s0 + 1:s1], in0=x[u][:, s0:s1 - 1],
                                                           scalar=par[:, ct, 0:1], in1=y[u][:, s0 + 1:s1],
                                                           op0=ALU.mult, op1=ALU.add))
                for i, (s0, s1) in enumerate(((0, SEQ), (SEQ, TOK))):
                    st.join()
                    ins = nc.vector.scalar_tensor_tensor(out=y[u][:, s0:s1 - 1], in0=x[u][:, s0 + 1:s1],
                                                         scalar=par[:, ct, 2:3], in1=y[u][:, s0:s1 - 1],
                                                         op0=ALU.mult, op1=ALU.add)
                    if i == 0:
                        st.mark(ins)
                    else:
                        ins.then_inc(conv_ok, 1)

            def log_sigmoid(j):
                dve.wait_ge(log_ok, (L * NJ + j + 1) * 3)
                nc.vector.scalar_tensor_tensor(out=e[:], in0=y[j % 2][:], scalar=0.0, in1=e[:], op0=ALU.min,
                                               op1=ALU.subtract).then_inc(logsig_ok, 1)

            def gated(j):
                u, ct = j % 2, SMOOTH[j]
                dve.wait_ge(sig_ok, L * NJ + j + 1)
                nc.vector.scalar_tensor_tensor(out=y[u][:], in0=y[u][:], scalar=sm_scale[:, ct:ct + 1], in1=e[:],
                                               op0=ALU.mult, op1=ALU.mult).then_inc(smooth_ok, 1)

            def gate_sums():
                st = gates
                st.mark(nc.vector.memset(zero[:], 0.0))
                st.mark(nc.vector.memset(m_out[0][:], 0.0))
                st.mark(nc.vector.memset(m_out[1][:], 0.0))
                dve.wait_ge(g_in, (L + 1) * NIN * DMA)
                for d in range(2):
                    st.mark(nc.vector.tensor_scalar(mn[d][:], gf[d][:], bias[:, 2 * d + 1:2 * d + 2], 0.0, ALU.add, ALU.min))
                dve.wait_ge(sa, L * NA + NA1)
                for d in range(2):
                    st.join()
                    st.mark(nc.vector.tensor_tensor(mn[d][:], mn[d][:], ge[d][:], ALU.subtract))
                st.join()
                for d in range(2):
                    st.mark(nc.vector.tensor_tensor_scan(flow(b, d), flow(mn, d), zero[:], 0.0, ALU.add, ALU.add))
                st.join()
                for d in range(2):
                    st.mark(nc.vector.scalar_tensor_tensor(out=a_[d][:], in0=gi[d][:], scalar=bias[:, 2 * d:2 * d + 1],
                                                           in1=b[d][:], op0=ALU.add, op1=ALU.subtract))
                st.join()
                nc.vector.tensor_copy(ends[0][:, 1:2], ends_of(b, 0))
                nc.vector.tensor_copy(ends[1][:, 1:2], ends_of(b, 1))
                st.mark(nc.vector.tensor_reduce(ends[0][:, 0:1], a_[0][:], AX.X, ALU.max))
                st.mark(nc.vector.tensor_reduce(ends[1][:, 0:1], a_[1][:], AX.X, ALU.max))
                st.mark(nc.vector.memset(n_end[0][:], 0.0))
                assert st.n == NV1, st.n

            def gate_stabilisers():
                st = gates
                dve.wait_ge(hop, (L * 8 + 4) * DMA)

                def run(d, out_, in_):
                    st.mark(nc.vector.tensor_tensor_scan(m_out[d][:, out_], m_in[d][:, in_, 0], m_in[d][:, in_, 1], 0.0,
                                                         ALU.max, ALU.add))

                run(0, slice(1, NTP), slice(0, NTP - 1))
                run(0, slice(NTP + 1, NT), slice(NTP, NT - 1))
                run(1, slice(0, NTP - 1), slice(1, NTP))
                run(1, slice(NT - 2, NTP - 1, -1), slice(NT - 1, NTP, -1))
                st.mark(nc.vector.memset(n_end[1][:], 0.0))
                st.mark(nc.vector.memset(n_end[0][:], 0.0))
                assert st.n == NV2, st.n

            def gate_maxima():
                st = gates
                dve.wait_ge(hop, (L + 1) * 8 * DMA)
                for d in range(2):
                    st.mark(nc.vector.tensor_tensor_scan(flow(M, d), flow(a_, d), zero[:], m_col[d][:, 0:1], ALU.max, ALU.add))
                st.join()
                for d in range(2):
                    st.mark(nc.vector.tensor_tensor(bm[d][:], b[d][:], M[d][:], ALU.add))
                    st.mark(nc.vector.tensor_scalar(n_end[d][:, 0:1], ends_of(M, d), -1.0, None, ALU.mult))
                for d in range(2):
                    st.mark(nc.vector.tensor_scalar(n_end[d][:, 1:2], ends_of(M, d), -1.0, None, ALU.mult))

            def gate_carries():
                st = gates
                dve.wait_ge(sa, L * NA + NA)
                for d in range(2):
                    st.mark(nc.vector.tensor_scalar(wi[d][:], wi[d][:], carries[:, d:d + 1], None, ALU.mult))
                    st.mark(nc.vector.tensor_scalar(dec[d][:], dec[d][:], carries[:, d:d + 1], None, ALU.mult))
                assert st.n == NV3, st.n

            dve.wait_ge(const_in, consts_value(L, "prepare"))
            nc.vector.tensor_tensor(gain[:], gain[:], scale[:], ALU.mult).then_inc(gain_ok, 1)
            dve.wait_ge(gain_ok, L + 1)
            for j in range(NJ):
                if j == 1:
                    gate_stabilisers()
                if j == 2:
                    gate_maxima()
                outer_taps(j)
                if j == 0:
                    gate_sums()
                copy_turned(dve, nc.vector.tensor_copy, 1, turns_of(j)[0])
                normalise(j, 0)
                normalise(j, 1)
                add_turn(j, 0)
                log_sigmoid(j)
                add_turn(j, 1)
                if j == 2:
                    gate_carries()
                low_part(j, 0)
                low_part(j, 1)
                gated(j)
                copy_turned(dve, nc.vector.tensor_copy, 1, turns_of(j)[1])

        @block.gpsimd
        def _(pool):
            pool.wait_ge(table_in, (L + 1) * 2 * DMA)
            for j in range(NJ):
                for u, (a, z) in enumerate(PIECES):
                    pool.wait_ge(qn_ok, item(j, u) + 1)
                    if j:
                        pool.wait_ge(lo_ok, item(j - 1, u) + 1)
                    nc.gpsimd.tensor_tensor(t1[u][:], qn[u][:], cos[:, a:z], ALU.mult).then_inc(t1_ok, 1)

        @block.tensor
        def _(pe):
            def each_512(u, out, weights, src):
                m = PIECES[u][1] - PIECES[u][0]
                for c in range(0, m, 512):
                    mm = pe.matmul(out[:, c:min(c + 512, m)], weights[:], src[u][:, c:min(c + 512, m)], start=True, stop=True)
                return mm

            def sum_squares(j, u):
                n = item(j, u)
                pe.wait_ge(sq_ok, n + 1)
                if j or u:
                    pe.wait_ge(ln_ok, n)
                each_512(u, ss, blk, sq).then_inc(ss_ok, 1)

            def swap_halves(j, u):
                n = item(j, u)
                pe.wait_ge(qn_ok, n + 1)
                if j or u:
                    pe.wait_ge(rs_sin_ok, n)
                each_512(u, rx, rot, qn).then_inc(rx_ok, 1)

            def turn(i):
                if i is None:
                    return
                _, how, src = TURNS[i]
                if how == "load":
                    w = [t for t, (_, h, _) in enumerate(TURNS) if h == "load"].index(i)
                    pe.wait_ge(tv_in[w % 2], (L * (2 - w % 2) + w // 2 + 1) * DMA)
                    tile_src = tv[w % 2]
                else:
                    pe.wait_ge(smooth_ok, L * NJ + src + 1)
                    tile_src = y[src % 2]
                for g, tile, n in groups(i):
                    if g >= 2:
                        pe.wait_ge((tr_act, tr_dve)[g % 2], L * (TRA, TRD)[g % 2] + g // 2)
                    for t in range(n):
                        mm = pe.transpose(tr[g % 2][:, t, :], tile_src[:, (tile + t) * P:(tile + t + 1) * P], ident)
                    mm.then_inc(turned, 1)

            pe.wait_ge(const_in, consts_value(L, "prepare"))
            for j in range(NJ):
                sum_squares(j, 0)
                sum_squares(j, 1)
                turn(turns_of(j)[0])
                swap_halves(j, 0)
                swap_halves(j, 1)
                turn(turns_of(j)[1])
            pe.wait_ge(sv, (L + 1) * NV)
            pe.wait_ge(tr_act, (L + 1) * TRA)
            pe.wait_ge(tr_dve, (L + 1) * TRD)
            for d in range(2):
                for i, t in enumerate((a_, wi, em, kws)):
                    mm = pe.transpose(tr[d][:, i, 0:GR], t[d][:], ident[0:GR, 0:GR])
                mm.then_inc(g_turned, 1)


def attend_gqa(k, L, ident, cols, zeros):
    nc = k.nc
    phases = k.sem("phases_stored")
    NKT = DEC_SEQ // P
    MAX_AT = 5
    ROWS_AT = NKT - 2
    with ExitStack() as ctx:
        k_both = [sbuf(k, ctx, f"ga_kboth{g}", [P, TOK], F32R) for g in range(2)]
        k_one = [sbuf(k, ctx, f"ga_kone{g}", [P, TOK], F32R) for g in range(2)]
        v = pair(k, ctx, "ga_v", [P, NT, HD])
        v_hi = [sbuf(k, ctx, f"ga_vhi{g}", [P, NT, P], F32R) for g in range(2)]
        v_lo = [sbuf(k, ctx, f"ga_vlo{g}", [P, NT, P], F32R) for g in range(2)]
        q_hi2 = [sbuf(k, ctx, f"ga_qhi2{c}", [P, QC], F32R) for c in range(NQC)]
        q_lom = [sbuf(k, ctx, f"ga_qlom{c}", [P, QC], F32R) for c in range(NQC)]
        prob = pair(k, ctx, "ga_prob", [P, QC])
        p_hi = [sbuf(k, ctx, f"ga_phi{r}", [P, QC], F32R) for r in range(4)]
        p_lo = [sbuf(k, ctx, f"ga_plo{r}", [P, QC], F32R) for r in range(4)]
        mx = pair(k, ctx, "ga_mx", [P, 4, 4])
        nmax = pair(k, ctx, "ga_nmax", [P, 4])
        rden = pair(k, ctx, "ga_rden", [HD, QC])
        o_t = pair(k, ctx, "ga_o", [HD, QC])
        ps_s = [psum(k, ctx, f"ga_ps_s{r}", [P, QC]) for r in range(2)]
        ps_x = [psum(k, ctx, f"ga_ps_x{r}", [P, QC]) for r in range(2)]
        ps_o = [psum(k, ctx, f"ga_ps_o{r}", [P, QC]) for r in range(2)]
        ps_m = psum(k, ctx, "ga_ps_m", [P, QC])
        fill, fill_q, kv_in, kone_in, v_in, vhi_ok, vlo_ok = (
            k.sem("ga_" + s) for s in ("fill", "fill_q", "kv_in", "kone_in", "v_in", "vhi_ok", "vlo_ok"))
        q_in = [k.sem(f"ga_q_in{c}") for c in range(NQC)]
        stored = [k.sem(f"stored{u}") for u in range(2)]
        (scored, phi_ok, exped, plo_pool, plo_dve, pv_done, max_done, max_read, nmax_ok, row_done, row_ok, rden_ok, o_ok) = (
            k.sem("ga_" + s) for s in ("scored", "phi_ok", "exped", "plo_pool", "plo_dve", "pv_done", "max_done",
                                       "max_read", "nmax_ok", "row_done", "row_ok", "rden_ok", "o_ok"))
        block = ctx.enter_context(nc.Block())
        SAMPLE = GQ_HEADS * NQC
        ITEMS = SAMPLE + GQ_HEADS
        TILES = SAMPLE * NKT + GQ_HEADS * NTP
        USES = [GQ_HEADS + len(range(c, GQ_HEADS, NQC)) for c in range(NQC)]
        NFILL = 4 * KV_HEADS
        POOL_LO, DVE_LO = NKT - NKT // 4, NKT // 4
        POOL_ALL, DVE_ALL = SAMPLE * POOL_LO + GQ_HEADS * NTP, SAMPLE * DVE_LO

        def item_no(i):
            return L * ITEMS + i

        def tile_no(i):
            return L * TILES + i * NKT

        def prompt_tile_no(p):
            return L * TILES + SAMPLE * NKT + p * NTP

        def low_made(i, kt):
            if kt < 0:
                return (plo_pool, L * POOL_ALL + i * POOL_LO + 1) if kt == -2 else (plo_dve, L * DVE_ALL + i * DVE_LO + 1)
            if kt % 4 == 3:
                return plo_dve, L * DVE_ALL + i * DVE_LO + (kt // 4 + 1) + 1
            return plo_pool, L * POOL_ALL + i * POOL_LO + (kt - kt // 4 + 1) + 1

        def prompt_low_made(p, kt):
            if p < 0:
                return low_made(SAMPLE, kt - 2)
            return plo_pool, L * POOL_ALL + SAMPLE * POOL_LO + p * NTP + kt + 1 + 1

        @block.sync
        def _(sp):
            def load_k(g, half, name, dst, sem):
                sp.dma_start(dst[g][half * HD:(half + 1) * HD, :].bitcast(F32), k.a[name][3, g * HD:(g + 1) * HD, :]).then_inc(sem, DMA)

            def load(h, c, a, w):
                hi, lo = (k.a[x].rearrange("c (h d) t -> (c h) d t", d=HD)[at(h)].rearrange("a d t -> (a d) t")[:, a:a + w]
                          for x in ("gqk_hi", "gqk_lo"))
                for dst, src in ((q_hi2[c][0:HD, 0:w], hi), (q_hi2[c][HD:P, 0:w], hi), (q_lom[c][0:HD, 0:w], lo)):
                    sp.dma_start(dst.bitcast(F32), src).then_inc(q_in[c], DMA)

            def store(i, u, rows, a, w):
                sp.wait_ge(o_ok, item_no(i) + 1 + 2)
                sp.dma_start(rows[:, a:a + w], o_t[u][:, 0:w]).then_inc(stored[u], DMA)

            def store_head(h, c):
                store(h * NQC + c, c % 2, k.a["gqo"][at(h)].rearrange("a d t -> (a d) t"), SEQ + c * QC, QC)

            for g in range(2):
                load_k(g, 0, "gqk_hi", k_both, kv_in)
                load_k(g, 1, "gqk_lo", k_both, kv_in)
                if g == 0:
                    load(0, 0, SEQ, QC)
            for g in range(2):
                load_k(g, 0, "gqk_hi", k_one, kone_in)
            for g in range(2):
                v_cols = slice(4 * P + g * HD, 4 * P + (g + 1) * HD)
                sp.dma_start(v[g][:], k.a["tokmaj"][:, v_cols].rearrange("(n p) d -> p n d", p=P)).then_inc(v_in, DMA)
            for c in range(1, NQC):
                load(0, c, SEQ + c * QC, QC)
            with sp.Fori(1, GQ_HEADS) as h:
                for c in range(NQC):
                    sp.wait_ge(pv_done, tile_no(h * NQC + c - NQC + 1) + 4)
                    load(h, c, SEQ + c * QC, QC)
                    store_head(h - 1, c)
            for p in range(GQ_HEADS):
                sp.wait_ge(pv_done, (tile_no(SAMPLE + p - NQC + 1) if p < NQC else prompt_tile_no(p - NQC + 1)) + 4)
                load(p, p % NQC, 0, SEQ)
                if p < NQC:
                    store_head(GQ_HEADS - 1, p)
                else:
                    store(SAMPLE + p - NQC, p % 2, k.a["gqo"][p - NQC], 0, SEQ)
            for p in range(GQ_HEADS - NQC, GQ_HEADS):
                store(SAMPLE + p, p % 2, k.a["gqo"][p], 0, SEQ)
            for u in range(2):
                sp.wait_ge(stored[u], stored_value(L, "gqa", u, ITEMS // 2))
            sp.sem_inc(phases, 1)

        @block.tensor
        def _(pe):
            pe.wait_ge(kv_in, (L + 1) * 4 * DMA)

            def max_product(g, c, q, key0, w, m, r):
                pe.wait_ge(max_read, m + 1)
                pe.matmul(ps_x[r][:, 0:w], q_hi2[c][:, q * P:(q + 1) * P], k_both[g][:, key0:key0 + w],
                          start=True, stop=True).then_inc(max_done, 1)

            def sample_max(g, c, i, n, loads):
                if n == 0:
                    pe.wait_ge(q_in[c], (L * USES[c] + loads) * 3 * DMA)
                max_product(g, c, n // 4, SEQ + (n % 4) * QC, QC, tile_no(i) + n, n % 2)

            def prompt_max(p, n):
                g, c = p // GQ_PER_KV, p % NQC
                if n == 0:
                    pe.wait_ge(q_in[c], (L * USES[c] + GQ_HEADS + p // NQC + 1) * 3 * DMA)
                max_product(g, c, n, 0, SEQ, prompt_tile_no(p) + n, n % 2)

            def max_rows(u, nq, i):
                pe.wait_ge(nmax_ok, item_no(i) + 1)
                for q in range(nq):
                    mm = pe.matmul(ps_m[HD:HD + 1, q * P:(q + 1) * P], nmax[u][:, q:q + 1], ident, start=True, stop=True)
                mm.then_inc(row_done, 1)

            def scores(g, c, t, kt, w, r, i, first):
                pe.wait_ge(exped, t + 1)
                tile = slice(kt * P, (kt + 1) * P)
                pe.matmul(ps_s[r][:, 0:w], k_both[g][:, tile], q_hi2[c][:, 0:w], start=True, stop=False)
                if first:
                    pe.wait_ge(row_ok, item_no(i) + 1)
                pe.matmul(ps_s[r][:, 0:w], k_one[g][:, tile], q_lom[c][:, 0:w], start=False, stop=True).then_inc(scored, 1)

            def weigh(g, u, i, t, kt, w, r, low, first, last):
                if first:
                    pe.wait_ge(o_ok, item_no(i) + 1)
                pe.wait_ge(phi_ok, t + 1)
                pe.matmul(ps_o[u][:, 0:w], v_hi[g][:, kt, :], p_hi[r][:, 0:w], start=first, stop=False)
                pe.matmul(ps_o[u][:, 0:w], v_lo[g][:, kt, :], p_hi[r][:, 0:w], start=False, stop=False)
                pe.wait_ge(*low)
                pe.matmul(ps_o[u][:, 0:w], v_hi[g][:, kt, :], p_lo[r][:, 0:w], start=False, stop=last).then_inc(pv_done, 1)

            def sample_weigh(g, c, i, kt):
                weigh(g, c % 2, i, tile_no(i) + kt, NTP + kt, QC, kt % 4, low_made(i, kt), kt == 0, kt == NKT - 1)

            def head(g, hh, last):
                for c in range(NQC):
                    i = (g * GQ_PER_KV + hh) * NQC + c
                    cn, next_prompt = (c + 1) % NQC, last and c == NQC - 1 and g == KV_HEADS - 1
                    gn = g + 1 if last and c == NQC - 1 else g
                    loads = g * GQ_PER_KV + hh + (c == NQC - 1) + 1
                    for kt in range(NKT):
                        scores(g, c, tile_no(i) + kt, NTP + kt, QC, kt % 2, i, kt == 0)
                        for n in range((kt - MAX_AT) * 2, (kt - MAX_AT) * 2 + 2):
                            if next_prompt and 0 <= n < NTP:
                                prompt_max(0, n)
                            elif not next_prompt and 0 <= n < NKT:
                                sample_max(gn, cn, i + 1, n, loads)
                        if kt >= 2:
                            sample_weigh(g, c, i, kt - 2)
                        elif c:
                            sample_weigh(g, c - 1, i - 1, NKT - 2 + kt)
                        if kt == ROWS_AT:
                            max_rows(cn % 2, NTP if next_prompt else 4, i + 1)
                for kt in range(NKT - 2, NKT):
                    sample_weigh(g, NQC - 1, (g * GQ_PER_KV + hh) * NQC + (NQC - 1), kt)

            for n in range(NKT):
                sample_max(0, 0, 0, n, 1)
            pe.wait_ge(kone_in, (L + 1) * 2 * DMA)
            pe.wait_ge(fill, (L + 1) * NFILL)
            pe.wait_ge(vlo_ok, (L + 1) * 2)
            max_rows(0, 4, 0)
            for g in range(KV_HEADS):
                with pe.Fori(0, GQ_PER_KV - 1) as hh:
                    head(g, hh, False)
                head(g, GQ_PER_KV - 1, True)
            for p in range(GQ_HEADS):
                g, c, t0 = p // GQ_PER_KV, p % NQC, prompt_tile_no(p)
                for kt in range(NTP):
                    scores(g, c, t0 + kt, kt, SEQ, kt, SAMPLE + p, kt == 0)
                if p + 1 < GQ_HEADS:
                    for n in range(NTP):
                        prompt_max(p + 1, n)
                    max_rows((p + 1) % 2, NTP, SAMPLE + p + 1)
                for kt in range(NTP):
                    weigh(g, c % 2, SAMPLE + p, t0 + kt, kt, SEQ, kt, prompt_low_made(p, kt), kt == 0, kt == NTP - 1)

        @block.scalar
        def _(act):
            def exp_tile(t, w, kt, low, free):
                act.wait_ge(scored, t + 1)
                act.wait_ge(pv_done, free)
                nc.scalar.activation(p_hi[kt % 4][:, 0:w], ps_s[kt % 2][:, 0:w], ACT.Exp).then_inc(phi_ok, 1)
                act.wait_ge(*low)
                nc.scalar.activation(prob[kt % 2][:, 0:w], ps_s[kt % 2][:, 0:w], ACT.Exp).then_inc(exped, 1)

            def row(c, i, w):
                act.wait_ge(row_done, item_no(i) + 1)
                nc.scalar.copy(q_lom[c][HD:HD + 1, 0:w], ps_m[HD:HD + 1, 0:w]).then_inc(row_ok, 1)

            def head(g, hh, last):
                for c in range(NQC):
                    i = (g * GQ_PER_KV + hh) * NQC + c
                    for kt in range(NKT):
                        t = tile_no(i) + kt
                        exp_tile(t, QC, kt, low_made(i, kt - 2), t + 1)
                        if kt == ROWS_AT:
                            row((c + 1) % NQC, i + 1, SEQ if last and c == NQC - 1 and g == KV_HEADS - 1 else QC)

            st = Steps(act, fill, L * NFILL)
            one = cols["one"]
            for g in range(KV_HEADS):
                st.mark(nc.scalar.copy(k_one[g][HD:P, :].rearrange("p (n t) -> p n t", t=SIDE),
                                       zeros[HD:P, :].unsqueeze(1).to_broadcast([P - HD, TOK // SIDE, SIDE])))
                st.join()
                st.mark(nc.scalar.copy(k_one[g][HD:HD + 1, :], one[HD:HD + 1, :].to_broadcast([1, TOK])))
                st.mark(nc.scalar.copy(v_hi[g][:, :, HD:P], one.unsqueeze(1).to_broadcast([P, NT, P - HD])))
                st.mark(nc.scalar.copy(v_lo[g][:, :, HD:P], zeros[:, :].unsqueeze(1).to_broadcast([P, NT, P - HD])))
            act.wait_ge(v_in, (L + 1) * 2 * DMA)
            for g in range(2):
                nc.scalar.copy(v_hi[g][:, :, 0:HD], v[g][:]).then_inc(vhi_ok, 1)
            act.wait_ge(fill_q, (L + 1) * NQC)
            row(0, 0, QC)
            for g in range(KV_HEADS):
                with act.Fori(0, GQ_PER_KV - 1) as hh:
                    head(g, hh, False)
                head(g, GQ_PER_KV - 1, True)
            for p in range(GQ_HEADS):
                for kt in range(NTP):
                    t = prompt_tile_no(p) + kt
                    exp_tile(t, SEQ, kt, prompt_low_made(p - 1, kt), t + 1 + 2)
                if p + 1 < GQ_HEADS:
                    row((p + 1) % NQC, SAMPLE + p + 1, SEQ)

        def low_half(engine, vector, t, w, kt, free, sem):
            engine.wait_ge(exped, t + 1 + 2)
            engine.wait_ge(pv_done, free)
            vector.tensor_tensor(p_lo[kt % 4][:, 0:w], prob[kt % 2][:, 0:w], p_hi[kt % 4][:, 0:w].bitcast(F32),
                                 ALU.subtract).then_inc(sem, 1)

        @block.gpsimd
        def _(pool):
            with pool.Fori(0, SAMPLE) as i:
                for kt in range(NKT):
                    if kt % 4 != 3:
                        t = tile_no(i) + kt
                        low_half(pool, nc.gpsimd, t, QC, kt, t + 1, plo_pool)
            for p in range(GQ_HEADS):
                for kt in range(NTP):
                    t = prompt_tile_no(p) + kt
                    low_half(pool, nc.gpsimd, t, SEQ, kt, t + 1 + 2, plo_pool)

        @block.vector
        def _(dve):
            def maximum(u, t0, nk, w, n):
                dve.wait_ge(max_done, t0 + n + 1)
                nc.vector.tensor_reduce(mx[u][:, n // nk, n % nk:n % nk + 1], ps_x[n % 2][:, 0:w], AX.X,
                                        ALU.max).then_inc(max_read, 1)

            def negated(u, t0, nq, nk):
                dve.wait_ge(max_read, t0 + nq * nk + 2)
                nc.vector.tensor_reduce(nmax[u][:, 0:nq], mx[u][:, 0:nq, 0:nk], AX.X, ALU.max,
                                        negate=True).then_inc(nmax_ok, 1)

            def output(u, i, t_end, w, stored_before):
                dve.wait_ge(pv_done, t_end + 4)
                dve.wait_ge(o_ok, item_no(i) + 1)
                nc.vector.reciprocal(rden[u][:, 0:w], ps_o[u][HD:P, 0:w]).then_inc(rden_ok, 1)
                dve.wait_ge(rden_ok, item_no(i) + 1)
                dve.wait_ge(stored[u], stored_value(L, "gqa", u, stored_before))
                nc.vector.tensor_tensor(o_t[u][:, 0:w], ps_o[u][0:HD, 0:w], rden[u][:, 0:w], ALU.mult).then_inc(o_ok, 1)

            def sample_output(g, hh, c):
                i = (g * GQ_PER_KV + hh) * NQC + c
                output(c % 2, i, tile_no(i + 1), QC, (g * GQ_PER_KV + hh) * 2 + c // 2)

            def head(g, hh, last):
                for c in range(NQC):
                    i, un = (g * GQ_PER_KV + hh) * NQC + c, (c + 1) % 2
                    next_prompt = last and c == NQC - 1 and g == KV_HEADS - 1
                    nq, nk, w = (NTP, 1, SEQ) if next_prompt else (4, 4, QC)
                    if c:
                        sample_output(g, hh, c - 1)
                    for kt in range(2, NKT):
                        if kt % 4 == 0:
                            t = tile_no(i) + kt - 1
                            low_half(dve, nc.vector, t, QC, kt - 1, t + 1, plo_dve)
                        for n in range((kt - MAX_AT) * 2, (kt - MAX_AT) * 2 + 2):
                            if 0 <= n < nq * nk:
                                maximum(un, tile_no(i + 1), nk, w, n)
                                if n == nq * nk - 1:
                                    negated(un, tile_no(i + 1), nq, nk)
                    t = tile_no(i) + NKT - 1
                    low_half(dve, nc.vector, t, QC, NKT - 1, t + 1, plo_dve)
                sample_output(g, hh, NQC - 1)

            for c in range(NQC):
                nc.vector.memset(q_lom[c][HD:P, :].bitcast(F32), 0.0).then_inc(fill_q, 1)
            for n in range(NKT):
                maximum(0, tile_no(0), 4, QC, n)
            negated(0, tile_no(0), 4, 4)
            for g in range(KV_HEADS):
                dve.wait_ge(vhi_ok, L * 2 + g + 1)
                nc.vector.tensor_tensor(v_lo[g][:, :, 0:HD], v[g][:], v_hi[g][:, :, 0:HD].bitcast(F32), ALU.subtract).then_inc(vlo_ok, 1)
            for g in range(KV_HEADS):
                with dve.Fori(0, GQ_PER_KV - 1) as hh:
                    head(g, hh, False)
                head(g, GQ_PER_KV - 1, True)
            for p in range(GQ_HEADS):
                if p + 1 < GQ_HEADS:
                    for n in range(NTP):
                        maximum((p + 1) % 2, prompt_tile_no(p + 1), 1, SEQ, n)
                    negated((p + 1) % 2, prompt_tile_no(p + 1), NTP, 1)
                output(p % 2, SAMPLE + p, prompt_tile_no(p + 1), SEQ, SAMPLE // 2 + p // 2)


def mlstm(k, L, gate_cols, decay):
    nc = k.nc
    phases = k.sem("phases_stored")
    NU = 3
    NB = NT // NU
    with ExitStack() as ctx:
        def six(name, shape):
            return [[sbuf(k, ctx, f"ml_{name}{u}{d}", shape) for d in range(2)] for u in range(NU)]

        qk, kv, mb = six("qk", [P, 6, P]), six("kv", [P, 2 * MH, HD + 1]), six("mb", [P, MH, P])
        h_out, at_, kw = six("h", [P, MH, HD]), six("at", [P, MH, P]), six("kw", [P, MH, HD])
        arg, w, nd, den = (pair(k, ctx, "ml_" + x, s) for x, s in (
            ("arg", [P, MH, P]), ("w", [P, MH, P]), ("nd", [P, MH, HD + 1]), ("den", [P, MH])))
        state = pair(k, ctx, "ml_state", [P, 2, HD + 1])
        causal = sbuf(k, ctx, "ml_causal", [P, 2, P])
        ps_s = [psum(k, ctx, f"ml_ps_s{d}", [P, MH, P]) for d in range(2)]
        ps_i = [psum(k, ctx, f"ml_ps_i{d}", [P, 512]) for d in range(2)]
        ps_n = [psum(k, ctx, f"ml_ps_n{d}", [P, 512]) for d in range(2)]
        ps_c = [psum(k, ctx, f"ml_ps_c{d}", [P, 512]) for d in range(2)]
        loaded = [[k.sem(f"ml_loaded{u}{d}") for d in range(2)] for u in range(NU)]
        stored = [[k.sem(f"ml_stored{u}{d}") for d in range(2)] for u in range(NU)]
        const_in = k.sem("consts_in")
        fill, arg_ok, w_ok, s_ok, at_ok, kw_ok, mm_ok, chain, h_ok, state_ok, nd_ok = (
            k.sem("ml_" + s) for s in ("fill", "arg_ok", "w_ok", "s_ok", "at_ok", "kw_ok", "mm_ok", "chain",
                                       "h_ok", "state_ok", "nd_ok"))
        block = ctx.enter_context(nc.Block())
        W = HD + 1
        NFILL = 2 + 2 * NU
        NLOAD = 3

        def chunk(b, u, d):
            return b * NU + u if d == 0 else b * -NU + (NT - 1 - u)

        def number(b, u, d):
            return (L * NB + b) * (2 * NU) + u * 2 + d

        def gate(which, d, c):
            t = gate_cols[:, d * 4 + which, :].rearrange("p (h c) -> p h c", c=NT)
            return t[:, :, at(c)].rearrange("p h x -> p (h x)")

        def heads(ps):
            return ps[:, 0:MH * W].rearrange("p (h e) -> p h e", e=W)

        def slots(engine, early, late):
            early(0, 0)
            with engine.Fori(0, NB - 1) as b:
                for u in range(NU):
                    early(b + (u + 1) // NU, (u + 1) % NU)
                    late(b, u)
            for u in range(NU):
                if u + 1 < NU:
                    early(NB - 1, u + 1)
                late(NB - 1, u)

        @block.sync
        def _(sp):
            sp.dma_start(causal[:], k.a["causal"]).then_inc(const_in, DMA)

            def loads(b, u):
                for d in range(2):
                    c = chunk(b, u, d)
                    sp.wait_ge(mm_ok, number(b, u, d) + 1)
                    tok, s = at(c * P, P), loaded[u][d]
                    sp.dma_start(qk[u][d][:], k.a["mqk"][:, :, tok].rearrange("c p t -> p c t")).then_inc(s, DMA)
                    M = k.a["gate_M"][d].rearrange("(h c) l -> c h l", c=NT)[at(c)].rearrange("c h l -> (c h) l")
                    sp.dma_start(mb[u][d][:], M.partition_broadcast(P)).then_inc(s, DMA)
                    sp.dma_start(kv[u][d][:, :, 0:HD],
                                 k.a["tokmaj"][tok, 0:2 * MH * HD].rearrange("t (h e) -> t h e", e=HD)).then_inc(s, DMA)

            def stores(b, u):
                for d in range(2):
                    sp.wait_ge(h_ok, number(b, u, d) + 1)
                    sp.dma_start(rows_of(k.a["mh"][d], chunk(b, u, d) * P, P, 0, MH * HD),
                                 h_out[u][d][:].rearrange("p h e -> p (h e)")).then_inc(stored[u][d], DMA)

            for u in range(NU):
                loads(0, u)
            with sp.Fori(0, NB - 1) as b:
                for u in range(NU):
                    loads(b + 1, u)
                    stores(b, u)
            for u in range(NU):
                stores(NB - 1, u)
            for u in range(NU):
                for d in range(2):
                    sp.wait_ge(stored[u][d], (L + 1) * NB * DMA + DMA)
            sp.sem_inc(phases, 1)

        @block.gpsimd
        def _(pool):
            with pool.Fori(0, NB) as b:
                pool.wait_ge(const_in, consts_value(L, "mlstm"))
                for u in range(NU):
                    for d in range(2):
                        m = number(b, u, d)
                        pool.wait_ge(loaded[u][d], (L * NB + b + 1) * NLOAD * DMA)
                        pool.wait_ge(w_ok, m + 1)
                        mask = causal[:, d, :].unsqueeze(1).to_broadcast([P, MH, P])
                        nc.gpsimd.tensor_tensor(arg[d][:], mask, mb[u][d][:], ALU.subtract).then_inc(arg_ok, 1)
                        pool.wait_ge(mm_ok, m + 1)
                        nc.gpsimd.tensor_tensor(kw[u][d][:], kv[u][d][:, 0:MH, 0:HD], bc_free(gate(3, d, chunk(b, u, d)), HD),
                                                ALU.mult).then_inc(kw_ok, 1)

        @block.scalar
        def _(act):
            with act.Fori(0, NB) as b:
                for u in range(NU):
                    for d in range(2):
                        m = number(b, u, d)
                        act.wait_ge(arg_ok, m + 1)
                        act.wait_ge(at_ok, m + 1)
                        a = gate_cols[:, d * 4, :]
                        for h in range(MH):
                            ins = nc.scalar.activation(w[d][:, h, :], arg[d][:, h, :], ACT.Exp,
                                                       bias=a[:, at(chunk(b, u, d) + h * NT)])
                        ins.then_inc(w_ok, 1)

        @block.vector
        def _(dve):
            for d in range(2):
                nc.vector.memset(state[d][:], 0.0).then_inc(fill, 1)
                for u in range(NU):
                    nc.vector.memset(kv[u][d][:, MH:, HD:W], 1.0).then_inc(fill, 1)
            dve.wait_ge(fill, (L + 1) * NFILL)

            def weigh_scores(b, u):
                for d in range(2):
                    m = number(b, u, d)
                    dve.wait_ge(w_ok, m + 1 + 2)
                    dve.wait_ge(s_ok, m + 1)
                    dve.wait_ge(mm_ok, m + 1)
                    nc.vector.tensor_tensor(at_[u][d][:], w[d][:], ps_s[d][:], ALU.mult).then_inc(at_ok, 1)

            def outputs(b, u):
                for d in range(2):
                    m, c = number(b, u, d), chunk(b, u, d)
                    st = Steps(dve, chain, m * 4)
                    dve.wait_ge(mm_ok, m + 1 + 2 * NU)
                    st.mark(nc.vector.tensor_tensor(nd[d][:], heads(ps_i[d]), bc_free(gate(1, d, c), W), ALU.mult))
                    for pr in range(2):
                        for e in range(2):
                            rows = slice(e * HD, (e + 1) * HD)
                            ins = nc.vector.scalar_tensor_tensor(
                                out=state[d][rows, pr, :], in0=state[d][rows, pr, :], scalar=decay[rows, d, pr, at(c)],
                                in1=heads(ps_c[d])[rows, pr * 2 + e, :], op0=ALU.mult, op1=ALU.add)
                    ins.then_inc(state_ok, 1)
                    st.join()
                    nc.vector.tensor_tensor(nd[d][:], nd[d][:], heads(ps_n[d]), ALU.add).then_inc(nd_ok, 1)
                    dve.wait_ge(nd_ok, m + 1 + 2)
                    dcol = nd[d][:, :, HD:W].rearrange("p h x -> p (h x)")
                    st.mark(nc.vector.scalar_tensor_tensor(out=den[d][:], in0=dcol, scalar=-1.0, in1=dcol,
                                                           op0=ALU.mult, op1=ALU.max))
                    st.join()
                    st.mark(nc.vector.tensor_tensor(den[d][:], den[d][:], gate(2, d, c), ALU.max))
                    st.join()
                    st.mark(nc.vector.reciprocal(den[d][:], den[d][:]))
                    st.join()
                    dve.wait_ge(stored[u][d], (L * NB + b) * DMA + DMA)
                    nc.vector.tensor_tensor(h_out[u][d][:], nd[d][:, :, 0:HD], bc_free(den[d][:], HD),
                                            ALU.mult).then_inc(h_ok, 1)

            slots(dve, weigh_scores, outputs)

        @block.tensor
        def _(pe):
            pe.wait_ge(fill, (L + 1) * NFILL)

            def scores(b, u):
                for d in range(2):
                    m = number(b, u, d)
                    pe.wait_ge(loaded[u][d], (L * NB + b + 1) * NLOAD * DMA)
                    pe.wait_ge(at_ok, m + 1)
                    for pr in range(2):
                        mm = pe.matmul(ps_s[d][:, pr * 2:pr * 2 + 2, :], qk[u][d][:, 4 + pr, :], qk[u][d][:, pr * 2:pr * 2 + 2, :],
                                       start=True, stop=True)
                    mm.then_inc(s_ok, 1)

            def products(b, u):
                for d in range(2):
                    m = number(b, u, d)
                    pe.wait_ge(state_ok, m + 1)
                    for h in range(MH):
                        pe.matmul(ps_i[d][:, h * W:(h + 1) * W], qk[u][d][:, h, :], state[d][:, h // 2, :],
                                  start=True, stop=True)
                    pe.wait_ge(kw_ok, m + 1)
                    for h in range(MH):
                        both = kw[u][d][:, h // 2 * 2:h // 2 * 2 + 2, :].rearrange("p e f -> p (e f)")
                        pe.matmul(ps_c[d][:, h * W:(h + 1) * W], both, kv[u][d][:, MH + h, :], start=True, stop=True)
                    pe.wait_ge(at_ok, m + 1 + 2)
                    pe.wait_ge(nd_ok, m + 1)
                    for h in range(MH):
                        mm = pe.matmul(ps_n[d][:, h * W:(h + 1) * W], at_[u][d][:, h, :], kv[u][d][:, MH + h, :], start=True, stop=True)
                    mm.then_inc(mm_ok, 1)

            slots(pe, scores, products)


KW = P + 2 * SIDE


def attend_dilated(k, L, ident, w_hi, w_lo):
    nc = k.nc
    phases = k.sem("phases_stored")
    NBLK = NG * NT
    with ExitStack() as ctx:
        q, kv, dist = (pair(k, ctx, "dl_" + x, s) for x, s in (
            ("q", [P, 2, P]), ("kv", [P, 2, KW]), ("dist", [P, KW + 2])))
        v_t, sb_, pr, pt = (pair(k, ctx, "dl_" + x, s) for x, s in (
            ("v_t", [P, 2, P]), ("s", [P, 2, KW]), ("p", [P, 2, KW]), ("pt", [P, 4, P])))
        nmax, den, lnd, out = (pair(k, ctx, "dl_" + x, s) for x, s in (
            ("nmax", [P, 2]), ("den", [P, 4]), ("lnd", [P, 2]), ("out", [P, 2, HD + 1])))
        ps_s = [psum(k, ctx, f"dl_ps_s{u}", [P, 2, KW]) for u in range(2)]
        ps_v = [psum(k, ctx, f"dl_ps_v{u}", [P, 4, P]) for u in range(2)]
        ps_t = [psum(k, ctx, f"dl_ps_t{u}", [P, 4, P]) for u in range(2)]
        ps_o = [psum(k, ctx, f"dl_ps_o{u}", [P, 512]) for u in range(2)]
        w_raw = sbuf(k, ctx, "dl_wraw", [P, KT, D_MODEL])
        w_in, whi_ok, wlo_ok = [k.sem(f"dl_w_in{i}") for i in range(2)], k.sem("dl_whi_ok"), k.sem("dl_wlo_ok")
        loaded = [k.sem(f"dl_loaded{u}") for u in range(2)]
        stored = [k.sem(f"stored{u}") for u in range(2)]
        s_ok, vt_ok, vc_ok, bias_ok, nmax_ok, p_ok, turned, pt_ok, pv_ok, ln_ok, lse_ok, chain, out_ok = (
            k.sem("dl_" + s) for s in ("s_ok", "vt_ok", "vc_ok", "bias_ok", "nmax_ok", "p_ok", "turned", "pt_ok",
                                       "pv_ok", "ln_ok", "lse_ok", "chain", "out_ok"))
        block = ctx.enter_context(nc.Block())

        def number(b, c):
            return L * NBLK + (b * 2 + c)

        def loads_before(b, c):
            return L * (NBLK // 2) + (b + c // 2)

        def exists(b, c):
            return not isinstance(b, int) or 0 <= c < NBLK

        SPLIT_AT = [NT // 2 + 2 + 2 * i for i in range(KT // 2)] + [NT + 2 * i + 1 for i in range(KT // 2)]

        def slots(engine, slot, split=None):
            for c in range(-2, 0):
                slot(0, c)
            stops = [0] + (SPLIT_AT if split else []) + [NBLK // 2 - 1]
            for t, (start, stop) in enumerate(zip(stops, stops[1:])):
                if t:
                    split(t - 1)
                with engine.Fori(start, stop) as b:
                    for v_ in range(2):
                        slot(b, v_)
            for c in range(NBLK - 2, NBLK):
                slot(0, c)

        @block.sync
        def _(sp):
            def loads(g, b, c, m):
                u, a, s = c % 2, (b * 2 + c) * P, loaded[c % 2]
                if m is not None:
                    past = m + 1
                    sp.wait_ge(bias_ok, past)
                    sp.wait_ge(vt_ok, past)
                sp.dma_start(q[u][:], k.a["dil_q"][g][:, :, at(a, P)].rearrange("h p t -> p h t")).then_inc(s, DMA)
                sp.dma_start(kv[u][:], k.a["dil_kv"][g][:, :, at(a, KW)].rearrange("c p t -> p c t")).then_inc(s, DMA)
                sp.dma_start(dist[u][:], k.a["dil_dist"][g][at(b * 2 + c)].rearrange("a p t -> (a p) t")).then_inc(s, DMA)

            def store(g, b, c, m):
                sp.wait_ge(out_ok, m + 3)
                sp.dma_start(rows_of(k.a["dil_out"][g], (b * 2 + c) * P, P, 0, 2 * (HD + 1)),
                             out[c % 2][:].rearrange("p h e -> p (h e)")).then_inc(stored[c % 2], DMA)

            for c in range(4):
                loads(0, 0, c, number(0, c) if c >= 2 else None)
            for g in range(NG):
                with sp.Fori(0, (NT - 4) // 2) as b:
                    for c in range(2):
                        loads(g, b, c + 4, number(b, g * NT + c + 4))
                        store(g, b, c, number(b, g * NT + c))
                for c in range(NT - 4, NT):
                    if g + 1 < NG:
                        t = g * (KT // 2) + c - (NT - 4)
                        sp.dma_start(w_raw[:, t, :], k.a["w_out"][at(L), t].rearrange("a p c -> p (a c)")).then_inc(w_in[g], DMA)
                        loads(g + 1, 0, c + 4 - NT, number(0, g * NT + c + 4))
                    store(g, 0, c, number(0, g * NT + c))
            for u in range(2):
                sp.wait_ge(stored[u], stored_value(L, "dilated", u, NBLK // 2))
            sp.sem_inc(phases, 1)

        @block.tensor
        def _(pe):
            def score(b, c):
                u, m = c % 2, number(b, c)
                pe.wait_ge(loaded[u], (loads_before(b, c) + 1) * 3 * DMA)
                pe.wait_ge(bias_ok, m + 1)
                for h in range(2):
                    mm = pe.matmul(ps_s[u][:, h, :], q[u][:, h, :], kv[u][:, 0, :], start=True, stop=True)
                mm.then_inc(s_ok, 1)

            def turn_v(b, c):
                u, m = c % 2, number(b, c)
                pe.wait_ge(vc_ok, m + 1)
                for i in range(2):
                    mm = pe.transpose(ps_v[u][:, i, :], kv[u][:, 1, i * P:(i + 1) * P], ident)
                mm.then_inc(vt_ok, 1)

            def turn(b, c):
                u, m = c % 2, number(b, c)
                pe.wait_ge(p_ok, m + 3)
                pe.wait_ge(pt_ok, m + 1)
                for h in range(2):
                    for i in range(2):
                        mm = pe.transpose(ps_t[u][:, h * 2 + i, :], pr[u][:, h, i * P:(i + 1) * P], ident)
                mm.then_inc(turned, 1)

            def weigh(b, c):
                u, m = c % 2, number(b, c)
                pe.wait_ge(pt_ok, m + 3)
                pe.wait_ge(vc_ok, m + 3)
                pe.wait_ge(out_ok, m + 1)
                for h in range(2):
                    for i in range(2):
                        mm = pe.matmul(ps_o[u][:, h * HD:(h + 1) * HD], pt[u][:, h * 2 + i, :],
                                       v_t[u][:, i, h * HD:(h + 1) * HD], start=(i == 0), stop=(i == 1))
                mm.then_inc(pv_ok, 1)

            def slot(b, c):
                if exists(b, c + 2):
                    score(b, c + 2)
                if exists(b, c + 1):
                    turn(b, c + 1)
                if exists(b, c):
                    weigh(b, c)
                if exists(b, c + 2):
                    turn_v(b, c + 2)

            slots(pe, slot)

        @block.scalar
        def _(act):
            def exp(b, c):
                u, m = c % 2, number(b, c)
                act.wait_ge(nmax_ok, m + 1)
                act.wait_ge(turned, m + 1)
                act.wait_ge(lse_ok, m + 1)
                for h in range(2):
                    ins = nc.scalar.activation(pr[u][:, h, :], sb_[u][:, h, :], ACT.Exp,
                                               bias=nmax[u][:, h:h + 1], accum_out=den[u][:, h:h + 1])
                ins.then_inc(p_ok, 1)

            def copy_v(b, c):
                u, m = c % 2, number(b, c)
                act.wait_ge(vt_ok, m + 3)
                act.wait_ge(pv_ok, m + 1)
                nc.scalar.copy(v_t[u][:], ps_v[u][:, 0:2, :]).then_inc(vc_ok, 1)

            def turn(b, c):
                u, m = c % 2, number(b, c)
                act.wait_ge(p_ok, m + 3)
                act.wait_ge(lse_ok, m + 1)
                nc.scalar.activation(lnd[u][:], den[u][:, 0:2], ACT.Ln).then_inc(ln_ok, 1)
                act.wait_ge(turned, m + 3)
                act.wait_ge(pv_ok, m + 1)
                nc.scalar.copy(pt[u][:], ps_t[u][:]).then_inc(pt_ok, 1)

            def slot(b, c):
                if exists(b, c + 1):
                    turn(b, c + 1)
                if exists(b, c + 2):
                    exp(b, c + 2)
                    copy_v(b, c + 2)

            def split(t):
                act.wait_ge(w_in[t // (KT // 2)], (L + 1) * (KT // 2) * DMA)
                nc.scalar.copy(w_hi[:, t, :], w_raw[:, t, :]).then_inc(whi_ok, 1)

            slots(act, slot, split)

        @block.vector
        def _(dve):
            def bias(b, c):
                u, m = c % 2, number(b, c)
                dve.wait_ge(s_ok, m + 1)
                dve.wait_ge(p_ok, m + 1)
                for h in range(2):
                    ins = nc.vector.scalar_tensor_tensor(
                        out=sb_[u][:, h, :], in0=dist[u][:, 0:KW], scalar=dist[u][:, KW + h:KW + h + 1],
                        in1=ps_s[u][:, h, :], op0=ALU.mult, op1=ALU.add)
                ins.then_inc(bias_ok, 1)
                dve.wait_ge(bias_ok, m + 3)
                dve.wait_ge(lse_ok, m + 1)
                nc.vector.tensor_reduce(nmax[u][:], sb_[u][:], AX.X, ALU.max, negate=True).then_inc(nmax_ok, 1)

            def denominators(b, c):
                u, m = c % 2, number(b, c)
                dve.wait_ge(ln_ok, m + 1)
                dve.wait_ge(out_ok, m + 1)
                nc.vector.reciprocal(den[u][:, 2:4], den[u][:, 0:2]).then_inc(chain, 1)
                dve.wait_ge(stored[u], stored_value(L, "dilated", u, b + c // 2))
                lse = out[u][:, :, HD:HD + 1].rearrange("p h x -> p (h x)")
                nc.vector.tensor_tensor(lse, lnd[u][:], nmax[u][:], ALU.subtract).then_inc(lse_ok, 1)

            def output(b, c):
                u, m = c % 2, number(b, c)
                dve.wait_ge(pv_ok, m + 3)
                dve.wait_ge(lse_ok, m + 3)
                nc.vector.tensor_tensor(out[u][:, :, 0:HD], ps_o[u][:, 0:2 * HD].rearrange("p (h e) -> p h e", e=HD),
                                        bc_free(den[u][:, 2:4], HD), ALU.mult).then_inc(out_ok, 1)

            def slot(b, c):
                if exists(b, c + 2):
                    bias(b, c + 2)
                if exists(b, c + 1):
                    denominators(b, c + 1)
                if exists(b, c):
                    output(b, c)

            def split(t):
                dve.wait_ge(whi_ok, L * KT + t + 1)
                nc.vector.tensor_tensor(w_lo[:, t, :], w_raw[:, t, :], w_hi[:, t, :].bitcast(F32), ALU.subtract).then_inc(wlo_ok, 1)

            slots(dve, slot, split)


NZ = 8


def finish(k, L, ident, cols, w_hi, w_lo):
    nc = k.nc
    phases = k.sem("phases_stored")
    with ExitStack() as ctx:
        gpost = sbuf(k, ctx, "fi_gpost", [P, D_MODEL])
        mgain = sbuf(k, ctx, "fi_mgain", [P, 2])
        x = pair(k, ctx, "fi_x", [P, D_MODEL])
        z = pair(k, ctx, "fi_z", [P, NZ + 2, P])
        e = sbuf(k, ctx, "fi_e", [P, NZ + 2, P])
        gq = pair(k, ctx, "fi_gq", [P, 3, P])
        hf = pair(k, ctx, "fi_hf", [P, MH, HD])
        hb = pair(k, ctx, "fi_hb", [P, MH, HD])
        dl = pair(k, ctx, "fi_dl", [P, NG, 2, HD + 1])
        od = sbuf(k, ctx, "fi_od", [P, NG, 2, HD])
        eo = sbuf(k, ctx, "fi_eo", [P, MH, HD])
        hsq = sbuf(k, ctx, "fi_hsq", [P, MH, HD])
        hst = sbuf(k, ctx, "fi_hst", [P, 3, MH])
        al = sbuf(k, ctx, "fi_al", [P, 2, 2, NG])
        am = sbuf(k, ctx, "fi_am", [P, 2, 2])
        m_hi = pair(k, ctx, "fi_mhi", [P, KT, P], F32R)
        m_lo = pair(k, ctx, "fi_mlo", [P, KT, P], F32R)
        mix = sbuf(k, ctx, "fi_mix", [P, KT, P])
        y = sbuf(k, ctx, "fi_y", [P, D_MODEL])
        xo = pair(k, ctx, "fi_xo", [P, D_MODEL])
        yst = sbuf(k, ctx, "fi_yst", [P, 4])
        ps_y = [psum(k, ctx, f"fi_ps_y{u}", [P, D_MODEL]) for u in range(2)]
        ps_o = psum(k, ctx, "fi_ps_o", [P, 512])
        ps_h = psum(k, ctx, "fi_ps_h", [P, 4, P])
        ps_d = psum(k, ctx, "fi_ps_d", [P, 4, P])
        const_in = k.sem("consts_in")
        loaded = [k.sem(f"fi_loaded{u}") for u in range(2)]
        x_in = [k.sem(f"fi_x_in{u}") for u in range(2)]
        stored = [k.sem(f"stored{u}") for u in range(2)]
        (sig_chain, ln_ok, logsig_ok, sig_ok, z_ok, o_ok, hs_ok, hss_ok, hrs_a, hrs_ok, lse_ok, ea_ok,
         hn_ok, gqz_ok, turned, mix_ok, hi_ok, lo_ok, y_done, ys_ok, yr_ok, yn_ok, x_ok, chain) = (
            k.sem("fi_" + s) for s in (
                "sig_chain", "ln_ok", "logsig_ok", "sig_ok", "z_ok", "o_ok", "hs_ok", "hss_ok",
                "hrs_a", "hrs_ok", "lse_ok", "ea_ok", "hn_ok", "gqz_ok", "turned", "mix_ok", "hi_ok", "lo_ok",
                "y_done", "ys_ok", "yr_ok", "yn_ok", "x_ok", "chain"))
        block = ctx.enter_context(nc.Block())
        NB = NT // 2
        NLOAD = 3 + 1 + 1 + 2 + NG
        NCHAIN = 9

        def number(b, c):
            return L * NT + (b * 2 + c)

        def uses(b, c):
            return L * NB + (b + c // 2)

        def exists(b, c):
            return not isinstance(b, int) or 0 <= c < NT

        def slots(engine, slot):
            for c in range(-2, 1):
                slot(0, c)
            with engine.Fori(0, NB - 2) as b:
                for v in range(2):
                    slot(b, 1 + v)
            for c in range(NT - 3, NT + 1):
                slot(0, c)

        @block.sync
        def _(sp):
            def loads(b, c, prompt):
                u, n = c % 2, b * 2 + c
                if not prompt:
                    sp.wait_ge(mix_ok, number(b, c) - 1)
                s, tok = loaded[u], at(n * P, P)
                for i, ct, m in ((0, CT_MZ, 2), (2, CT_GZ, 3), (5, CT_DZ, 3), (NZ, CT_MO, 2)):
                    sp.dma_start(z[u][:, i:i + m, :], k.a["proj"][ct:ct + m, :, tok].rearrange("c p t -> p c t")).then_inc(s, DMA)
                for t, d in ((hf, 0), (hb, 1)):
                    sp.dma_start(t[u][:].rearrange("p h e -> p (h e)"), rows_of(k.a["mh"][d], n * P, P, 0, MH * HD)).then_inc(s, DMA)
                sp.dma_start(gq[u][:], k.a["gqo"].rearrange("(c h) d t -> (h d) c t", h=2)[:, :, tok]).then_inc(s, DMA)
                for g, (_, dil) in enumerate(DIL):
                    s0, s1 = (0, SEQ) if prompt else (SEQ, TOK)
                    seq = k.a["dil_out"][g][s0:s1, :].rearrange("(r j) e -> j r e", r=dil)
                    j0 = (n * (P // dil)) if prompt else (n - NTP) * (P // dil)
                    sp.dma_start(dl[u][:, g].rearrange("p h e -> p (h e)"), seq[at(j0, P // dil)]).then_inc(s, DMA)

            def load_x(b, c):
                sp.dma_start(x[c % 2][:], rows_of(k.a["x"], (b * 2 + c) * P, P, 0, D_MODEL)).then_inc(x_in[c % 2], DMA)

            def slot(b, c):
                if exists(b, c - 1):
                    sp.wait_ge(x_ok, number(b, c - 1) + 2)
                    sp.dma_start(rows_of(k.a["x"], (b * 2 + c - 1) * P, P, 0, D_MODEL), xo[(c - 1) % 2][:]
                                 ).then_inc(stored[(c - 1) % 2], DMA)
                    if exists(b, c + 1):
                        load_x(b, c + 1)
                if exists(b, c + 3) and not (isinstance(b, int) and c + 3 < NTP):
                    loads(b, c + 3, False)

            loads(0, 0, True)
            loads(0, 1, True)
            sp.dma_start(gpost[:], k.a["gain_post"][at(L), :].partition_broadcast(P)).then_inc(const_in, DMA)
            sp.dma_start(mgain[:], k.a["gain_mlstm"][at(L)].rearrange("a p c -> p (a c)")).then_inc(const_in, DMA)
            load_x(0, 0)
            load_x(0, 1)
            slots(sp, slot)
            for u in range(2):
                sp.wait_ge(stored[u], stored_value(L, "finish", u, NB))
            sp.sem_inc(phases, 1)

        @block.gpsimd
        def _(pool):
            def gate(b, c):
                u, m = c % 2, number(b, c)
                pool.wait_ge(loaded[u], (uses(b, c) + 1) * NLOAD * DMA)
                nc.gpsimd.tensor_tensor(hf[u][:], hf[u][:], hb[u][:], ALU.add).then_inc(hs_ok, 1)
                pool.wait_ge(sig_ok, m + 1)
                nc.gpsimd.tensor_tensor(z[u][:, 0:NZ], z[u][:, 0:NZ], e[:, 0:NZ], ALU.mult).then_inc(z_ok, 1)

            def mix_gq(b, c):
                u, m = c % 2, number(b, c)
                pool.wait_ge(z_ok, m + 2)
                pool.wait_ge(lo_ok, m + 1)
                nc.gpsimd.tensor_tensor(mix[:, 2:5, :], gq[u][:], z[u][:, 2:5, :], ALU.mult).then_inc(gqz_ok, 1)

            def residual(b, c):
                u, m = c % 2, number(b, c)
                pool.wait_ge(yn_ok, m + 1)
                pool.wait_ge(x_in[u], (uses(b, c) + 1) * DMA)
                pool.wait_ge(stored[u], stored_value(L, "finish", u, b + c // 2))
                nc.gpsimd.tensor_tensor(xo[u][:], x[u][:], y[:], ALU.add).then_inc(x_ok, 1)

            def slot(b, c):
                if exists(b, c + 1):
                    mix_gq(b, c + 1)
                if exists(b, c - 1):
                    residual(b, c - 1)
                if exists(b, c + 2):
                    gate(b, c + 2)

            slots(pool, slot)

        @block.scalar
        def _(act):
            def log_part(b, c):
                u, m = c % 2, number(b, c)
                st = Steps(act, sig_chain, m * 2)
                act.wait_ge(loaded[u], (uses(b, c) + 1) * NLOAD * DMA)
                act.wait_ge(z_ok, m + 1)
                act.wait_ge(o_ok, m + 1)
                st.mark(nc.scalar.activation(e[:], z[u][:], ACT.Abs))
                st.join()
                st.mark(nc.scalar.activation(e[:], e[:], ACT.Exp, scale=-1.0))
                st.join()
                nc.scalar.activation(e[:], e[:], ACT.Ln, bias=cols["one"]).then_inc(ln_ok, 1)

            def sigmoid(b, c):
                act.wait_ge(logsig_ok, number(b, c) + 1)
                nc.scalar.activation(e[:], e[:], ACT.Exp).then_inc(sig_ok, 1)

            def head_scales(b, c):
                m = number(b, c)
                act.wait_ge(hss_ok, m + 1)
                nc.scalar.activation(hst[:, 1, :], hst[:, 0, :], ACT.Ln, scale=1.0 / HD, bias=cols["eps"]).then_inc(hrs_a, 1)
                act.wait_ge(lse_ok, m + 1)
                nc.scalar.activation(al[:, 1], al[:, 0], ACT.Exp).then_inc(ea_ok, 1)
                act.wait_ge(hrs_a, m + 1)
                nc.scalar.activation(hst[:, 2, :], hst[:, 1, :], ACT.Exp, scale=-0.5).then_inc(hrs_ok, 1)

            def high_part(b, c):
                act.wait_ge(mix_ok, number(b, c) + 1)
                nc.scalar.copy(m_hi[c % 2][:], mix[:]).then_inc(hi_ok, 1)

            def row_scale(b, c):
                u, m = c % 2, number(b, c)
                st = Steps(act, ys_ok, m * 2)
                act.wait_ge(y_done, m + 1)
                act.wait_ge(x_ok, m + 1)
                st.mark(nc.scalar.activation(y[:], ps_y[u][:], ACT.Square, accum_out=yst[:, 0:1]))
                st.join()
                st.mark(nc.scalar.activation(yst[:, 1:2], yst[:, 0:1], ACT.Ln, scale=1.0 / D_MODEL, bias=cols["eps"]))
                st.join()
                nc.scalar.activation(yst[:, 2:3], yst[:, 1:2], ACT.Exp, scale=-0.5).then_inc(yr_ok, 1)

            def slot(b, c):
                if exists(b, c - 1):
                    row_scale(b, c - 1)
                if exists(b, c + 1):
                    head_scales(b, c + 1)
                if exists(b, c + 2):
                    log_part(b, c + 2)
                    sigmoid(b, c + 2)
                if exists(b, c + 1):
                    high_part(b, c + 1)

            slots(act, slot)

        @block.vector
        def _(dve):
            dve.wait_ge(const_in, consts_value(L, "finish"))

            def normalise(b, c):
                u, m = c % 2, number(b, c)
                st = Steps(dve, chain, m * NCHAIN)
                dve.wait_ge(o_ok, m + 2)
                dve.wait_ge(hs_ok, m + 1)
                st.mark(nc.vector.tensor_tensor(eo[:], ps_o[:, 0:MH * HD].rearrange("p (h e) -> p h e", e=HD), hf[u][:],
                                                ALU.mult))
                lse = dl[u][:, :, :, HD].rearrange("p g h -> p h g")
                st.mark(nc.vector.tensor_reduce(am[:, 0, :], lse, AX.X, ALU.max))
                st.join()
                st.mark(nc.vector.tensor_tensor(hsq[:], eo[:], eo[:], ALU.mult))
                nc.vector.tensor_tensor(al[:, 0], lse, bc_free(am[:, 0, :], NG), ALU.subtract).then_inc(lse_ok, 1)
                st.join()
                nc.vector.tensor_reduce(hst[:, 0, :], hsq[:], AX.X, ALU.add).then_inc(hss_ok, 1)
                dve.wait_ge(ea_ok, m + 1)
                st.mark(nc.vector.tensor_reduce(am[:, 1, :], al[:, 1], AX.X, ALU.add))
                st.join()
                st.mark(nc.vector.reciprocal(am[:, 1, :], am[:, 1, :]))
                st.join()
                st.mark(nc.vector.tensor_tensor(al[:, 1], al[:, 1], bc_free(am[:, 1, :], NG), ALU.mult))
                st.join()
                for h in range(2):
                    st.mark(nc.vector.tensor_tensor(od[:, :, h, :], dl[u][:, :, h, 0:HD],
                                                    bc_free(al[:, 1, h, :], HD), ALU.mult))
                dve.wait_ge(hrs_ok, m + 1)
                nc.vector.tensor_tensor(hf[u][:], eo[:], bc_free(hst[:, 2, :], HD), ALU.mult).then_inc(hn_ok, 1)
                return st

            def gate_mixed(b, c, st):
                u, m = c % 2, number(b, c)
                dve.wait_ge(turned, m + 1)
                dve.wait_ge(gqz_ok, m + 1)
                for j in range(2):
                    ins = nc.vector.scalar_tensor_tensor(out=mix[:, j, :], in0=ps_h[:, j, :], scalar=mgain[:, j:j + 1],
                                                         in1=z[u][:, j, :], op0=ALU.mult, op1=ALU.mult)
                st.mark(ins)
                nc.vector.tensor_tensor(mix[:, 5:8, :], ps_d[:, 0:3, :], z[u][:, 5:8, :], ALU.mult).then_inc(mix_ok, 1)
                dve.wait_ge(hi_ok, m + 1)
                nc.vector.tensor_tensor(m_lo[u][:], mix[:], m_hi[u][:].bitcast(F32), ALU.subtract).then_inc(lo_ok, 1)
                assert st.n == NCHAIN, st.n

            def scale_rows(b, c):
                u, m = c % 2, number(b, c)
                dve.wait_ge(yr_ok, m + 1)
                nc.vector.scalar_tensor_tensor(out=y[:], in0=ps_y[u][:], scalar=yst[:, 2:3], in1=gpost[:],
                                               op0=ALU.mult, op1=ALU.mult).then_inc(yn_ok, 1)

            def log_sigmoid(b, c):
                u, m = c % 2, number(b, c)
                dve.wait_ge(ln_ok, m + 1)
                nc.vector.scalar_tensor_tensor(out=e[:], in0=z[u][:], scalar=0.0, in1=e[:], op0=ALU.min,
                                               op1=ALU.subtract).then_inc(logsig_ok, 1)

            def slot(b, c):
                if exists(b, c + 1):
                    st = normalise(b, c + 1)
                if exists(b, c - 1):
                    scale_rows(b, c - 1)
                if exists(b, c + 2):
                    log_sigmoid(b, c + 2)
                if exists(b, c + 1):
                    gate_mixed(b, c + 1, st)

            slots(dve, slot)

        @block.tensor
        def _(pe):
            def turn_o(b, c):
                pe.wait_ge(sig_ok, number(b, c) + 1)
                for j in range(2):
                    mm = pe.transpose(ps_o[:, j * P:(j + 1) * P], e[:, NZ + j, :], ident)
                mm.then_inc(o_ok, 1)

            def turn_heads(b, c):
                pe.wait_ge(hn_ok, number(b, c) + 1)
                h = hf[c % 2][:].rearrange("p h e -> p (h e)")
                for j in range(2):
                    pe.transpose(ps_h[:, j, :], h[:, j * P:(j + 1) * P], ident)
                for g in range(NG):
                    mm = pe.transpose(ps_d[:, g, :], od[:, g].rearrange("p h e -> p (h e)"), ident)
                mm.then_inc(turned, 1)

            def multiply(b, c, half):
                u, cols_ = c % 2, slice(half * 512, (half + 1) * 512)
                for t in range(KT):
                    for i, (a, w) in enumerate(((m_hi, w_hi), (m_lo, w_hi), (m_hi, w_lo))):
                        mm = pe.matmul(ps_y[u][:, cols_], a[u][:, t, :], w[:, t, cols_],
                                       start=(t == 0 and i == 0), stop=(t == KT - 1 and i == 2))
                return mm

            def slot(b, c):
                if exists(b, c):
                    pe.wait_ge(lo_ok, number(b, c) + 2)
                    multiply(b, c, 0)
                if exists(b, c + 1):
                    turn_heads(b, c + 1)
                if exists(b, c):
                    multiply(b, c, 1).then_inc(y_done, 1)
                if exists(b, c + 2):
                    turn_o(b, c + 2)

            slots(pe, slot)



def constants():
    c = {"ident": np.eye(P, dtype=np.float32)}
    half = HD // 2
    inv = (10000.0 ** (-np.arange(0, half, 2, dtype=np.float32) / half)).astype(np.float32)

    def angles(T):
        t = np.arange(T)
        r, col = (t // 64).astype(np.float32), (t % 64).astype(np.float32)
        return np.concatenate([r[:, None] * inv, col[:, None] * inv], axis=-1)

    ang = np.concatenate([angles(SEQ), angles(DEC_SEQ)], axis=0)
    c["cos"] = np.ascontiguousarray(np.tile(np.cos(ang).T, (4, 1)).astype(np.float32))
    c["sin"] = np.ascontiguousarray(np.tile(np.sin(ang).T, (4, 1)).astype(np.float32))
    d = np.arange(P)
    c["head_ones"] = (d[:, None] // HD == d[None, :] // HD).astype(np.float32)
    swap = np.zeros((P, P), np.float32)
    for o in range(P):
        swap[o + half if o % HD < half else o - half, o] = -1.0 if o % HD < half else 1.0
    c["rope_swap"] = swap
    s = np.full(4, HD ** -0.5, np.float32)
    c["rq_scale"] = np.tile(np.array([s[0], s[0], s[0], 1.0], np.float32), (P, 1))
    c["cv_scale"] = np.tile(np.array([1.0, 1.0, s[0], s[0]], np.float32), (P, 1))
    chunk = np.arange(GR) % NT
    c["carries"] = np.stack([~np.isin(chunk, (0, NTP)), ~np.isin(chunk, (NTP - 1, NT - 1))], axis=1).astype(np.float32)
    causal = np.zeros((P, 2, P), np.float32)
    causal[:, 0][d[:, None] > d[None, :]] = -BIG
    causal[:, 1][d[:, None] < d[None, :]] = -BIG
    c["causal"] = causal
    dist = np.full((NG, NT, P, KW + 2), BIG, np.float32)
    for g, (_, dil) in enumerate(DIL):
        for h in range(2):
            dist[g, :, :, KW + h] = -2.0 ** (-8.0 * (2 * g + h + 1) / 6.0) * dil
        for n in range(NT):
            s0, T = (0, SEQ) if n < NTP else (SEQ, DEC_SEQ)
            qi = n * P - s0 + np.arange(P)[:, None]
            ki = n * P - s0 - SIDE + np.arange(KW)[None, :]
            near = (ki >= 0) & (ki < T) & (np.abs(ki - qi) <= SIDE) & (qi // (T // dil) == ki // (T // dil))
            dist[g, n, :, :KW][near] = np.abs(ki - qi)[near]
    c["dil_dist"] = dist
    return c


def encoder(nc, arrays):
    with ExitStack() as ctx:
        k = Kernel(nc, ctx, arrays)
        k.a["x"] = k.a["y"]
        k.dram("proj", (NCT, P, TOK))
        k.dram("mqk", (6, P, TOK))
        k.dram("tokmaj", (TOK, TM * P))
        k.dram("gqk_hi", (4, P, TOK))
        k.dram("gqk_lo", (4, P, TOK))
        k.dram("gqo", (GQ_HEADS, HD, TOK))
        k.dram("gate_ends", (2, GR, 2))
        k.dram("gate_m", (2, GR))
        k.dram("gate_M", (2, GR, P))
        k.dram("gate_dec", (2, GR))
        k.dram("mh", (2, TOK, MH * HD))
        k.dram("dil_q", (NG, 2, P, TOK))
        k.dram("dil_kv", (NG, 2, P, PADTOK))
        k.dram("dil_out", (NG, TOK, 2 * (HD + 1)))
        ident_t = sbuf(k, ctx, "ident", [P, P])
        col = sbuf(k, ctx, "cols", [P, 4])
        zeros = sbuf(k, ctx, "zeros", [P, SIDE])
        gate_cols = sbuf(k, ctx, "gate_cols", [P, 8, GR])
        decay = sbuf(k, ctx, "decay", [P, 2, 2, NT])
        ident = ident_t[:]
        cols = {"eps": col[:, 0:1], "one": col[:, 1:2]}
        once, filled = k.sem("once_dma"), k.sem("once_fill")
        with nc.Block() as block:
            @block.vector
            def _(dve):
                nc.vector.memset(col[:, 0:1], EPS).then_inc(filled, 1)
                nc.vector.memset(col[:, 1:2], 1.0).then_inc(filled, 1)
                nc.vector.memset(zeros[:], 0.0).then_inc(filled, 1)
                dve.wait_ge(filled, 3)

            @block.sync
            def _(sp):
                sp.dma_start(k.a["x"], k.a["x_all"]).then_inc(once, DMA)
                sp.dma_start(ident_t[:], k.a["ident"]).then_inc(once, DMA)
                sp.wait_ge(filled, 3)
                for g in range(NG):
                    for a in (0, SIDE + TOK):
                        for c in range(2):
                            sp.dma_start(k.a["dil_kv"][g, c, :, a:a + SIDE], zeros[:]).then_inc(once, DMA)
                planes = [k.a["mqk"][2 * r:2 * r + 2] for r in range(2)] + [k.a["dil_q"][g] for g in range(NG)]
                for plane in planes:
                    for e in range(2):
                        rows = slice((1 - e) * HD, (2 - e) * HD)
                        sp.dma_start(plane[e, rows, :].rearrange("d (n t) -> d n t", t=SIDE),
                                     zeros[rows, :].unsqueeze(1).to_broadcast([HD, TOK // SIDE, SIDE])).then_inc(once, DMA)
                sp.wait_ge(once, (2 + NG * 4 + len(planes) * 2) * DMA)

            @block.scalar
            def _(act):
                nc.scalar.preload_act_table_set("natural_log_exp_and_others")
                for name, credit in CREDITS.items():
                    act.sem_inc(k.sem(name), credit)

        with nc.Fori(0, DEPTH) as L:
            with ExitStack() as held:
                h_hi = sbuf(k, held, "h_hi", [P, KT, TOK], F32R)
                h_lo = sbuf(k, held, "h_lo", [P, KT, TOK], F32R)
                pre_norm(k, L, h_hi, h_lo, ident, cols)
                project(k, L, h_hi, h_lo)
            prepare(k, L, gate_cols, decay, ident, cols)
            attend_gqa(k, L, ident, cols, zeros)
            mlstm(k, L, gate_cols, decay)
            with ExitStack() as held:
                w_hi = sbuf(k, held, "w_out_hi", [P, KT, D_MODEL], F32R)
                w_lo = sbuf(k, held, "w_out_lo", [P, KT, D_MODEL], F32R)
                attend_dilated(k, L, ident, w_hi, w_lo)
                finish(k, L, ident, cols, w_hi, w_lo)


def laid_out(inputs):
    f = {n: np.ascontiguousarray(np.asarray(v)) for n, v in inputs.items()}
    D = f["w_in"].shape[0]
    gates0 = 4 * MH * HD
    ng = 4 * MH
    w = f["w_in"]
    plain, dilated, dilated_z = np.split(w[:, :, gates0 + ng:], [(CT_DZ - CT_MZ) * P, (CT_DZ - CT_MZ + 3 * NG) * P], axis=2)
    w = np.concatenate([w[:, :, :gates0], plain, dilated_z, w[:, :, gates0:gates0 + ng],
                        np.zeros((D, D_MODEL, P - ng), w.dtype), dilated], axis=2)
    w = w.reshape(D, KT, P, NCT, P).transpose(0, 3, 2, 1, 4).reshape(D, NCT, P, KT * P)
    taps = np.stack([f["mlstm_conv_w"][:, 0], f["mlstm_conv_w"][:, 1], f["mlstm_conv_w"][:, 2], f["mlstm_conv_b"]], axis=-1)
    gb = f["mlstm_gate_bias"].reshape(D, 4, MH)
    qk = np.stack([np.tile(f["gqa_q_norm"], (1, 2))] * 3 + [np.tile(f["gqa_k_norm"], (1, 2))], axis=-1)
    return {
        "x_all": np.concatenate([f["x_prompt"][0], f["x_sample"][0]], axis=0),
        "w_in": w,
        "w_out": f["w_out"].reshape(D, KT, P, D_MODEL),
        "gain_pre": f["norm_pre"],
        "gain_post": f["norm_post"],
        "gain_qk": qk,
        "gain_mlstm": f["mlstm_out_gain"].reshape(D, 2, P).transpose(0, 2, 1),
        "conv_par": taps.reshape(D, 4, P, 4).transpose(0, 2, 1, 3),
        "gate_bias": np.repeat(gb, NT, axis=2).transpose(0, 2, 1),
    }


def kernel(**inputs):
    from concourse import bacc
    from concourse.bass_utils import run_bass_kernel_spmd

    nc = bacc.Bacc("TRN2", target_bir_lowering=False, num_devices=1)
    data = {n: np.ascontiguousarray(v) for n, v in (laid_out(inputs) | constants()).items()}
    arrays = {n: nc.dram_tensor(f"in_{n}", list(v.shape), F32, kind="ExternalInput").ap() for n, v in data.items()}
    arrays["y"] = nc.dram_tensor("y", [TOK, D_MODEL], F32, kind="ExternalOutput").ap()
    encoder(nc, arrays)
    y = run_bass_kernel_spmd(nc, [{f"in_{n}": v for n, v in data.items()}], core_ids=[0]).results[0]["y"]
    return y[None, :SEQ], y[None, SEQ:]
```
